# Optimizing a Trainium2 kernel written in Bass

```python
import math
import jax, jax.numpy as jnp
from jax import lax
import numpy as np

D_MODEL = 1024
BATCH = 1
SEQ = 512
DEPTH = 2

DA_HEADS = 4
DA_QK_DIM = 64
DA_V_DIM = 2 * DA_QK_DIM
DA_QK_WIDTH = DA_HEADS * 2 * DA_QK_DIM
DA_WIDTH = DA_HEADS * DA_V_DIM
ROPE_THETA = 500000.0
ROT_DIM = DA_QK_DIM // 4
Q_BLOCK = 128
HG_HEADS = 4
HG_K_DIM = 128
HG_V_DIM = 128
HG_K_WIDTH = HG_HEADS * HG_K_DIM
HG_V_WIDTH = HG_HEADS * HG_V_DIM
HG_CHUNK = 64
FFN_HIDDEN = -(-8 * D_MODEL // (3 * 256)) * 256
NORM_EPS = 1e-6
IN_SIZES = (DA_QK_WIDTH, DA_QK_WIDTH, DA_WIDTH,
            HG_K_WIDTH, HG_K_WIDTH, HG_K_WIDTH, HG_V_WIDTH, HG_V_WIDTH,
            D_MODEL, D_MODEL)
IN_WIDTH = sum(IN_SIZES)


def rmsnorm(x, gain):
    xf = x.astype(jnp.float32)
    y = xf * lax.rsqrt(jnp.mean(xf * xf, axis=-1, keepdims=True) + NORM_EPS)
    return (y * gain.astype(jnp.float32)).astype(x.dtype)

def split_columns(p):
    outs, start = [], 0
    for size in IN_SIZES:
        outs.append(p[..., start:start + size])
        start += size
    return outs

def rope_tables(positions):
    inv_freq = ROPE_THETA ** (-(jnp.arange(0, ROT_DIM, 2, dtype=jnp.float32) / ROT_DIM))
    ang = positions.astype(jnp.float32)[..., None] * inv_freq
    return jnp.cos(ang), jnp.sin(ang)

def apply_partial_rope(t, cos, sin):
    c = cos[:, :, None, None, :].astype(t.dtype)
    s = sin[:, :, None, None, :].astype(t.dtype)
    half = ROT_DIM // 2
    t1 = t[..., :half]
    t2 = t[..., half:ROT_DIM]
    rot = jnp.concatenate([t1 * c - t2 * s, t2 * c + t1 * s], axis=-1)
    return jnp.concatenate([rot, t[..., ROT_DIM:]], axis=-1)

def diff_attention(h_q, h_k, h_v, cos, sin, lam, norm_gain, layer):
    B, S, _ = h_q.shape
    q = h_q.reshape(B, S, DA_HEADS, 2, DA_QK_DIM)
    k = h_k.reshape(B, S, DA_HEADS, 2, DA_QK_DIM)
    v = h_v.reshape(B, S, DA_HEADS, DA_V_DIM)
    q = apply_partial_rope(q, cos, sin) * (DA_QK_DIM ** -0.5)
    k = apply_partial_rope(k, cos, sin)
    lam_init = 0.8 - 0.6 * math.exp(-0.3 * layer)
    l32 = lam.astype(jnp.float32)
    lam_full = (jnp.exp(jnp.sum(l32[0] * l32[1])) - jnp.exp(jnp.sum(l32[2] * l32[3]))
                + lam_init)
    nq = S // Q_BLOCK
    qb = q.reshape(B, nq, Q_BLOCK, DA_HEADS, 2, DA_QK_DIM).transpose(1, 0, 2, 3, 4, 5)

    def block(qi):
        s = jnp.einsum('bqhcd,bkhcd->bhcqk', qi, k).astype(jnp.float32)
        p = jax.nn.softmax(s, axis=-1)
        w = p[:, :, 0] - lam_full * p[:, :, 1]
        return jnp.einsum('bhqk,bkhv->bqhv', w.astype(v.dtype), v)

    o = lax.map(block, qb)
    o = o.transpose(1, 0, 2, 3, 4).reshape(B, S, DA_HEADS, DA_V_DIM)
    o = rmsnorm(o, norm_gain.reshape(DA_HEADS, DA_V_DIM)) * (1.0 - lam_init)
    return o.reshape(B, S, DA_WIDTH)

def hgrn_lower_bounds(lb_logits):
    p = jax.nn.softmax(lb_logits.astype(jnp.float32), axis=1)
    c = jnp.cumsum(p, axis=1)
    return c - c[:, :1]

def log_forget(z, lb):
    return jnp.logaddexp(jnp.log(lb), jnp.log1p(-lb) + jax.nn.log_sigmoid(z))

def chunk_scan(q, k, g, v):
    B, S, H, dk = q.shape
    dv = v.shape[-1]
    n = S // HG_CHUNK

    def to_chunks(t):
        return t.reshape(B, n, HG_CHUNK, H, t.shape[-1]).transpose(1, 0, 3, 2, 4)

    tril = jnp.tril(jnp.ones((HG_CHUNK, HG_CHUNK), dtype=bool))

    def step(state, inp):
        qc, kc, gc, vc = inp
        b = jnp.cumsum(gc, axis=2)
        inter = jnp.einsum('bhck,bhkv->bhcv', qc * jnp.exp(b), state)
        diff = b[:, :, :, None, :] - b[:, :, None, :, :]
        decay = jnp.exp(jnp.where(tril[:, :, None], diff, -jnp.inf))
        scores = jnp.einsum('bhtk,bhsk,bhtsk->bhts', qc, kc, decay)
        intra = jnp.einsum('bhts,bhsv->bhtv', scores, vc)
        b_last = b[:, :, -1, :]
        state = (jnp.exp(b_last)[..., None] * state
                 + jnp.einsum('bhck,bhcv->bhkv', kc * jnp.exp(b_last[:, :, None, :] - b), vc))
        return state, inter + intra

    s0 = jnp.zeros((B, H, dk, dv), jnp.float32)
    _, out = lax.scan(step, s0, (to_chunks(q), to_chunks(k), to_chunks(g), to_chunks(v)))
    return out.transpose(1, 0, 3, 2, 4).reshape(B, S, H, dv)

def hgrn2_bidirectional(h_q, h_ff, h_fb, h_i, h_g, lb_f, lb_b, norm_gain):
    B, S, _ = h_q.shape
    f32 = jnp.float32
    q = h_q.astype(f32).reshape(B, S, HG_HEADS, HG_K_DIM)
    v = h_i.astype(f32).reshape(B, S, HG_HEADS, HG_V_DIM)
    g_f = log_forget(h_ff.astype(f32).reshape(B, S, HG_HEADS, HG_K_DIM),
                     lb_f.reshape(HG_HEADS, HG_K_DIM))
    g_b = log_forget(h_fb.astype(f32).reshape(B, S, HG_HEADS, HG_K_DIM),
                     lb_b.reshape(HG_HEADS, HG_K_DIM))
    k_f = -jnp.expm1(g_f)
    k_b = -jnp.expm1(g_b)
    out_f = chunk_scan(q, k_f, g_f, v)
    out_b = chunk_scan(q[:, ::-1], k_b[:, ::-1], g_b[:, ::-1], v[:, ::-1])[:, ::-1]
    o = rmsnorm(out_f + out_b, norm_gain.reshape(HG_HEADS, HG_V_DIM))
    o = o * jax.nn.sigmoid(h_g.astype(f32).reshape(B, S, HG_HEADS, HG_V_DIM))
    return o.reshape(B, S, HG_V_WIDTH).astype(h_q.dtype)

def first_inputs(seed: int = 0) -> dict:
    key = jax.random.key(seed)
    ks = jax.random.split(key, 18)
    nrm = jax.random.normal
    f32 = jnp.float32
    x = nrm(ks[0], (BATCH, SEQ, D_MODEL), f32)
    offset = jax.random.randint(ks[1], (BATCH, 1), 0, 1024, dtype=jnp.int32)
    positions = offset + jnp.arange(SEQ, dtype=jnp.int32)[None, :]
    w_in = nrm(ks[2], (DEPTH, D_MODEL, IN_WIDTH), f32) * D_MODEL ** -0.5
    da_lambda = nrm(ks[3], (DEPTH, 4, DA_QK_DIM), f32) * 0.1
    da_norm = 1.0 + 0.02 * nrm(ks[4], (DEPTH, DA_WIDTH), f32)
    hg_lb_logits = 0.5 * nrm(ks[5], (2, DEPTH, HG_K_WIDTH), f32)
    hg_norm = 1.0 + 0.02 * nrm(ks[6], (DEPTH, HG_V_WIDTH), f32)
    w_a = nrm(ks[7], (DEPTH, DA_WIDTH, D_MODEL), f32) * DA_WIDTH ** -0.5
    w_b = nrm(ks[8], (DEPTH, HG_V_WIDTH, D_MODEL), f32) * HG_V_WIDTH ** -0.5
    w_o = nrm(ks[9], (DEPTH, D_MODEL, D_MODEL), f32) * D_MODEL ** -0.5
    attn_norm = 1.0 + 0.02 * nrm(ks[10], (DEPTH, D_MODEL), f32)
    ffn_norm = 1.0 + 0.02 * nrm(ks[11], (DEPTH, D_MODEL), f32)
    w_gate = nrm(ks[12], (DEPTH, D_MODEL, FFN_HIDDEN), f32) * D_MODEL ** -0.5
    w_up = nrm(ks[13], (DEPTH, D_MODEL, FFN_HIDDEN), f32) * D_MODEL ** -0.5
    w_down = nrm(ks[14], (DEPTH, FFN_HIDDEN, D_MODEL), f32) * FFN_HIDDEN ** -0.5
    final_norm = 1.0 + 0.02 * nrm(ks[15], (D_MODEL,), f32)
    return {"x": x, "positions": positions, "w_in": w_in, "da_lambda": da_lambda,
            "da_norm": da_norm, "hg_lb_logits": hg_lb_logits, "hg_norm": hg_norm,
            "w_a": w_a, "w_b": w_b, "w_o": w_o, "attn_norm": attn_norm,
            "ffn_norm": ffn_norm, "w_gate": w_gate, "w_up": w_up, "w_down": w_down,
            "final_norm": final_norm}

def first_block(x, positions, w_in, da_lambda, da_norm, hg_lb_logits, hg_norm, w_a, w_b,
              w_o, attn_norm, ffn_norm, w_gate, w_up, w_down, final_norm):
    cos, sin = rope_tables(positions)
    lbs = hgrn_lower_bounds(hg_lb_logits)
    for layer in range(DEPTH):
        h = rmsnorm(x, attn_norm[layer])
        proj = h @ w_in[layer]
        (a_q, a_k, a_v, b_q, b_ff, b_fb, b_i, b_g, gate_a, gate_b) = split_columns(proj)
        y_a = diff_attention(a_q, a_k, a_v, cos, sin, da_lambda[layer], da_norm[layer],
                             layer) @ w_a[layer]
        y_b = hgrn2_bidirectional(b_q, b_ff, b_fb, b_i, b_g,
                                  lbs[0, layer].astype(x.dtype).astype(jnp.float32),
                                  lbs[1, layer].astype(x.dtype).astype(jnp.float32),
                                  hg_norm[layer]) @ w_b[layer]
        merged = jax.nn.sigmoid(gate_a) * y_a + jax.nn.sigmoid(gate_b) * y_b
        x = x + merged @ w_o[layer]
        h = rmsnorm(x, ffn_norm[layer])
        x = x + (jax.nn.silu(h @ w_gate[layer]) * (h @ w_up[layer])) @ w_down[layer]
    return rmsnorm(x, final_norm)


DEPTH_2 = 1

N_Q_HEADS = 8
N_KV_HEADS = 2
HEAD_DIM = 64
Q_GROUP = N_Q_HEADS // N_KV_HEADS
ATTN_WIDTH = N_Q_HEADS * HEAD_DIM
KV_WIDTH = N_KV_HEADS * HEAD_DIM
WINDOW = 128
BLOCK = 128
N_BUCKETS = 32
MAX_DISTANCE = 128
NEG_INF = -1e30
SSM_WIDTH = D_MODEL // 2
SSM_GROUP = 16
SSM_GROUPS = SSM_WIDTH // SSM_GROUP
SSM_STATE = 64
DT_MIN = 1e-3
DT_MAX = 1e-1
N_BRANCHES = 2
D_FF = 4 * D_MODEL
IN_WIDTH_2 = ATTN_WIDTH + 2 * KV_WIDTH + SSM_WIDTH + N_BRANCHES * D_MODEL
SPLITS = (ATTN_WIDTH, ATTN_WIDTH + KV_WIDTH, ATTN_WIDTH + 2 * KV_WIDTH,
          ATTN_WIDTH + 2 * KV_WIDTH + SSM_WIDTH, ATTN_WIDTH + 2 * KV_WIDTH + SSM_WIDTH + D_MODEL)
RMS_EPS = 1e-6


def rmsnorm_2(x, g):
    xf = x.astype(jnp.float32)
    y = xf * lax.rsqrt(jnp.mean(xf * xf, axis=-1, keepdims=True) + RMS_EPS)
    return (y * g.astype(jnp.float32)).astype(x.dtype)

def t5_causal_bucket(dist):
    max_exact = N_BUCKETS // 2
    d = jnp.maximum(dist, 0)
    df = jnp.maximum(d, 1).astype(jnp.float32)
    large = max_exact + (jnp.log(df / max_exact) / math.log(MAX_DISTANCE / max_exact)
                         * (N_BUCKETS - max_exact)).astype(jnp.int32)
    large = jnp.minimum(large, N_BUCKETS - 1)
    return jnp.where(d < max_exact, d, large)

def sliding_window_attention(q, k, v, sinks, rel_bias):
    B, L = q.shape[0], q.shape[1]
    nb = L // BLOCK
    qb = q.reshape(B, nb, BLOCK, N_KV_HEADS, Q_GROUP, HEAD_DIM)

    def band(t):
        tb = t.reshape(B, nb, BLOCK, N_KV_HEADS, HEAD_DIM)
        prev = jnp.pad(tb, ((0, 0), (1, 0), (0, 0), (0, 0), (0, 0)))[:, :-1]
        return jnp.concatenate([prev, tb], axis=2)

    kb, vb = band(k), band(v)
    logits = jnp.einsum('bnqkgd,bnskd->bnkgqs', qb, kb,
                        preferred_element_type=jnp.float32) * (HEAD_DIM ** -0.5)
    qi = jnp.arange(BLOCK)[:, None]
    kj = jnp.arange(2 * BLOCK)[None, :]
    dist = qi + BLOCK - kj
    band_ok = (dist >= 0) & (dist < WINDOW)
    key_pos = jnp.arange(nb)[:, None] * BLOCK - BLOCK + jnp.arange(2 * BLOCK)[None, :]
    mask = band_ok[None] & (key_pos >= 0)[:, None, :]
    bias = rel_bias.astype(jnp.float32)[t5_causal_bucket(dist)]
    bias = jnp.transpose(bias, (2, 0, 1)).reshape(N_KV_HEADS, Q_GROUP, BLOCK, 2 * BLOCK)
    logits = jnp.where(mask[None, :, None, None], logits + bias[None, None], NEG_INF)
    s = sinks.astype(jnp.float32).reshape(1, 1, N_KV_HEADS, Q_GROUP, 1, 1)
    m = jnp.maximum(jnp.max(logits, axis=-1, keepdims=True), s)
    p = jnp.exp(logits - m)
    denom = jnp.sum(p, axis=-1, keepdims=True) + jnp.exp(s - m)
    probs = (p / denom).astype(v.dtype)
    out = jnp.einsum('bnkgqs,bnskd->bnqkgd', probs, vb)
    return out.reshape(B, L, ATTN_WIDTH)

def s5_ssm(u, lam_re, lam_im, log_dt, b_re, b_im, c_re, c_im, d_skip):
    B, L = u.shape[0], u.shape[1]
    uf = u.astype(jnp.float32).reshape(B, L, SSM_GROUPS, SSM_GROUP)
    dt = jnp.exp(log_dt.astype(jnp.float32))[:, None]
    lr = lam_re.astype(jnp.float32)
    li = lam_im.astype(jnp.float32)
    mag = jnp.exp(lr * dt)
    ab_re = mag * jnp.cos(li * dt)
    ab_im = mag * jnp.sin(li * dt)
    nr = ab_re - 1.0
    den = lr * lr + li * li
    f_re = (nr * lr + ab_im * li) / den
    f_im = (ab_im * lr - nr * li) / den
    br = b_re.astype(jnp.float32)
    bi = b_im.astype(jnp.float32)
    bb_re = f_re[..., None] * br - f_im[..., None] * bi
    bb_im = f_re[..., None] * bi + f_im[..., None] * br
    bu_re = jnp.einsum('blgc,gpc->blgp', uf, bb_re)
    bu_im = jnp.einsum('blgc,gpc->blgp', uf, bb_im)
    a_re = jnp.broadcast_to(ab_re, bu_re.shape)
    a_im = jnp.broadcast_to(ab_im, bu_im.shape)

    def combine(e1, e2):
        a1r, a1i, b1r, b1i = e1
        a2r, a2i, b2r, b2i = e2
        return (a2r * a1r - a2i * a1i,
                a2r * a1i + a2i * a1r,
                a2r * b1r - a2i * b1i + b2r,
                a2r * b1i + a2i * b1r + b2i)

    _, _, h_re, h_im = lax.associative_scan(combine, (a_re, a_im, bu_re, bu_im), axis=1)
    y = (jnp.einsum('blgp,gcp->blgc', h_re, c_re.astype(jnp.float32))
         - jnp.einsum('blgp,gcp->blgc', h_im, c_im.astype(jnp.float32)))
    y = y + d_skip.astype(jnp.float32).reshape(SSM_GROUPS, SSM_GROUP) * uf
    return y.reshape(B, L, SSM_WIDTH).astype(u.dtype)

def second_inputs(seed: int = 0) -> dict:
    key = jax.random.key(seed)
    ks = jax.random.split(key, 24)
    f32 = jnp.float32
    nrm = lambda k, shape, scale: jax.random.normal(k, shape, f32) * scale
    n_idx = jnp.arange(SSM_STATE, dtype=f32)
    return {
        "x": jax.random.normal(ks[0], (BATCH, SEQ, D_MODEL), f32),
        "norm_mix_pre": 1.0 + nrm(ks[1], (DEPTH_2, D_MODEL), 0.05),
        "norm_mix_post": 1.0 + nrm(ks[2], (DEPTH_2, D_MODEL), 0.05),
        "norm_mlp_pre": 1.0 + nrm(ks[3], (DEPTH_2, D_MODEL), 0.05),
        "norm_mlp_post": 1.0 + nrm(ks[4], (DEPTH_2, D_MODEL), 0.05),
        "w_in": nrm(ks[5], (DEPTH_2, D_MODEL, IN_WIDTH_2), D_MODEL ** -0.5),
        "rel_bias": nrm(ks[6], (N_BUCKETS, N_Q_HEADS), 0.5),
        "sinks": nrm(ks[7], (DEPTH_2, N_Q_HEADS), 0.5),
        "lam_re": -0.5 + nrm(ks[8], (DEPTH_2, SSM_GROUPS, SSM_STATE), 0.02),
        "lam_im": math.pi * n_idx + nrm(ks[9], (DEPTH_2, SSM_GROUPS, SSM_STATE), 0.02),
        "log_dt": jax.random.uniform(ks[10], (DEPTH_2, SSM_GROUPS), f32,
                                     math.log(DT_MIN), math.log(DT_MAX)),
        "b_re": nrm(ks[11], (DEPTH_2, SSM_GROUPS, SSM_STATE, SSM_GROUP), SSM_GROUP ** -0.5),
        "b_im": nrm(ks[12], (DEPTH_2, SSM_GROUPS, SSM_STATE, SSM_GROUP), SSM_GROUP ** -0.5),
        "c_re": nrm(ks[13], (DEPTH_2, SSM_GROUPS, SSM_GROUP, SSM_STATE), SSM_STATE ** -0.5),
        "c_im": nrm(ks[14], (DEPTH_2, SSM_GROUPS, SSM_GROUP, SSM_STATE), SSM_STATE ** -0.5),
        "d_skip": nrm(ks[15], (DEPTH_2, SSM_WIDTH), 1.0),
        "w_glu": nrm(ks[16], (DEPTH_2, SSM_WIDTH, SSM_WIDTH), SSM_WIDTH ** -0.5),
        "w_attn_branch": nrm(ks[17], (DEPTH_2, ATTN_WIDTH, D_MODEL), ATTN_WIDTH ** -0.5),
        "w_ssm_branch": nrm(ks[18], (DEPTH_2, SSM_WIDTH, D_MODEL), SSM_WIDTH ** -0.5),
        "w_out": nrm(ks[19], (DEPTH_2, D_MODEL, D_MODEL), D_MODEL ** -0.5),
        "w_ff_in": nrm(ks[20], (DEPTH_2, D_MODEL, D_FF), D_MODEL ** -0.5),
        "w_ff_out": nrm(ks[21], (DEPTH_2, D_FF, D_MODEL), D_FF ** -0.5),
    }

def second_block(x, norm_mix_pre, norm_mix_post, norm_mlp_pre, norm_mlp_post, w_in, rel_bias,
              sinks, lam_re, lam_im, log_dt, b_re, b_im, c_re, c_im, d_skip, w_glu,
              w_attn_branch, w_ssm_branch, w_out, w_ff_in, w_ff_out):
    B, L = x.shape[0], x.shape[1]
    for l in range(DEPTH_2):
        h = rmsnorm_2(x, norm_mix_pre[l])
        proj = h @ w_in[l]
        q, k, v, u, g_attn, g_ssm = jnp.split(proj, SPLITS, axis=-1)
        q = q.reshape(B, L, N_Q_HEADS, HEAD_DIM)
        k = k.reshape(B, L, N_KV_HEADS, HEAD_DIM)
        v = v.reshape(B, L, N_KV_HEADS, HEAD_DIM)
        y_attn = sliding_window_attention(q, k, v, sinks[l], rel_bias) @ w_attn_branch[l]
        z = jax.nn.gelu(s5_ssm(u, lam_re[l], lam_im[l], log_dt[l], b_re[l], b_im[l],
                               c_re[l], c_im[l], d_skip[l]))
        z = z * jax.nn.sigmoid(z @ w_glu[l])
        y_ssm = z @ w_ssm_branch[l]
        merged = jax.nn.sigmoid(g_attn) * y_attn + jax.nn.sigmoid(g_ssm) * y_ssm
        x = x + rmsnorm_2(merged @ w_out[l], norm_mix_post[l])
        h = rmsnorm_2(x, norm_mlp_pre[l])
        f = jnp.square(jax.nn.relu(h @ w_ff_in[l])) @ w_ff_out[l]
        x = x + rmsnorm_2(f, norm_mlp_post[l])
    return x


def setup_inputs(seed=0):
    out = dict(first_inputs(seed))
    for name, value in second_inputs(seed + 1).items():
        if name != "x":
            out[name + "_2"] = value
    return out


def reference(
    x, positions, w_in, da_lambda, da_norm, hg_lb_logits, hg_norm, w_a, w_b, w_o, attn_norm,
    ffn_norm, w_gate, w_up, w_down, final_norm, norm_mix_pre_2, norm_mix_post_2, norm_mlp_pre_2,
    norm_mlp_post_2, w_in_2, rel_bias_2, sinks_2, lam_re_2, lam_im_2, log_dt_2, b_re_2, b_im_2,
    c_re_2, c_im_2, d_skip_2, w_glu_2, w_attn_branch_2, w_ssm_branch_2, w_out_2, w_ff_in_2,
    w_ff_out_2,
):
    x = first_block(
        x, positions, w_in, da_lambda, da_norm, hg_lb_logits, hg_norm, w_a, w_b, w_o, attn_norm,
        ffn_norm, w_gate, w_up, w_down, final_norm,
    )
    return second_block(
        x, norm_mix_pre_2, norm_mix_post_2, norm_mlp_pre_2, norm_mlp_post_2, w_in_2, rel_bias_2,
        sinks_2, lam_re_2, lam_im_2, log_dt_2, b_re_2, b_im_2, c_re_2, c_im_2, d_skip_2,
        w_glu_2, w_attn_branch_2, w_ssm_branch_2, w_out_2, w_ff_in_2, w_ff_out_2,
    )


_drawn_inputs = setup_inputs


def setup_inputs(seed=0):
    import zlib

    import numpy as np

    out = dict(_drawn_inputs(seed))
    spreads = {}
    factors = {'da_norm': 3.727,
     'hg_norm': 6.02,
     'ffn_norm': 2.699,
     'sinks_2': 8.0,
     'lam_re_2': 64.0,
     'b_re_2': 3.062,
     'b_im_2': 3.071,
     'c_re_2': 3.086,
     'c_im_2': 3.091}
    for name, (base, spread) in spreads.items():
        noise = np.random.default_rng([zlib.crc32(name.encode()), seed]).standard_normal(out[name].shape)
        drawn = base * np.exp(spread * noise) if base else spread * noise
        out[name] = __import__('jax').numpy.asarray(drawn.astype(out[name].dtype))
    for name, factor in factors.items():
        out[name] = (out[name] * factor).astype(out[name].dtype)
    return out
```

```python
import math
from contextlib import ExitStack

import numpy as np

import concourse.bass as bass
from concourse import mybir

F32 = mybir.dt.float32
F32R = mybir.dt.float32r
I32 = mybir.dt.int32
U8 = mybir.dt.uint8
ALU = mybir.AluOpType
ACT = mybir.ActivationFunctionType
AX = mybir.AxisListType
ds = bass.ds

P = 128
D = 1024
S = 512
KD = D // P
TB = S // P
DEPTH = 2
HEADS = 4
BW = HEADS * P
FT = -(-8 * D // (3 * 256)) * 2
EPS = 1e-6
UC = 256
UNIT = KD * UC

C_AQ, C_AK, C_AV, C_BQ, C_BFF, C_BFB, C_BI, C_BG, C_GA, C_GB = (
    0, 512, 1024, 1536, 2048, 2560, 3072, 3584, 4096, 5120)
WIN_RUNS = [(C_BFF, 2), (C_BQ, 1), (C_BI, 1), (C_AQ, 3), (C_BG, 5)]

U_BFF, U_BQ, U_BI, U_ATT, U_BG, U_GATES, U_WA, U_WB, U_WO, U_GU, U_DN, U_LAYER = (
    0, 2, 3, 4, 7, 8, 12, 13, 14, 16, 27, 33)
J_WA, J_WB, J_WO, J_GU, J_DN, J_LAYER = 12, 14, 16, 18, 29, 31

QH, KVH, HD = 8, 2, 64
D_FF = 4 * D
GROUPS, GC, NS = 32, 16, 64
PAIRS = GROUPS // 2
CT = 8
CH = S // CT
NEG = -1e30
U_SECOND = 27
C2_Q, C2_K, C2_V, C2_U, C2_GA, C2_GB = 0, 512, 640, 768, 1280, 2304

TWO_PI = 2 * math.pi
PI_HI = 6.28125
PI_MID = float(np.float32(np.floor((TWO_PI - PI_HI) * 2**21) / 2**21))
PI_LO = float(np.float32(TWO_PI - PI_HI - PI_MID))
GELU = 2 * math.sqrt(2 / math.pi)
ROUND = 1.5 * 2**23
PI_MAX = 3.1415925

R_ATTN, R_FFN, R_DA, R_HG, R_LB, R_FINAL, R_PRE2, R_POST2, R_MPRE2, R_MPOST2, R_ALL = (
    0, 16, 32, 40, 48, 64, 72, 80, 88, 96, 104)
L_ATTN, L_FFN, L_DA, L_HG, L_LB, L_OMLB, L_NLAM, L_ALL = 0, 8, 16, 20, 24, 32, 40, 41

KB = 1024


class Signal:

    def __init__(self, sem, per_layer=0, credit=0):
        self.sem, self.per, self.credit = sem, per_layer, credit

    def at(self, layer, k):
        return layer * self.per + (k + self.credit)


def step(m, s, k):
    return m + (s + k) // 2, (s + k) % 2


def lam_init(layer):
    return 0.8 - 0.6 * math.exp(-0.3 * layer)


def t5_bucket(d, buckets=32, most=128):
    exact = buckets // 2
    if d < exact:
        return d
    f = np.float32(np.log(np.float32(d) / np.float32(exact))) / np.float32(math.log(most / exact))
    return min(exact + int(np.float32(f) * np.float32(buckets - exact)), buckets - 1)


def build_kernel(nc, io, stop_after=None):
    with ExitStack() as ctx:
        build_in(nc, io, ctx)


def build_in(nc, io, ctx):
    def sb(name, shape, dt=F32):
        return ctx.enter_context(nc.sbuf_tensor(name, shape, dt))

    def sem(name, per_layer=0, credit=0):
        return Signal(ctx.enter_context(nc.semaphore(name)), per_layer, credit)

    xT = sb("xT", [P, KD, S])
    h_hi_at = nc.sbuf_base
    h_hi = sb("h_hi", [P, KD, S], F32R)
    h_lo_at = nc.sbuf_base
    h_lo = sb("h_lo", [P, KD, S], F32R)
    raw = sb("raw", [P, 2, UNIT])
    w_hi = sb("w_hi", [P, 2, UNIT], F32R)
    w_lo = sb("w_lo", [P, 2, UNIT], F32R)
    ident = sb("ident", [P, P])
    ones = sb("ones", [P, 2])
    par = sb("par", [P, R_ALL])
    lay = sb("lay", [P, DEPTH, L_ALL])
    cur = sb("cur", [P, L_ALL])
    lbw = sb("lbw", [P, 5, 2, HEADS])
    s5_at = nc.sbuf_base
    masks = sb("masks", [P, 7, P], U8)
    ropec = sb("ropec", [P, TB, 8])
    ropes = sb("ropes", [P, TB, 8])
    ropew = sb("ropew", [P, 3, TB, 8])
    small = sb("small", [P, 64])
    stat = sb("stat", [P, 2, 8])
    exch = sb("exch", [P, P])
    d_col = sb("d_col", [P, CT])
    eye16 = sb("eye16", [P, GC])
    sink = sb("sink", [P, QH])
    st2 = sb("st2", [P, 6, 4])
    ARENA = 107 * KB
    base = nc.sbuf_base
    sb("arena", [P, ARENA // 4])

    def at(name, kb, shape, dt=F32):
        n = 4 * int(np.prod(shape[1:])) if dt != U8 else int(np.prod(shape[1:]))
        assert kb * KB + n <= ARENA, name
        return nc.alloc_sbuf_tensor_at(name, shape, dt, offset=base + int(kb * KB))

    h_tmp = nc.alloc_sbuf_tensor_at("h_tmp", [P, KD, S], F32, offset=h_lo_at)

    x_tok = at("x_tok", 0, [P, TB, D])
    par_rows = at("par_rows", 16, [R_ALL, P])
    lam_rows = at("lam_rows", 20, [P, DEPTH * 4, 64])
    pos_i = at("pos_i", 24, [P, TB], I32)
    pos_f = at("pos_f", 25, [P, TB])
    iota_s = at("iota_s", 26, [P, P], I32)
    iota_t = at("iota_t", 27, [P, P], I32)
    xor = at("xor", 28, [P, P], I32)
    Qf = at("Qf", 0, [P, HEADS, S])
    Kf = at("Kf", 8, [P, HEADS, S])
    Qb = at("Qb", 16, [P, HEADS, S])
    Kb = at("Kb", 24, [P, HEADS, S])
    Tx = at("Tx", 32, [P, 2, HEADS * S])
    Ty = at("Ty", 48, [P, 2, HEADS * S // 2])
    s_diag = at("s_diag", 56, [P, HEADS, S])
    b_v = at("b_v", 64, [P, TB, BW])
    s_mate = at("s_mate", 72, [P, HEADS, TB, P])
    s_far = at("s_far", 32, [P, 2, 2 * TB, P])
    ob = at("ob", 40, [P, HEADS, S])
    a_q = at("a_q", 80, [P, TB, BW])
    a_k = at("a_k", 88, [P, TB, BW])
    a_v = at("a_v", 96, [P, TB, BW])
    qT = at("qT", 0, [P, HEADS, S])
    kT = at("kT", 8, [P, HEADS, S])
    prob = at("prob", 16, [P, 2, 2, S])
    wdiff = at("wdiff", 24, [P, 2, S])
    wT = at("wT", 48, [P, 2, TB, S])
    oa = at("oa", 32, [P, HEADS, S])
    sq_b = at("sq_b", 0, [P, HEADS, S])
    sq_a = at("sq_a", 16, [P, HEADS, S])
    rope_w = at("rope_w", 64, [P, 4, TB, 8, 8])
    rope_w2 = at("rope_w2", 68, [P, 4, TB, 8, 8])
    ga = at("ga", 0, [P, KD, S])
    gb = at("gb", 16, [P, KD, S])
    o_hi = at("o_hi", 64, [P, 2 * HEADS, S], F32R)
    o_lo = at("o_lo", 80, [P, 2 * HEADS, S], F32R)
    sg = at("sg", 96, [P, HEADS, S])
    m_hi = at("m_hi", 32, [P, KD, S], F32R)
    m_lo = at("m_lo", 48, [P, KD, S], F32R)
    hid_hi = at("hid_hi", 0, [P, FT, S], F32R)
    hid_lo = at("hid_lo", 44, [P, FT, S], F32R)
    sgu = at("sgu", 88, [P, 2, S])
    ht = at("ht", 92, [P, 2, S])
    q2 = at("q2", 0, [P, 4, S])
    k2 = at("k2", 8, [P, S])
    v2 = at("v2", 10, [P, TB, P])
    g2a = at("g2a", 12, [P, KD, S])
    g2b = at("g2b", 28, [P, KD, S])
    uc = at("uc", 44, [P, GROUPS, 4, GC])
    U = at("U", 60, [P, GROUPS, CH])
    Wt = at("Wt", 68, [P, 2, PAIRS, CT + 1, GC])
    Et = at("Et", 44, [P, 2, PAIRS, CT, GC])
    wt_tmp = at("wt_tmp", 44, [P, PAIRS, CT + 1, GC])
    bias = at("bias", 86.5, [P, QH, 2 * P])
    k_pad = at("k_pad", 86.5, [P, CT, 2 * P])
    him = at("him", 86.5, [P, PAIRS, CH])
    b_re, b_im = at("b_re", 94.5, [P, PAIRS, GC]), at("b_im", 95.5, [P, PAIRS, GC])
    c_tok = at("c_tok", 96.5, [P, 2, 4, 2, NS])
    c_t = at("c_t", 100.5, [P, 2, PAIRS, GC])
    e_tmp = at("e_tmp", 94.5, [P, PAIRS, CT, GC])
    lg = at("lg", 94.5, [P, 4, 2 * P])
    pT = at("pT", 98.5, [P, 2, 4 * P])
    rot = at("rot", 94.5, [P, 2, PAIRS, CH])
    bb = at("bb", 102.5, [P, 2, PAIRS, GC])
    hre = at("hre", 102.5, [P, PAIRS, CH])
    pw = at("pw", 104.5, [P, 2, PAIRS, CT + 1])
    pr = at("pr", 105.6875, [P, 2, PAIRS, CT])
    d0 = at("d0", 8, [P, PAIRS, CH])
    s5 = nc.alloc_sbuf_tensor_at("s5", [P, 16, PAIRS], F32, offset=s5_at)
    s_rows = at("s_rows", 60, [16, 2])
    s_log = at("s_log", 60.5, [16, 2, NS])
    s_lam = at("s_lam", 61, [32, P])
    s_eye = at("s_eye", 8, [P, CT, GC])
    t5_rows = at("t5_rows", 62, [QH, 3 * P])
    t5_rb = at("t5_rb", 64, [QH, 32])
    t5_up = at("t5_up", 12, [P, QH, 2 * P])
    s_tmp = at("s_tmp", 44, [P, 3, PAIRS, CH])
    yt = at("yt", 44, [CH, CT, GROUPS * GC])
    z2 = at("z2", 60, [P, 4, S])
    z_w = at("z_w", 44, [P, 2, 4, S])
    Win = nc.alloc_sbuf_tensor_at("Win", [P, 2, PAIRS, P], F32, offset=h_hi_at)
    Toep = nc.alloc_sbuf_tensor_at("Toep", [P, GROUPS, P], F32, offset=h_lo_at)
    z_hi = at("z_hi", 68, [P, 4, S], F32R)
    z_lo = at("z_lo", 76, [P, 4, S], F32R)
    zz_hi = nc.alloc_sbuf_tensor_at("zz_hi", [P, 4, S], F32R, offset=h_hi_at)
    zz_lo = nc.alloc_sbuf_tensor_at("zz_lo", [P, 4, S], F32R, offset=h_hi_at + 8 * KB)
    o2_hi = nc.alloc_sbuf_tensor_at("o2_hi", [P, 4, S], F32R, offset=h_lo_at)
    o2_lo = nc.alloc_sbuf_tensor_at("o2_lo", [P, 4, S], F32R, offset=h_lo_at + 8 * KB)
    m2_hi = at("m2_hi", 44, [P, KD, S], F32R)
    m2_lo = at("m2_lo", 84, [P, KD, S], F32R)
    HT2 = D_FF // P // 2
    hid2_hi = at("hid2_hi", 0, [P, HT2, S], F32R)
    hid2_lo = at("hid2_lo", 32, [P, HT2, S], F32R)
    y2 = at("y2", 64, [P, KD, S])
    r2 = at("r2", 80, [P, 2, S])
    hq2 = at("hq2", 84, [P, 2, S])
    x_out = at("x_out", 0, [P, TB, D])
    t5_dram = nc.dram_tensor("t5_dram", (QH, 3 * P), F32, kind="Internal").ap()

    psG = ctx.enter_context(nc.psum_tensor("psG", [P, 4, S], F32))
    psH = ctx.enter_context(nc.psum_tensor("psH", [P, 4, S], F32))

    NORMS = 4
    NT = 2 * KD + HEADS
    raw_in = [sem("raw_in0"), sem("raw_in1")]
    hi_done = sem("hi_done")
    lo_done = sem("lo_done", credit=2)
    tick = sem("tick", credit=4)
    psum_free = [sem("psum_free0", credit=1), sem("psum_free1", credit=1)]
    ld_x, ld_par, ld_misc = sem("ld_x"), sem("ld_par"), sem("ld_misc")
    consts = sem("consts")
    setup = sem("setup")
    setup_pe = sem("setup_pe")
    setup_act = sem("setup_act")
    x_tr = sem("x_tr")
    x_cp = sem("x_cp")
    x_cp2 = sem("x_cp2")
    n_sq = sem("n_sq", NORMS)
    n_ss = sem("n_ss", NORMS)
    n_sd = sem("n_sd", NORMS)
    n_rs = sem("n_rs", NORMS)
    n_rb = sem("n_rb", NORMS)
    n_tmp = sem("n_tmp", NT)
    n_hi = sem("n_hi", NT)
    n_lo = sem("n_lo", NT)
    x_done = sem("x_done", 2 * KD, credit=KD)
    b_sig = sem("b_sig", 4)
    b_q = sem("b_q", 2)
    b_tok = sem("b_tok", 2)
    lev_up = sem("lev_up", 10)
    lev_mm = sem("lev_mm", 9)
    lev_cp = sem("lev_cp", 8)
    mate_cp = sem("mate_cp", 1)
    far_mm = sem("far_mm", HEADS)
    far_cp = sem("far_cp", HEADS)
    av_mm = sem("av_mm", HEADS)
    av_cp = sem("av_cp", HEADS)
    a_tok = sem("a_tok", 6)
    rope_d = sem("rope_d", 2)
    qk_tr = sem("qk_tr", 8)
    qk_cp = sem("qk_cp", 8)
    sc_mm = sem("sc_mm", 32)
    sc_max = sem("sc_max", 32)
    sc_exp = sem("sc_exp", 32)
    w_done = sem("w_done", 16)
    w_tr = sem("w_tr", 16)
    w_cp = sem("w_cp", 16)
    oa_mm = sem("oa_mm", HEADS)
    oa_cp = sem("oa_cp", HEADS)
    g_sig = sem("g_sig", 3)
    g_mul = sem("g_mul", 4)
    g_hi = sem("g_hi", 4)
    g_lo = sem("g_lo", 4)
    m_sum = sem("m_sum", 8)
    m_hid = sem("m_hid", 8)
    m_lod = sem("m_lod", 8)
    f_sig = sem("f_sig", FT)
    f_mul = sem("f_mul", FT, credit=2)
    f_hid = sem("f_hid", FT)
    f_lod = sem("f_lod", FT)
    st_out = sem("st_out")

    block = ctx.enter_context(nc.Block())

    def w_src(m, s, src, eng):
        eng.wait_ge(lo_done.sem, m * 2 + (s + 1))
        k, c = src.shape[1], src.shape[2]
        dst = raw[:, s, 0:k * c].rearrange("p (k c) -> p k c", k=k)
        for half in (slice(0, 64), slice(64, P)):
            eng.dma_start(dst[half], src[half]).then_inc(raw_in[s].sem, 16)

    def split_hi(act, m, s):
        act.wait_ge(raw_in[s].sem, m * 32 + 32)
        act.wait_ge(tick.sem, m * 4 + (2 * s + 2))
        act.copy(w_hi[:, s, :], raw[:, s, :]).then_inc(hi_done.sem, 1)

    def T(m, s, half):
        return m * 4 + (2 * s + 1 + half + tick.credit)

    def triple(pe, out, a_hi, a_lo, b_hi, b_lo, first, last):
        pe.matmul(out, a_hi, b_hi, start=first, stop=False)
        pe.matmul(out, a_hi, b_lo, start=False, stop=False)
        return pe.matmul(out, a_lo, b_hi, start=False, stop=last)

    def unit_ready(pe, m, s):
        pe.wait_ge(lo_done.sem, m * 2 + (s + 1 + lo_done.credit))

    def bank_ready(pe, jm, b):
        pe.wait_ge(psum_free[b].sem, jm + 1)

    def pe_feature(pe, m, s, jm, b, x_hi, x_lo, k_wait=None):
        unit_ready(pe, m, s)
        bank_ready(pe, jm, b)
        wh = w_hi[:, s, :].rearrange("p (k c) -> p k c", k=KD)
        wl = w_lo[:, s, :].rearrange("p (k c) -> p k c", k=KD)
        for j in range(2):
            for k in range(KD):
                if k_wait is not None and j == 0:
                    k_wait(k)
                c = slice(j * P, (j + 1) * P)
                mm = triple(pe, psG[:, 2 * b + j, :], wh[:, k, c], wl[:, k, c], x_hi[:, k, :], x_lo[:, k, :],
                            k == 0, k == KD - 1)
            mm.then_inc(tick.sem, 1)

    def pe_token(pe, m, s, jm, b):
        unit_ready(pe, m, s)
        bank_ready(pe, jm, b)
        wh = w_hi[:, s, :].rearrange("p (k c) -> p k c", k=KD)
        wl = w_lo[:, s, :].rearrange("p (k c) -> p k c", k=KD)
        for t in range(TB):
            for k in range(KD):
                c = slice(t * P, (t + 1) * P)
                out = psG[:, 2 * b + t // 2, (t % 2) * UC:(t % 2 + 1) * UC]
                mm = triple(pe, out, h_hi[:, k, c], h_lo[:, k, c], wh[:, k, :], wl[:, k, :], k == 0, k == KD - 1)
            if t % 2:
                mm.then_inc(tick.sem, 1)

    def pe_branch(pe, m, s, jm, x_hi, x_lo, k0):
        unit_ready(pe, m, s)
        wh = w_hi[:, s, :].rearrange("p (k c) -> p k c", k=4)
        wl = w_lo[:, s, :].rearrange("p (k c) -> p k c", k=4)
        for j in range(4):
            if j % 2 == 0:
                bank_ready(pe, jm, j // 2)
            for k in range(4):
                c = slice(j * P, (j + 1) * P)
                mm = triple(pe, psG[:, j, :], wh[:, k, c], wl[:, k, c], x_hi[:, k0 + k, :], x_lo[:, k0 + k, :],
                            k == 0, k == 3)
            if j % 2:
                mm.then_inc(tick.sem, 1)

    def norm_act(act, layer, i, t0, src, sq, groups, width, tmp=None, hi=None):
        act.activation(sq, src, ACT.Square).then_inc(n_sq.sem, 1)
        act.wait_ge(n_ss.sem, n_ss.at(layer, i + 1))
        act.activation(small[:, 0:TB * len(groups)], psH[:, 0, 0:TB * len(groups)], ACT.Sqrt,
                       scale=1.0 / width, bias=eps_ap).then_inc(n_sd.sem, 1)
        if hi is not None:
            for k in range(sum(len(g) for g in groups)):
                act.wait_ge(n_tmp.sem, n_tmp.at(layer, t0 + k + 1))
                act.copy(hi(k), tmp[:, k, :]).then_inc(n_hi.sem, 1)

    def norm_pe(pe, layer, i, sq, groups):
        pe.wait_ge(n_sq.sem, n_sq.at(layer, i + 1))
        for g, tiles in enumerate(groups):
            for t in range(TB):
                for n, k in enumerate(tiles):
                    mm = pe.matmul(psH[:, 0, g * TB + t:g * TB + t + 1], sq[:, k, t * P:(t + 1) * P],
                                   ones[:, 0:1], start=n == 0, stop=n == len(tiles) - 1)
        mm.then_inc(n_ss.sem, 1)
        pe.wait_ge(n_rs.sem, n_rs.at(layer, i + 1))
        for g in range(len(groups)):
            for t in range(TB):
                c = g * TB + t
                mm = pe.matmul(psH[:, g, t * P:(t + 1) * P], small[:, 16 + c:17 + c].broadcast_to([P, P]),
                               ident[:, :], start=True, stop=True)
        mm.then_inc(n_rb.sem, 1)

    def norm_dve_head(dve, layer, i, groups):
        n = TB * len(groups)
        dve.wait_ge(n_sd.sem, n_sd.at(layer, i + 1))
        dve.reciprocal(small[:, 16:16 + n], small[:, 0:n]).then_inc(n_rs.sem, 1)
        dve.wait_ge(n_rb.sem, n_rb.at(layer, i + 1))

    def norm_dve_split(dve, layer, i, t0, src, tmp, gain, groups, hi, lo):
        norm_dve_head(dve, layer, i, groups)
        n = sum(len(g) for g in groups)
        for k in range(n + 1):
            if k < n:
                g = next(j for j, tiles in enumerate(groups) if k in tiles)
                dve.scalar_tensor_tensor(out=tmp[:, k, :], in0=src[:, k, :], scalar=gain[:, k:k + 1],
                                         in1=psH[:, g, :], op0=ALU.mult, op1=ALU.mult).then_inc(n_tmp.sem, 1)
            if k > 0:
                dve.wait_ge(n_hi.sem, n_hi.at(layer, t0 + k))
                dve.tensor_tensor(lo(k - 1), tmp[:, k - 1, :], hi(k - 1).bitcast(F32), ALU.subtract)\
                   .then_inc(n_lo.sem, 1)

    ALL8 = [list(range(KD))]
    EACH4 = [[k] for k in range(HEADS)]
    eps_ap = small[:, 48:49]

    def h_hi_t(k):
        return h_hi[:, k, :]

    def h_lo_t(k):
        return h_lo[:, k, :]

    T_ATTN, T_DA, T_FFN = 0, KD, KD + HEADS

    def halves(x, h):
        return x[:, :, :].rearrange("p a (n two i) -> p (a n) two i", two=2, i=h)

    def totals(level):
        n = HEADS * S >> level
        t = Tx if level % 2 == 0 else Ty
        return t[:, :, 0:n]


    ALL_PAIRS = DEPTH * U_LAYER + U_SECOND

    def level_update(dve, h):
        if h == 1:
            dve.tensor_tensor(Qb[:, :, :], Qf[:, :, :], Tx[:, 1, :].rearrange("p (a t) -> p a t", a=HEADS), ALU.mult)
            dve.drain()
            dve.tensor_tensor(Qf[:, :, :], Qf[:, :, :], Tx[:, 0, :].rearrange("p (a t) -> p a t", a=HEADS),
                              ALU.mult).then_inc(lev_up.sem, 1)
            return
        b = h // 2
        lg = b.bit_length() - 1
        n = HEADS * S // (2 * b)
        t = totals(lg).rearrange("p d (n two) -> p d n two", two=2)
        if h < 2 * P:
            dve.tensor_tensor(totals(lg + 1), t[:, :, :, 0], t[:, :, :, 1], ALU.mult)
        for x, side, d in ((Qf, 1, 0), (Kf, 0, 0), (Qb, 0, 1), (Kb, 1, 1)):
            part = halves(x, b)[:, :, side, :]
            mm = dve.tensor_tensor(part, part, t[:, d, :, 1 - side:2 - side].broadcast_to([P, n, b]), ALU.mult)
        mm.then_inc(lev_up.sem, 1)

    def level_pe(pe, layer, lv):
        pe.wait_ge(lev_up.sem, lev_up.at(layer, lv + 1))
        if lv == 0:
            pe.wait_ge(b_q.sem, b_q.at(layer, 2))
        else:
            pe.wait_ge(lev_cp.sem, lev_cp.at(layer, lv))
        for a in range(HEADS):
            for blk in range(TB):
                c = slice(blk * P, (blk + 1) * P)
                out = psH[:, a, c]
                if lv == 0:
                    pe.matmul(out, Kf[:, a, c], Qf[:, a, c], start=True, stop=False)
                    mm = pe.matmul(out, Kb[:, a, c], Qf[:, a, c], start=False, stop=True)
                    continue
                for k, q, side in ((Kf, Qf, 1), (Kb, Qb, 0)):
                    cut = "p (n two i) -> p n two i"
                    i = 1 << (lv - 1)
                    mm = pe.matmul(out.rearrange(cut, two=2, i=i)[:, :, side, :], k[:, a, c],
                                   q[:, a, c].rearrange(cut, two=2, i=i)[:, :, side, :], start=True, stop=True)
        mm.then_inc(lev_mm.sem, 1)

    def level_copy(dve, layer, lv):
        dve.wait_ge(lev_mm.sem, lev_mm.at(layer, lv + 1))
        if lv:
            dve.memset(small[:, 63:64], 0.0)
        for a in range(HEADS):
            if lv == 0:
                mm = dve.tensor_copy(s_diag[:, a, :], psH[:, a, :])
            else:
                m = masks[:, lv - 1:lv, :].broadcast_to([P, TB, P])
                mm = dve.copy_predicated(s_diag[:, a, :].rearrange("p (b t) -> p b t", b=TB), m,
                                         psH[:, a, :].rearrange("p (b t) -> p b t", b=TB))
        mm.then_inc(lev_cp.sem, 1)
        dve.wait_ge(lev_cp.sem, lev_cp.at(layer, lv + 1))

    def blk(x, a, j):
        return x[:, a, j * P:(j + 1) * P]

    def mate_pe(pe, layer):
        pe.wait_ge(lev_up.sem, lev_up.at(layer, 9))
        pe.wait_ge(lev_cp.sem, lev_cp.at(layer, 8))
        for a in range(HEADS):
            for s in range(TB):
                k, q = (Kf, Qf) if s % 2 == 0 else (Kb, Qb)
                mm = pe.matmul(psH[:, a, s * P:(s + 1) * P], blk(k, a, s), blk(q, a, s ^ 1), start=True, stop=True)
        mm.then_inc(lev_mm.sem, 1)

    def far_pe(pe, layer, a):
        pe.wait_ge(lev_up.sem, lev_up.at(layer, 10))
        if a == 0:
            pe.wait_ge(mate_cp.sem, mate_cp.at(layer, 1))
        else:
            pe.wait_ge(far_cp.sem, far_cp.at(layer, a))
        for s in range(TB):
            k, q = (Kf, Qf) if s < 2 else (Kb, Qb)
            t0 = 2 * P if s < 2 else 0
            mm = pe.matmul(psH[:, s // 2, (s % 2) * 2 * P:(s % 2 + 1) * 2 * P], blk(k, a, s),
                           q[:, a, t0:t0 + 2 * P], start=True, stop=True)
        mm.then_inc(far_mm.sem, 1)

    def hgrn_out_pe(pe, layer, a):
        pe.wait_ge(far_cp.sem, far_cp.at(layer, a + 1))
        pe.wait_ge(b_tok.sem, b_tok.at(layer, 2))
        if a >= 2:
            pe.wait_ge(av_cp.sem, av_cp.at(layer, a - 1))
        for t in range(TB):
            for s in range(TB):
                if s == t:
                    sc = blk(s_diag, a, t)
                elif s == t ^ 1:
                    sc = s_mate[:, a, s, :]
                else:
                    sc = s_far[:, a % 2, 2 * s + t % 2, :]
                mm = pe.matmul(psH[:, 2 + a % 2, t * P:(t + 1) * P], b_v[:, s, a * P:(a + 1) * P], sc,
                               start=s == 0, stop=s == TB - 1)
        mm.then_inc(av_mm.sem, 1)

    def rope(dve, layer):
        for n, x in enumerate((a_q, a_k)):
            dve.wait_ge(a_tok.sem, a_tok.at(layer, 2 * n + 2))
            v = x[:, :, :].rearrange("p t (c d) -> p t c d", d=64)
            w = rope_w if n == 0 else rope_w2
            for t in range(TB):
                cos = ropec[:, t:t + 1, :].broadcast_to([P, 8, 8])
                sin = ropes[:, t:t + 1, :].broadcast_to([P, 8, 8])
                t1, t2 = v[:, t, :, 0:8], v[:, t, :, 8:16]
                for j, (a, b) in enumerate(((t1, cos), (t2, sin), (t2, cos), (t1, sin))):
                    dve.tensor_tensor(w[:, j, t], a, b, ALU.mult)
            dve.drain()
            for t in range(TB):
                dve.tensor_tensor(v[:, t, :, 0:8], w[:, 0, t], w[:, 1, t], ALU.subtract)
                mm = dve.tensor_tensor(v[:, t, :, 8:16], w[:, 2, t], w[:, 3, t], ALU.add)
            mm.then_inc(rope_d.sem, 1)

    def qk_pe(pe, layer):
        for n, x in enumerate((a_q, a_k)):
            pe.wait_ge(rope_d.sem, rope_d.at(layer, n + 1))
            for a in range(HEADS):
                i = n * HEADS + a
                if n:
                    pe.wait_ge(qk_cp.sem, qk_cp.at(layer, i - 3))
                for t in range(TB):
                    mm = pe.transpose(psH[:, a, t * P:(t + 1) * P], x[:, t, a * P:(a + 1) * P], ident[:, :])
                mm.then_inc(qk_tr.sem, 1)

    def qk_act(act, layer):
        for i in range(2 * HEADS):
            act.wait_ge(qk_tr.sem, qk_tr.at(layer, i + 1))
            if i < HEADS:
                act.activation(qT[:, i, :], psH[:, i, :], ACT.Copy, scale=64 ** -0.5).then_inc(qk_cp.sem, 1)
            else:
                act.copy(kT[:, i - HEADS, :], psH[:, i - HEADS, :]).then_inc(qk_cp.sem, 1)

    STEPS = HEADS * TB

    def attention_pe(pe, layer):
        pe.wait_ge(qk_cp.sem, qk_cp.at(layer, 8))
        pe.wait_ge(a_tok.sem, a_tok.at(layer, 6))
        for it in range(STEPS + 2):
            if it < STEPS:
                a, qb = divmod(it, TB)
                if it >= 2:
                    pe.wait_ge(sc_exp.sem, sc_exp.at(layer, 2 * it - 2))
                for c in range(2):
                    d = slice(64 * c, 64 * c + 64)
                    pe.matmul(psG[:, 2 * (it % 2) + c, :], qT[d, a, qb * P:(qb + 1) * P], kT[d, a, :],
                              start=True, stop=True).then_inc(sc_mm.sem, 1)
            if 1 <= it <= STEPS:
                j = it - 1
                pe.wait_ge(w_done.sem, w_done.at(layer, j + 1))
                if j >= 2:
                    pe.wait_ge(w_cp.sem, w_cp.at(layer, j - 1))
                for s in range(TB):
                    mm = pe.transpose(psH[:, j % 2, s * P:(s + 1) * P], wdiff[:, j % 2, s * P:(s + 1) * P],
                                      ident[:, :])
                mm.then_inc(w_tr.sem, 1)
            if it >= 2 and (it - 2) % TB == TB - 1:
                a = (it - 2) // TB
                pe.wait_ge(w_cp.sem, w_cp.at(layer, TB * (a + 1)))
                if a >= 2:
                    pe.wait_ge(oa_cp.sem, oa_cp.at(layer, a - 1))
                for s in range(TB):
                    mm = pe.matmul(psH[:, 2 + a % 2, :], a_v[:, s, a * P:(a + 1) * P], wT[:, a % 2, s, :],
                                   start=s == 0, stop=s == TB - 1)
                mm.then_inc(oa_mm.sem, 1)

    def attention_act(act, layer):
        for it in range(STEPS + 1):
            if it < STEPS:
                if it >= 2:
                    act.wait_ge(w_done.sem, w_done.at(layer, it - 1))
                for c in range(2):
                    act.wait_ge(sc_max.sem, sc_max.at(layer, 2 * it + c + 1))
                    act.activation(prob[:, it % 2, c, :], psG[:, 2 * (it % 2) + c, :], ACT.Exp,
                                   bias=stat[:, it % 2, c:c + 1],
                                   accum_out=stat[:, it % 2, 2 + c:3 + c]).then_inc(sc_exp.sem, 1)
            if it >= 1:
                j = it - 1
                a, qb = divmod(j, TB)
                act.wait_ge(w_tr.sem, w_tr.at(layer, j + 1))
                if a >= 2 and qb == 0:
                    act.wait_ge(oa_mm.sem, oa_mm.at(layer, a - 1))
                act.copy(wT[:, a % 2, :, qb * P:(qb + 1) * P],
                         psH[:, j % 2, :].rearrange("p (s q) -> p s q", s=TB)).then_inc(w_cp.sem, 1)

    def attention_dve(dve, layer):
        for it in range(STEPS + 3):
            if it < STEPS:
                if it >= 2:
                    dve.wait_ge(w_done.sem, w_done.at(layer, it - 1))
                for c in range(2):
                    dve.wait_ge(sc_mm.sem, sc_mm.at(layer, 2 * it + c + 1))
                    dve.tensor_reduce(stat[:, it % 2, c:c + 1], psG[:, 2 * (it % 2) + c, :], AX.X, ALU.max,
                                      negate=True).then_inc(sc_max.sem, 1)
            if 1 <= it <= STEPS:
                j = it - 1
                st = stat[:, j % 2, :]
                dve.wait_ge(sc_exp.sem, sc_exp.at(layer, 2 * j + 2))
                dve.reciprocal(st[:, 4:6], st[:, 2:4])
                dve.drain()
                dve.tensor_scalar(st[:, 6:7], st[:, 5:6], cur[:, L_NLAM:L_NLAM + 1], None, ALU.mult)
                dve.tensor_scalar(prob[:, j % 2, 0, :], prob[:, j % 2, 0, :], st[:, 4:5], None, ALU.mult)
                dve.drain()
                if j >= 2:
                    dve.wait_ge(w_tr.sem, w_tr.at(layer, j - 1))
                dve.scalar_tensor_tensor(out=wdiff[:, j % 2, :], in0=prob[:, j % 2, 1, :], scalar=st[:, 6:7],
                                         in1=prob[:, j % 2, 0, :], op0=ALU.mult, op1=ALU.add)\
                   .then_inc(w_done.sem, 1)
            if it >= 3 and (it - 3) % TB == TB - 1:
                a = (it - 3) // TB
                dve.wait_ge(oa_mm.sem, oa_mm.at(layer, a + 1))
                dve.tensor_copy(oa[:, a, :], psH[:, 2 + a % 2, :]).then_inc(oa_cp.sem, 1)

    inv_freq = [float(np.float32(500000.0) ** np.float32(-i / 16)) for i in range(0, 16, 2)]

    def reduce_angle(dve, out, ang, k, cosine):
        dve.tensor_scalar(k, ang, 1 / TWO_PI, 0.25 if cosine else 0.0, ALU.mult, ALU.add)
        dve.drain()
        dve.tensor_scalar(k, k, ROUND, ROUND, ALU.add, ALU.subtract)
        dve.drain()
        dve.scalar_tensor_tensor(out=out, in0=k, scalar=-PI_HI, in1=ang, op0=ALU.mult, op1=ALU.add)
        dve.drain()
        dve.scalar_tensor_tensor(out=out, in0=k, scalar=-PI_MID, in1=out, op0=ALU.mult, op1=ALU.add)
        dve.drain()
        dve.scalar_tensor_tensor(out=out, in0=k, scalar=-PI_LO, in1=out, op0=ALU.mult, op1=ALU.add)
        dve.drain()
        if cosine:
            dve.tensor_scalar(out, out, math.pi / 2, None, ALU.add)
            dve.drain()
        return dve.tensor_scalar(out, out, PI_MAX, -PI_MAX, ALU.min, ALU.max)

    def setup_pool(pool):
        pool.sem_inc(lo_done.sem, lo_done.credit)
        pool.memset(ident[:, :], 0.0).then_inc(consts.sem, 1)
        pool.memset(ones[:, :], 1.0).then_inc(consts.sem, 1)
        pool.memset(small[:, 48:49], EPS).then_inc(consts.sem, 1)
        pool.iota(iota_s[:, :], [[0, P]], base=0, channel_multiplier=1).then_inc(consts.sem, 1)
        pool.iota(iota_t[:, :], [[1, P]], base=0, channel_multiplier=0).then_inc(consts.sem, 1)
        pool.wait_ge(consts.sem, 5)
        pool.affine_select(out=ident[:, :], in_=ident[:, :], compare_op=ALU.not_equal, fill=1.0, base=0,
                           pattern=[[-1, P]], channel_multiplier=1).then_inc(consts.sem, 1)

    def setup_sync(sp):
        sp.dma_start(x_tok[:, :, :], io["x"].rearrange("a (t p) d -> p (a t) d", p=P)).then_inc(ld_x.sem, 16)
        rows = [(R_ATTN, io["attn_norm"].rearrange("l (k p) -> (l k) p", p=P)),
                (R_FFN, io["ffn_norm"].rearrange("l (k p) -> (l k) p", p=P)),
                (R_DA, io["da_norm"].rearrange("l (k p) -> (l k) p", p=P)),
                (R_HG, io["hg_norm"].rearrange("l (k p) -> (l k) p", p=P)),
                (R_LB, io["hg_lb_logits"].rearrange("d l (k p) -> (d l k) p", p=P)),
                (R_FINAL, io["final_norm"].rearrange("(k p) -> k p", p=P)),
                (R_PRE2, io["norm_mix_pre_2"].rearrange("l (k p) -> (l k) p", p=P)),
                (R_POST2, io["norm_mix_post_2"].rearrange("l (k p) -> (l k) p", p=P)),
                (R_MPRE2, io["norm_mlp_pre_2"].rearrange("l (k p) -> (l k) p", p=P)),
                (R_MPOST2, io["norm_mlp_post_2"].rearrange("l (k p) -> (l k) p", p=P))]
        for r, src in rows:
            sp.dma_start(par_rows[r:r + src.shape[0], :], src).then_inc(ld_par.sem, 16)
        sp.dma_start(lam_rows[:, :, :].rearrange("p a d -> p (a d)"),
                     io["da_lambda"].rearrange("l a d -> (l a d)").partition_broadcast(P))\
          .then_inc(ld_misc.sem, 16)
        with nc.allow_non_contiguous_dma(reason="512 positions, one word each"):
            sp.dma_start(pos_i[:, :], io["positions"].rearrange("a (t p) -> p (a t)", p=P)).then_inc(ld_misc.sem, 16)

    def setup_pe_part(pe):
        pe.sem_inc(tick.sem, tick.credit)
        pe.wait_ge(consts.sem, 6)
        pe.wait_ge(ld_par.sem, 160)
        pe.transpose(psG[:, 0, 0:R_ALL], par_rows[:, :], ident[0:R_ALL, 0:R_ALL]).then_inc(setup_pe.sem, 1)
        pe.wait_ge(ld_x.sem, 16)
        for k in range(KD):
            if k >= TB:
                pe.wait_ge(x_cp.sem, k - TB + 1)
            for t in range(TB):
                mm = pe.transpose(psH[:, k % TB, t * P:(t + 1) * P], x_tok[:, t, k * P:(k + 1) * P], ident[:, :])
            mm.then_inc(x_tr.sem, 1)

    def setup_dve(dve):
        dve.sem_inc(psum_free[0].sem, 1)
        dve.sem_inc(f2_q.sem, f2_q.credit)
        dve.sem_inc(f_mul.sem, f_mul.credit)
        dve.sem_inc(psum_free[1].sem, 1)
        dve.wait_ge(setup_pe.sem, 1)
        dve.tensor_copy(par[:, :], psG[:, 0, 0:R_ALL])
        dve.drain()
        lg = par[:, R_LB:R_LB + 16].rearrange("p (d l a) -> p d l a", d=2, l=DEPTH)
        dve.tensor_tensor(lbw[:, 0], lg[:, :, 0, :], lg[:, :, 1, :], ALU.max)
        dve.drain()
        for l in range(DEPTH):
            mm = dve.tensor_tensor(lbw[:, 1 + l], lg[:, :, l, :], lbw[:, 0], ALU.subtract)
        mm.then_inc(setup.sem, 1)
        dve.wait_ge(ld_misc.sem, 32)
        lam = lam_rows[:, :, :].rearrange("p (a b) d -> p a b d", b=2)
        dve.tensor_tensor(lam[:, :, 0, :], lam[:, :, 0, :], lam[:, :, 1, :], ALU.mult)
        dve.tensor_copy(pos_f[:, :], pos_i[:, :])
        dve.drain()
        dve.tensor_reduce(small[:, 50:54], lam[:, :, 0, :], AX.X, ALU.add)
        for f in range(8):
            dve.tensor_scalar(ropew[:, 0, :, f], pos_f[:, :], inv_freq[f], None, ALU.mult)
        dve.drain()
        reduce_angle(dve, ropew[:, 1], ropew[:, 0], ropec[:, :, :], True)
        reduce_angle(dve, ropew[:, 2], ropew[:, 0], ropes[:, :, :], False)
        dve.drain().then_inc(setup.sem, 1)
        dve.wait_ge(setup_act.sem, 1)
        dve.tensor_tensor(lbw[:, 3], lbw[:, 1], lbw[:, 2], ALU.add)
        dve.drain()
        dve.reciprocal(lbw[:, 0], lbw[:, 3])
        dve.drain()
        for l in range(DEPTH):
            dve.tensor_tensor(lbw[:, 1 + l], lbw[:, 1 + l], lbw[:, 0], ALU.mult)
        dve.drain()
        dve.tensor_tensor(lbw[:, 3], lbw[:, 1], lbw[:, 2], ALU.add)
        dve.tensor_copy(lbw[:, 4], lbw[:, 1])
        dve.drain()
        for l in range(DEPTH):
            p0 = lay[:, l, :]
            dve.tensor_tensor(p0[:, L_LB:L_LB + 8].rearrange("p (d a) -> p d a", d=2), lbw[:, 4 - l], lbw[:, 1],
                              ALU.subtract)
            dve.tensor_copy(p0[:, L_ATTN:L_ATTN + 8], par[:, R_ATTN + 8 * l:R_ATTN + 8 * l + 8])
            dve.tensor_copy(p0[:, L_FFN:L_FFN + 8], par[:, R_FFN + 8 * l:R_FFN + 8 * l + 8])
            dve.tensor_scalar(p0[:, L_DA:L_DA + 4], par[:, R_DA + 4 * l:R_DA + 4 * l + 4], 1.0 - lam_init(l), None,
                              ALU.mult)
            dve.tensor_copy(p0[:, L_HG:L_HG + 4], par[:, R_HG + 4 * l:R_HG + 4 * l + 4])
            dve.scalar_tensor_tensor(out=p0[:, L_NLAM:L_NLAM + 1], in0=small[:, 55 + 2 * l:56 + 2 * l],
                                     scalar=-lam_init(l), in1=small[:, 54 + 2 * l:55 + 2 * l], op0=ALU.add,
                                     op1=ALU.subtract)
        dve.drain()
        for l in range(DEPTH):
            dve.tensor_scalar(lay[:, l, L_OMLB:L_OMLB + 8], lay[:, l, L_LB:L_LB + 8], -1.0, 1.0, ALU.mult, ALU.add)
        dve.wait_ge(consts.sem, 5)
        dve.tensor_tensor(xor[:, :], iota_s[:, :], iota_t[:, :], ALU.bitwise_xor)
        dve.drain()
        for j in range(7):
            dve.tensor_scalar(masks[:, j, :], xor[:, :], float(1 << j), None, ALU.is_ge)
        dve.drain()
        for k in range(KD):
            dve.wait_ge(x_tr.sem, k + 1)
            dve.tensor_copy(xT[:, k, :], psH[:, k % TB, :]).then_inc(x_cp.sem, 1)
        dve.drain().then_inc(x_done.sem, KD)

    def setup_act_part(act):
        act.wait_ge(setup.sem, 1)
        act.activation(lbw[:, 1:3], lbw[:, 1:3], ACT.Exp)
        act.wait_ge(setup.sem, 2)
        act.activation(small[:, 54:58], small[:, 50:54], ACT.Exp)
        act.activation(ropec[:, :, :], ropew[:, 1], ACT.Sin)
        act.activation(ropes[:, :, :], ropew[:, 2], ACT.Sin)
        act.drain().then_inc(setup_act.sem, 1)

    def layer_sync(sp, l):
        def w(name, rows, cols):
            return io[name][ds(l, 1), rows, cols].rearrange("a (k p) c -> p (a k) c", p=P)

        m = l * U_LAYER
        at_pair = 0
        for c0, pairs in WIN_RUNS:
            with sp.Fori(0, pairs) as i:
                for s in range(2):
                    w_src(m + i + at_pair, s, w("w_in", slice(0, D), ds(i * 512 + (c0 + 256 * s), UC)), sp)
            at_pair += pairs
        for name, u in (("w_a", U_WA), ("w_b", U_WB)):
            for s in range(2):
                w_src(m + u, s, w(name, slice(0, BW), slice(512 * s, 512 * s + 512)), sp)
        with sp.Fori(0, 2) as i:
            for s in range(2):
                w_src(m + i + U_WO, s, w("w_o", slice(0, D), ds(i * 512 + 256 * s, UC)), sp)
        with sp.Fori(0, FT // 2) as i:
            for s, name in enumerate(("w_gate", "w_up")):
                w_src(m + i + U_GU, s, w(name, slice(0, D), ds(i * UC, UC)), sp)
        with sp.Fori(0, 2) as i:
            for u in range(6):
                k0 = KD * (u % 3)
                rows = slice(k0 * P, min(k0 + KD, FT) * P)
                w_src(m + i * 3 + (U_DN + u // 2), u % 2, w("w_down", rows, ds(i * 512 + UC * (u // 3), UC)), sp)

    def layer_pe(pe, l):
        um, jm = l * U_LAYER, l * J_LAYER

        def first_tile(k):
            pe.wait_ge(n_lo.sem, n_lo.at(l, T_ATTN + k + 1))

        norm_pe(pe, l, 0, h_tmp, ALL8)
        for u in range(6):
            pe_feature(pe, um + u // 2, u % 2, jm + u // 2, u % 2, h_hi, h_lo, first_tile if u == 0 else None)
        for lv in range(8):
            level_pe(pe, l, lv)
            u = 6 + lv
            pe_token(pe, um + u // 2, u % 2, jm + u // 2, u % 2)
        mate_pe(pe, l)
        for a in range(HEADS):
            far_pe(pe, l, a)
            hgrn_out_pe(pe, l, a)
        norm_pe(pe, l, 1, sq_b, EACH4)
        qk_pe(pe, l)
        attention_pe(pe, l)
        norm_pe(pe, l, 2, sq_a, EACH4)
        with pe.Fori(0, 5) as i:
            for s in range(2):
                pe_feature(pe, um + i + U_BG, s, jm + i + U_BG, s, h_hi, h_lo)
        pe.wait_ge(n_lo.sem, n_lo.at(l, T_DA + HEADS))
        for u in range(2):
            pe_branch(pe, um + U_WA, u, jm + (J_WA + u), o_hi, o_lo, 0)
        pe.wait_ge(g_lo.sem, g_lo.at(l, HEADS))
        for u in range(2):
            pe_branch(pe, um + U_WB, u, jm + (J_WB + u), o_hi, o_lo, HEADS)

        def merged_tile(k):
            pe.wait_ge(m_lod.sem, m_lod.at(l, k + 1))

        for u in range(4):
            pe_feature(pe, um + (U_WO + u // 2), u % 2, jm + (J_WO + u // 2), u % 2, m_hi, m_lo,
                       merged_tile if u == 0 else None)
        norm_pe(pe, l, 3, h_tmp, ALL8)
        with pe.Fori(0, FT // 2) as i:
            pe.wait_ge(n_lo.sem, n_lo.at(l, NT))
            for s in range(2):
                pe_feature(pe, um + i + U_GU, s, jm + i + J_GU, s, h_hi, h_lo)
        with pe.Fori(0, 2) as i:
            pe.wait_ge(f_lod.sem, f_lod.at(l, FT))
            for c in range(2):
                bank_ready(pe, jm + i + J_DN, c)
                for v in range(3):
                    u = 3 * c + v
                    pe_part(pe, um + i * 3 + (U_DN + u // 2), u % 2, c, hid_hi, hid_lo, KD * v,
                            min(KD, FT - KD * v), v == 0, v == 2)

    def pe_part(pe, m, s, b, x_hi, x_lo, k0, nk, first, last):
        unit_ready(pe, m, s)
        wh = w_hi[:, s, 0:nk * UC].rearrange("p (k c) -> p k c", k=nk)
        wl = w_lo[:, s, 0:nk * UC].rearrange("p (k c) -> p k c", k=nk)
        for j in range(2):
            for k in range(nk):
                c = slice(j * P, (j + 1) * P)
                mm = triple(pe, psG[:, 2 * b + j, :], wh[:, k, c], wl[:, k, c], x_hi[:, k0 + k, :],
                            x_lo[:, k0 + k, :], first and k == 0, last and k == nk - 1)
            mm.then_inc(tick.sem, 1)

    def layer_act(act, l):
        um = l * U_LAYER
        act.wait_ge(x_done.sem, x_done.at(l, 0))
        norm_act(act, l, 0, T_ATTN, xT[:, :, :], h_tmp[:, :, :], ALL8, D, h_tmp, h_hi_t)
        for u in range(6):
            m, s = um + u // 2, u % 2
            split_hi(act, m + 1, s)
            for j in range(2):
                act.wait_ge(tick.sem, T(m, s, j))
                a = 2 * (u % 2) + j
                src = psG[:, 2 * s + j, :]
                if u < 4:
                    d = u // 2
                    act.activation(Tx[:, d, a * S:(a + 1) * S], src, ACT.Sigmoid)
                    mm = act.activation((Kf, Kb)[d][:, a, :], src, ACT.Sigmoid, scale=-1.0)
                else:
                    mm = act.copy(Qf[:, a, :], src)
            mm.then_inc(psum_free[s].sem, 1)
            act.drain().then_inc((b_sig if u < 4 else b_q).sem, 1)
        for u in range(6, 14):
            m, s = um + u // 2, u % 2
            split_hi(act, m + 1, s)
            dst = (b_v, a_q, a_k, a_v)[(u - 6) // 2]
            act.wait_ge(tick.sem, T(m, s, 1))
            act.copy(dst[:, :, s * UC:(s + 1) * UC],
                     psG[:, 2 * s:2 * s + 2, :].rearrange("p b (t c) -> p (b t) c", c=UC))\
               .then_inc(psum_free[s].sem, 1)
            act.drain().then_inc((b_tok if u < 8 else a_tok).sem, 1)
        act.wait_ge(lev_mm.sem, lev_mm.at(l, 9))
        act.copy(s_mate[:, :, :, :].rearrange("p a s t -> p (a s t)"),
                 psH[:, :, :].rearrange("p a t -> p (a t)")).then_inc(mate_cp.sem, 1)
        for a in range(HEADS):
            act.wait_ge(far_mm.sem, far_mm.at(l, a + 1))
            if a >= 2:
                act.wait_ge(av_mm.sem, av_mm.at(l, a - 1))
            act.copy(s_far[:, a % 2, :, :].rearrange("p s t -> p (s t)"),
                     psH[:, 0:2, :].rearrange("p a t -> p (a t)")).then_inc(far_cp.sem, 1)
        act.wait_ge(av_cp.sem, av_cp.at(l, HEADS))
        norm_act(act, l, 1, 0, ob[:, :, :], sq_b[:, :, :], EACH4, P)
        qk_act(act, l)
        attention_act(act, l)
        act.wait_ge(oa_cp.sem, oa_cp.at(l, HEADS))
        norm_act(act, l, 2, T_DA, oa[:, :, :], sq_a[:, :, :], EACH4, P, oa, lambda k: o_hi[:, k, :])
        for u in range(2):
            m, s = um + U_BG, u
            split_hi(act, m + 1, s)
            for j in range(2):
                act.wait_ge(tick.sem, T(m, s, j))
                mm = act.activation(sg[:, 2 * u + j, :], psG[:, 2 * s + j, :], ACT.Sigmoid)
            mm.then_inc(psum_free[s].sem, 1)
            act.drain().then_inc(g_sig.sem, 1)
        for a in range(HEADS):
            act.wait_ge(g_mul.sem, g_mul.at(l, a + 1))
            act.copy(o_hi[:, HEADS + a, :], ob[:, a, :]).then_inc(g_hi.sem, 1)
        for gate, u0 in ((ga, U_GATES), (gb, U_GATES + 2)):
            with act.Fori(0, 2) as i:
                for s in range(2):
                    m = um + i + u0
                    split_hi(act, m + 1, s)
                    for j in range(2):
                        act.wait_ge(tick.sem, T(m, s, j))
                        mm = act.activation(gate[:, ds(i * 4 + (2 * s + j), 1), :].rearrange("p a t -> p (a t)"),
                                            psG[:, 2 * s + j, :], ACT.Sigmoid)
                    mm.then_inc(psum_free[s].sem, 1)
        act.drain().then_inc(g_sig.sem, 1)
        for u in range(4):
            split_hi(act, um + (U_WA + 1 + u // 2), u % 2)
            if u >= 2:
                for k in range(4 * (u - 2), 4 * (u - 2) + 4):
                    act.wait_ge(m_sum.sem, m_sum.at(l, k + 1))
                    act.copy(m_hi[:, k, :], ga[:, k, :]).then_inc(m_hid.sem, 1)
        for u in range(4):
            split_hi(act, um + (U_WO + 1 + u // 2), u % 2)
        act.wait_ge(x_done.sem, x_done.at(l, KD))
        norm_act(act, l, 3, T_FFN, xT[:, :, :], h_tmp[:, :, :], ALL8, D, h_tmp, h_hi_t)
        with act.Fori(0, FT // 2) as i:
            m = um + i + U_GU
            split_hi(act, m + 1, 0)
            for j in range(2):
                act.wait_ge(f_mul.sem, f_mul.at(l, j - 1) + i * 2)
                act.wait_ge(tick.sem, T(m, 0, j))
                act.activation(sgu[:, j, :], psG[:, j, :], ACT.Sigmoid).then_inc(f_sig.sem, 1)
            split_hi(act, m + 1, 1)
            for j in range(2):
                act.wait_ge(f_mul.sem, f_mul.at(l, 0) + i * 2 + (j + 1))
                act.copy(hid_hi[:, ds(i * 2 + j, 1), :].rearrange("p a t -> p (a t)"), ht[:, j, :])\
                   .then_inc(f_hid.sem, 1)
        with act.Fori(0, 2) as i:
            for u in range(6):
                split_hi(act, um + i * 3 + (U_DN + 1 + u // 2), u % 2)

    def layer_dve(dve, l):
        um = l * U_LAYER
        dve.tensor_copy(cur[:, :], lay[:, ds(l, 1), :].rearrange("p a c -> p (a c)"))
        dve.drain()
        norm_dve_split(dve, l, 0, T_ATTN, xT, h_tmp, cur[:, L_ATTN:L_ATTN + KD], ALL8, h_hi_t, h_lo_t)
        for d in range(2):
            dve.wait_ge(b_sig.sem, b_sig.at(l, 2 * d + 2))
            for a in range(HEADS):
                c = 4 * d + a
                lb, omlb = cur[:, L_LB + c:L_LB + c + 1], cur[:, L_OMLB + c:L_OMLB + c + 1]
                t = Tx[:, d, a * S:(a + 1) * S]
                dve.tensor_scalar(t, t, omlb, lb, ALU.mult, ALU.add)
                k = (Kf, Kb)[d][:, a, :]
                mm = dve.tensor_scalar(k, k, omlb, None, ALU.mult)
        mm.then_inc(lev_up.sem, 1)
        dve.wait_ge(lev_up.sem, lev_up.at(l, 1))
        for lv in range(8):
            level_copy(dve, l, lv)
            level_update(dve, 1 << lv)
            dve.wait_ge(lev_up.sem, lev_up.at(l, lv + 2))
        dve.wait_ge(lev_mm.sem, lev_mm.at(l, 9))
        level_update(dve, 2 * P)
        for a in range(HEADS):
            dve.wait_ge(av_mm.sem, av_mm.at(l, a + 1))
            dve.tensor_copy(ob[:, a, :], psH[:, 2 + a % 2, :]).then_inc(av_cp.sem, 1)
        norm_dve_head(dve, l, 1, EACH4)
        for a in range(HEADS):
            dve.scalar_tensor_tensor(out=ob[:, a, :], in0=ob[:, a, :], scalar=cur[:, L_HG + a:L_HG + a + 1],
                                     in1=psH[:, a, :], op0=ALU.mult, op1=ALU.mult)
        rope(dve, l)
        attention_dve(dve, l)
        norm_dve_split(dve, l, 2, T_DA, oa, oa, cur[:, L_DA:L_DA + HEADS], EACH4,
                       lambda k: o_hi[:, k, :], lambda k: o_lo[:, k, :])
        for a in range(HEADS):
            dve.wait_ge(g_sig.sem, g_sig.at(l, a // 2 + 1))
            dve.tensor_tensor(ob[:, a, :], ob[:, a, :], sg[:, a, :], ALU.mult).then_inc(g_mul.sem, 1)
        for a in range(HEADS):
            dve.wait_ge(g_hi.sem, g_hi.at(l, a + 1))
            dve.tensor_tensor(o_lo[:, HEADS + a, :], ob[:, a, :], o_hi[:, HEADS + a, :].bitcast(F32),
                              ALU.subtract).then_inc(g_lo.sem, 1)
        dve.wait_ge(g_sig.sem, g_sig.at(l, 3))
        for u in range(2):
            for j in range(4):
                dve.wait_ge(tick.sem, T(um + U_WA, u, j // 2))
                t = 4 * u + j
                mm = dve.tensor_tensor(ga[:, t, :], ga[:, t, :], psG[:, j, :], ALU.mult)
                if j % 2:
                    mm.then_inc(psum_free[j // 2].sem, 1)
        for u in range(2):
            for j in range(4):
                dve.wait_ge(tick.sem, T(um + U_WB, u, j // 2))
                t = 4 * u + j
                mm = dve.tensor_tensor(gb[:, t, :], gb[:, t, :], psG[:, j, :], ALU.mult)
                if j % 2:
                    mm.then_inc(psum_free[j // 2].sem, 1)
            dve.drain()
            for t in range(4 * u, 4 * u + 4):
                dve.tensor_tensor(ga[:, t, :], ga[:, t, :], gb[:, t, :], ALU.add).then_inc(m_sum.sem, 1)
            for t in range(4 * u, 4 * u + 4):
                dve.wait_ge(m_hid.sem, m_hid.at(l, t + 1))
                dve.tensor_tensor(m_lo[:, t, :], ga[:, t, :], m_hi[:, t, :].bitcast(F32), ALU.subtract)\
                   .then_inc(m_lod.sem, 1)
        with dve.Fori(0, 2) as i:
            for s in range(2):
                for j in range(2):
                    dve.wait_ge(tick.sem, T(um + i + U_WO, s, j))
                    x = xT[:, ds(i * 4 + (2 * s + j), 1), :].rearrange("p a t -> p (a t)")
                    mm = dve.tensor_tensor(x, x, psG[:, 2 * s + j, :], ALU.add)
                mm.then_inc(psum_free[s].sem, 1)
        dve.drain().then_inc(x_done.sem, KD)
        norm_dve_split(dve, l, 3, T_FFN, xT, h_tmp, cur[:, L_FFN:L_FFN + KD], ALL8, h_hi_t, h_lo_t)
        with dve.Fori(0, FT // 2) as i:
            m = um + i + U_GU
            dve.drain()
            for j in range(2):
                dve.wait_ge(f_sig.sem, f_sig.at(l, 0) + i * 2 + (j + 1))
                mm = dve.tensor_tensor(ht[:, j, :], sgu[:, j, :], psG[:, j, :], ALU.mult)
            mm.then_inc(psum_free[0].sem, 1)
            dve.drain()
            for j in range(2):
                dve.wait_ge(tick.sem, T(m, 1, j))
                mm = dve.tensor_tensor(ht[:, j, :], ht[:, j, :], psG[:, 2 + j, :], ALU.mult)\
                        .then_inc(f_mul.sem, 1)
            dve.drain().then_inc(psum_free[1].sem, 1)
            for j in range(2):
                dve.wait_ge(f_hid.sem, f_hid.at(l, 0) + i * 2 + (j + 1))
                dve.tensor_tensor(hid_lo[:, ds(i * 2 + j, 1), :].rearrange("p a t -> p (a t)"), ht[:, j, :],
                                  hid_hi[:, ds(i * 2 + j, 1), :].bitcast(F32).rearrange("p a t -> p (a t)"),
                                  ALU.subtract).then_inc(f_lod.sem, 1)
        with dve.Fori(0, 2) as i:
            for c in range(2):
                for j in range(2):
                    u = 3 * c + 2
                    dve.wait_ge(tick.sem, T(um + i * 3 + (U_DN + u // 2), u % 2, j))
                    x = xT[:, ds(i * 4 + (2 * c + j), 1), :].rearrange("p a t -> p (a t)")
                    mm = dve.tensor_tensor(x, x, psG[:, 2 * c + j, :], ALU.add)
                mm.then_inc(psum_free[c].sem, 1)
        dve.drain().then_inc(x_done.sem, KD)

    UB, JB = DEPTH * U_LAYER, DEPTH * J_LAYER
    (V_Q, V_KV, V_U, V_G, V_GLU, V_WA, V_WS, V_WO, V_FA, V_DA, V_FB, V_DB) = (
        0, 2, 3, 5, 13, 14, 16, 18, 22, 30, 38, 46)
    (K_GLU, K_WA, K_WS, K_WO, K_FA, K_DA, K_FB, K_DB) = 13, 15, 19, 23, 27, 35, 39, 47

    def un(k):
        return step(UB, 0, k)

    def jn(k):
        return step(JB, 0, k)

    def Tn(k, half):
        return T(*un(k), half)

    def split_next(act, k):
        if k + 2 < 2 * U_SECOND:
            split_hi(act, *un(k + 2))

    ld2 = sem("ld2")
    t5_st = sem("t5_st")
    t5_ld = sem("t5_ld")
    toep_ld = sem("toep_ld")
    s2_pe, s2_act, s2_dve, s2_pool = sem("s2_pe"), sem("s2_act"), sem("s2_dve"), sem("s2_pool")
    q_ev, u_ev = sem("q_ev"), sem("u_ev")
    l_mm, l_lg, l_nm, l_ex, l_p = sem("l_mm"), sem("l_lg"), sem("l_nm"), sem("l_ex"), sem("l_p")
    l_tr, l_pt, l_av, l_ov = sem("l_tr"), sem("l_pt"), sem("l_av"), sem("l_ov")
    g2_sig = sem("g2_sig")
    u_tr, u_cp, e_ok = sem("u_tr"), sem("u_cp"), sem("e_ok")
    k_mm, k_cp = sem("k_mm"), sem("k_cp")
    win_tr, win_cp = sem("win_tr"), sem("win_cp")
    g_mm, h_ok = sem("g_mm"), sem("h_ok")
    y_mm, y_cp, z_tr, z_cp = sem("y_mm"), sem("y_cp"), sem("z_tr"), sem("z_cp")
    z_sq, z_in, z_sg, z_ok, z_hid, z_lod = (sem("z_sq"), sem("z_in"), sem("z_sg"), sem("z_ok"), sem("z_hid"),
                                            sem("z_lod"))
    glu_sg, zz_ok, zz_hid, zz_lod = sem("glu_sg"), sem("zz_ok"), sem("zz_hid"), sem("zz_lod")
    o2_hid, o2_lod = sem("o2_hid"), sem("o2_lod")
    m2_sum, m2_hid, m2_lod = sem("m2_sum"), sem("m2_hid"), sem("m2_lod")
    y_ok = sem("y_ok")
    x2_ok = sem("x2_ok")
    f2_r, f2_q, f2_hid, f2_lod = sem("f2_r"), sem("f2_q", credit=2), sem("f2_hid"), sem("f2_lod")
    o_tr, o_cp = sem("o_tr"), sem("o_cp")

    def second_sync(sp):
        w2 = io["w_in_2"][0].rearrange("(k p) c -> p k c", p=P)
        for s in range(2):
            w_src(*un(V_Q + s), w2[:, :, C2_Q + UC * s:C2_Q + UC * (s + 1)], sp)
        sp.wait_ge(x_done.sem, x_done.at(DEPTH, 0))
        with nc.allow_non_contiguous_dma(reason="small parameter layouts"):
            sp.dma_start(s_lam[0:16, :], io["lam_re_2"].rearrange("o (q g) p -> (o q) (g p)", g=2)).then_inc(ld2.sem, 16)
            sp.dma_start(s_lam[16:32, :], io["lam_im_2"].rearrange("o (q g) p -> (o q) (g p)", g=2)).then_inc(ld2.sem, 16)
            sp.dma_start(s_rows[:, :], io["log_dt_2"].rearrange("o (q g) -> (o q) g", g=2)).then_inc(ld2.sem, 16)
            for dst, name in ((b_re, "b_re_2"), (b_im, "b_im_2")):
                for g in range(2):
                    sp.dma_start(dst[NS * g:NS * g + NS, :, :], io[name][0].rearrange("(q g) p c -> g p q c", g=2)[g])\
                      .then_inc(ld2.sem, 16)
            for r, name in enumerate(("c_re_2", "c_im_2")):
                src = io[name].rearrange("o (t g) c p -> (o g c) t p", t=4)
                for dup in range(2):
                    sp.dma_start(c_tok[:, r, :, dup, :], src).then_inc(ld2.sem, 16)
            sp.dma_start(t5_rb[:, :], io["rel_bias_2"].rearrange("b h -> h b")).then_inc(ld2.sem, 16)
            sp.dma_start(sink[:, :], io["sinks_2"].rearrange("o h -> (o h)").partition_broadcast(P)).then_inc(ld2.sem, 16)
            dsk = io["d_skip_2"].rearrange("o (t q c) -> q c (o t)", q=4, c=GC)
            for q in range(4):
                sp.dma_start(d_col[32 * q:32 * q + GC, :], dsk[q]).then_inc(ld2.sem, 16)
        w_src(*un(V_KV), w2[:, :, C2_K:C2_U], sp)
        for s in range(2):
            w_src(*un(V_U + s), w2[:, :, C2_U + UC * s:C2_U + UC * (s + 1)], sp)
        sp.wait_ge(s2_pool.sem, 1)
        sp.dma_start(t5_dram, t5_rows[:, :]).then_inc(t5_st.sem, 16)
        sp.wait_ge(t5_st.sem, 16)
        with nc.allow_non_contiguous_dma(reason="overlapping rows"):
            sp.dma_start(t5_up[:, :, :], bass.AP(t5_dram.tensor, 0, [[1, P], [3 * P, QH], [1, 2 * P]]))\
              .then_inc(t5_ld.sem, 16)
        for k in range(8):
            w_src(*un(V_G + k), w2[:, :, C2_GA + UC * k:C2_GA + UC * (k + 1)], sp)
        w_src(*un(V_GLU), io["w_glu_2"][0].rearrange("(k p) c -> p k c", p=P), sp)
        wa = io["w_attn_branch_2"][0].rearrange("(g j d) c -> g d j c", g=KVH, d=HD)
        for s in range(2):
            m, sl = un(V_WA + s)
            sp.wait_ge(lo_done.sem, m * 2 + sl + 1)
            dst = raw[:, sl, :].rearrange("p (k c) -> p k c", k=4)
            for g in range(KVH):
                sp.dma_start(dst[HD * g:HD * g + HD], wa[g, :, :, 512 * s:512 * s + 512]).then_inc(raw_in[sl].sem, 16)
        sp.wait_ge(k_cp.sem, 1)
        for i in range(CT):
            for q in range(4):
                sp.dma_start(Toep[GC * i:GC * i + GC, :, :].rearrange("p (t q) c -> p q t c", q=4)[:, q],
                             k_pad[32 * q:32 * q + GC, :, P - GC * i:2 * P - GC * i]).then_inc(toep_ld.sem, 16)
        for s in range(2):
            w_src(*un(V_WS + s), io["w_ssm_branch_2"][0].rearrange("(k p) c -> p k c", p=P)
                  [:, :, 512 * s:512 * s + 512], sp)
        wo = io["w_out_2"][0].rearrange("(k p) c -> p k c", p=P)
        for s in range(4):
            w_src(*un(V_WO + s), wo[:, :, UC * s:UC * s + UC], sp)
        for half, vf, vd in ((0, V_FA, V_DA), (1, V_FB, V_DB)):
            with sp.Fori(0, 4) as i:
                for s in range(2):
                    c = ds(i * 512 + (half * D_FF // 2 + UC * s), UC)
                    w_src(i + (UB + vf // 2), s, io["w_ff_in_2"][0, :, c].rearrange("(k p) c -> p k c", p=P), sp)
            with sp.Fori(0, 4) as i:
                for s in range(2):
                    r0 = (half * HT2 + KD * s) * P
                    w_src(i + (UB + vd // 2), s, io["w_ff_out_2"][0, r0:r0 + D, ds(i * UC, UC)]
                          .rearrange("(k p) c -> p k c", p=P), sp)
        out = io["out"].rearrange("a (t p) d -> p (a t) d", p=P)
        for t in range(TB):
            sp.wait_ge(o_cp.sem, 2 * t + 2)
            sp.dma_start(out[:, t, :], x_out[:, t, :]).then_inc(st_out.sem, 16)
        sp.wait_ge(st_out.sem, 16 * TB)

    def norm2_act(act, i, src, width=D, split=None):
        act.activation(h_tmp[:, :, :], src, ACT.Square).then_inc(n_sq.sem, 1)
        act.wait_ge(n_ss.sem, n_ss.at(DEPTH, i + 1))
        act.activation(small[:, 0:TB], psH[:, 0, 0:TB], ACT.Sqrt, scale=1.0 / width, bias=eps_ap)\
           .then_inc(n_sd.sem, 1)
        if split is not None:
            for k in range(KD):
                act.wait_ge(n_tmp.sem, n_tmp.at(DEPTH, split + k + 1))
                act.copy(h_hi[:, k, :], h_tmp[:, k, :]).then_inc(n_hi.sem, 1)

    def second_pool(pool):
        pool.memset(exch[:, :], 0.0).then_inc(consts.sem, 1)
        pool.wait_ge(consts.sem, 7)
        pool.affine_select(out=exch[:, :], in_=exch[:, :], compare_op=ALU.not_equal, fill=1.0, base=-(P - 1),
                           pattern=[[1, P]], channel_multiplier=1).then_inc(consts.sem, 1)

    def tables_dve(dve):
        d, a = dve, s5
        DT, LR, LI, MAG, CO, SI, AR, AI, FR, FI, A, B, C = range(13)

        def tt(o, x, y, op):
            return d.tensor_tensor(o, x, y, op)

        d.wait_ge(ld2.sem, 16 * 17)
        d.memset(t5_rows[:, :], NEG)
        d.drain()
        lo = 0
        while lo < P:
            b = t5_bucket(lo)
            hi = lo
            while hi < P and t5_bucket(hi) == b:
                hi += 1
            dst = t5_rows[:, 2 * P - hi:2 * P - lo]
            d.tensor_copy(dst, t5_rb[:, b:b + 1].broadcast_to([QH, hi - lo]))
            lo = hi
        d.drain().then_inc(s2_pool.sem, 1)
        d.tensor_copy(s_log[:, 1, :], s_rows[:, 1:2].broadcast_to([16, NS]))
        d.tensor_copy(s_log[:, 0, :], s_rows[:, 0:1].broadcast_to([16, NS]))
        d.drain().then_inc(s2_dve.sem, 1)
        d.wait_ge(s2_pe.sem, 1)
        d.tensor_copy(a[:, 0:3, :].rearrange("p a q -> p (a q)"), psH[:, 0, 0:48])
        d.drain().then_inc(s2_dve.sem, 1)
        d.wait_ge(s2_act.sem, 1)
        tt(a[:, MAG], a[:, LR], a[:, DT], ALU.mult)
        tt(a[:, A], a[:, LI], a[:, DT], ALU.mult)
        d.drain()
        reduce_angle(d, a[:, CO], a[:, A], a[:, B], True)
        reduce_angle(d, a[:, SI], a[:, A], a[:, C], False)
        d.drain().then_inc(s2_dve.sem, 1)
        d.wait_ge(s2_act.sem, 2)
        tt(a[:, AR], a[:, MAG], a[:, CO], ALU.mult)
        tt(a[:, AI], a[:, MAG], a[:, SI], ALU.mult)
        tt(a[:, A], a[:, LR], a[:, LR], ALU.mult)
        tt(a[:, B], a[:, LI], a[:, LI], ALU.mult)
        d.drain()
        tt(a[:, A], a[:, A], a[:, B], ALU.add)
        d.tensor_scalar(a[:, C], a[:, AR], 1.0, None, ALU.subtract)
        d.drain()
        d.reciprocal(a[:, A], a[:, A])
        tt(a[:, FR], a[:, C], a[:, LR], ALU.mult)
        tt(a[:, B], a[:, AI], a[:, LI], ALU.mult)
        d.drain()
        tt(a[:, FR], a[:, FR], a[:, B], ALU.add)
        tt(a[:, FI], a[:, AI], a[:, LR], ALU.mult)
        tt(a[:, C], a[:, C], a[:, LI], ALU.mult)
        d.drain()
        tt(a[:, FI], a[:, FI], a[:, C], ALU.subtract)
        tt(a[:, FR], a[:, FR], a[:, A], ALU.mult)
        d.drain()
        tt(a[:, FI], a[:, FI], a[:, A], ALU.mult)
        d.drain()
        wide = [P, PAIRS, GC]
        fr = a[:, FR, :].unsqueeze(2).broadcast_to(wide)
        fi = a[:, FI, :].unsqueeze(2).broadcast_to(wide)
        t = wt_tmp[:, :, 0, :]
        tt(bb[:, 0], fr, b_re[:, :, :], ALU.mult)
        tt(t, fi, b_im[:, :, :], ALU.mult)
        tt(bb[:, 1], fr, b_im[:, :, :], ALU.mult)
        tt(wt_tmp[:, :, 1, :], fi, b_re[:, :, :], ALU.mult)
        d.drain()
        tt(bb[:, 0], bb[:, 0], t, ALU.subtract)
        tt(bb[:, 1], bb[:, 1], wt_tmp[:, :, 1, :], ALU.add)
        d.memset(pw[:, 0, :, 0:1], 1.0)
        d.memset(pw[:, 1, :, 0:1], 0.0)
        d.tensor_copy(pw[:, 0, :, 1], a[:, AR])
        d.tensor_copy(pw[:, 1, :, 1], a[:, AI])
        for n in (1, 2, 4):
            d.drain()
            w = [P, PAIRS, n]
            r0, i0 = pw[:, 0, :, n:n + 1].broadcast_to(w), pw[:, 1, :, n:n + 1].broadcast_to(w)
            r1, i1 = pw[:, 0, :, 1:n + 1], pw[:, 1, :, 1:n + 1]
            x, y = wt_tmp[:, :, 2, 0:n], wt_tmp[:, :, 3, 0:n]
            tt(pw[:, 0, :, n + 1:2 * n + 1], r0, r1, ALU.mult)
            tt(x, i0, i1, ALU.mult)
            tt(pw[:, 1, :, n + 1:2 * n + 1], r0, i1, ALU.mult)
            tt(y, i0, r1, ALU.mult)
            d.drain()
            tt(pw[:, 0, :, n + 1:2 * n + 1], pw[:, 0, :, n + 1:2 * n + 1], x, ALU.subtract)
            tt(pw[:, 1, :, n + 1:2 * n + 1], pw[:, 1, :, n + 1:2 * n + 1], y, ALU.add)
        d.drain()
        for i in range(CT):
            for r in range(2):
                d.tensor_copy(pr[:, r, :, i], pw[:, r, :, CT - 1 - i])
        for r in range(2):
            d.wait_ge(s2_pe.sem, 2 + r)
            for half in range(2):
                rows = slice(NS * half, NS * half + NS)
                src = psH[rows, 1 + r, :].rearrange("p (t g two c) -> p t g two c", t=4, two=2, c=GC)[:, :, :, half, :]
                dst = c_t[rows, r, :, :].rearrange("p (t g) c -> p t g c", t=4)
                d.tensor_copy(dst, src)
        d.drain()
        big = [P, PAIRS, CT + 1, GC]
        cr, ci = (c_t[:, r, :, :].unsqueeze(2).broadcast_to(big) for r in range(2))
        wr, wi = (pw[:, r, :, :].unsqueeze(3).broadcast_to(big) for r in range(2))
        tt(Wt[:, 0], cr, wr, ALU.mult)
        tt(wt_tmp[:, :, :, :], ci, wi, ALU.mult)
        d.drain()
        tt(Wt[:, 0], Wt[:, 0], wt_tmp[:, :, :, :], ALU.subtract)
        d.drain()
        tt(wt_tmp[:, :, :, :], cr, wi, ALU.mult)
        tt(Wt[:, 1], ci, wr, ALU.mult)
        d.drain()
        d.scalar_tensor_tensor(out=Wt[:, 1], in0=wt_tmp[:, :, :, :], scalar=-1.0, in1=Wt[:, 1], op0=ALU.mult,
                               op1=ALU.subtract)
        for q in range(4):
            d.tensor_copy(eye16[32 * q:32 * q + GC, :], ident[32 * q:32 * q + GC, 32 * q:32 * q + GC])
        d.drain().then_inc(s2_dve.sem, 1)

    def e_dve(dve):
        tt = dve.tensor_tensor
        big = [P, PAIRS, CT, GC]
        br, bi = (bb[:, r, :, :].unsqueeze(2).broadcast_to(big) for r in range(2))
        wr, wi = (pr[:, r, :, :].unsqueeze(3).broadcast_to(big) for r in range(2))
        tt(Et[:, 0], br, wr, ALU.mult)
        tt(e_tmp[:, :, :, :], bi, wi, ALU.mult)
        dve.drain()
        tt(Et[:, 0], Et[:, 0], e_tmp[:, :, :, :], ALU.subtract)
        dve.drain()
        tt(e_tmp[:, :, :, :], br, wi, ALU.mult)
        tt(Et[:, 1], bi, wr, ALU.mult)
        dve.drain()
        tt(Et[:, 1], Et[:, 1], e_tmp[:, :, :, :], ALU.add)
        dve.drain().then_inc(e_ok.sem, 1)

    def rot_dve(dve):
        tt, a = dve.tensor_tensor, s5
        MAG, CO, SI, A, B, C = 3, 4, 5, 10, 11, 12
        for _ in range(3):
            tt(a[:, A], a[:, CO], a[:, CO], ALU.mult)
            tt(a[:, B], a[:, SI], a[:, SI], ALU.mult)
            tt(a[:, C], a[:, CO], a[:, SI], ALU.mult)
            tt(a[:, MAG], a[:, MAG], a[:, MAG], ALU.mult)
            dve.drain()
            tt(a[:, CO], a[:, A], a[:, B], ALU.subtract)
            dve.tensor_scalar(a[:, SI], a[:, C], 2.0, None, ALU.mult)
            dve.drain()
        dve.memset(rot[:, 0, :, 0:1], 1.0)
        dve.memset(rot[:, 1, :, 0:1], 0.0)
        dve.tensor_copy(rot[:, 0, :, 1], a[:, CO])
        dve.tensor_copy(rot[:, 1, :, 1], a[:, SI])
        dve.tensor_copy(d0[:, :, :], a[:, MAG, :].unsqueeze(2).broadcast_to([P, PAIRS, CH]))
        dve.drain()
        dve.memset(d0[:, :, 0:1], 0.0)
        for n in (1, 2, 4, 8, 16, 32):
            m = min(n, CH - 1 - n)
            w = [P, PAIRS, m]
            r0, i0 = rot[:, 0, :, n:n + 1].broadcast_to(w), rot[:, 1, :, n:n + 1].broadcast_to(w)
            r1, i1 = rot[:, 0, :, 1:m + 1], rot[:, 1, :, 1:m + 1]
            x, y = s_tmp[:, 0, :, 0:m], s_tmp[:, 1, :, 0:m]
            ro, io_ = rot[:, 0, :, n + 1:n + m + 1], rot[:, 1, :, n + 1:n + m + 1]
            tt(ro, r0, r1, ALU.mult)
            tt(x, i0, i1, ALU.mult)
            tt(io_, r0, i1, ALU.mult)
            tt(y, i0, r1, ALU.mult)
            dve.drain()
            tt(ro, ro, x, ALU.subtract)
            tt(io_, io_, y, ALU.add)
            dve.drain()

    def second_pe(pe):
        pe.wait_ge(consts.sem, 8)
        norm_pe(pe, DEPTH, 0, h_tmp, ALL8)
        norm_pe(pe, DEPTH, 1, h_tmp, ALL8)

        def first_tile(k):
            pe.wait_ge(n_lo.sem, n_lo.at(DEPTH, k + 1))

        for k in range(2):
            pe_feature(pe, *un(V_Q + k), *jn(V_Q + k), h_hi, h_lo, first_tile if k == 0 else None)
        m, s = un(V_KV)
        jm, b = jn(V_KV)
        unit_ready(pe, m, s)
        bank_ready(pe, jm, b)
        wh = w_hi[:, s, :].rearrange("p (k c) -> p k c", k=KD)
        wl = w_lo[:, s, :].rearrange("p (k c) -> p k c", k=KD)
        for k in range(KD):
            mm = triple(pe, psG[:, 2 * b, :], wh[:, k, 0:P], wl[:, k, 0:P], h_hi[:, k, :], h_lo[:, k, :],
                        k == 0, k == KD - 1)
        mm.then_inc(tick.sem, 1)
        for t in range(TB):
            c = slice(t * P, (t + 1) * P)
            for k in range(KD):
                mm = triple(pe, psG[:, 2 * b + 1, c], h_hi[:, k, c], h_lo[:, k, c], wh[:, k, P:2 * P],
                            wl[:, k, P:2 * P], k == 0, k == KD - 1)
        mm.then_inc(tick.sem, 1)
        for v in range(2):
            m, s = un(V_U + v)
            jm, b = jn(V_U + v)
            unit_ready(pe, m, s)
            bank_ready(pe, jm, b)
            wh = w_hi[:, s, :].rearrange("p (k c) -> p k c", k=KD)
            wl = w_lo[:, s, :].rearrange("p (k c) -> p k c", k=KD)
            for t in range(4):
                for k in range(KD):
                    cut = "p (m i) -> p i m"
                    hh = h_hi[:, k, :].rearrange(cut, i=4)[:, t]
                    hl = h_lo[:, k, :].rearrange(cut, i=4)[:, t]
                    out = psG[:, 2 * b + t // 2, (t % 2) * UC:(t % 2 + 1) * UC]
                    mm = triple(pe, out, hh, hl, wh[:, k, :], wl[:, k, :], k == 0, k == KD - 1)
                if t % 2:
                    mm.then_inc(tick.sem, 1)
            if v == 0:
                pe.wait_ge(n_rb.sem, n_rb.at(DEPTH, 2))
                pe.wait_ge(s2_dve.sem, 1)
                pe.transpose(psH[:, 0, 0:16], s_log[:, :, :].rearrange("q g p -> q (g p)"), ident[0:16, 0:16])
                pe.transpose(psH[:, 0, 16:48], s_lam[:, :], ident[0:32, 0:32]).then_inc(s2_pe.sem, 1)
                for r in range(2):
                    for t in range(4):
                        mm = pe.transpose(psH[:, 1 + r, t * P:(t + 1) * P],
                                          c_tok[:, r, t, :, :].rearrange("p a b -> p (a b)"), ident[:, :])
                    mm.then_inc(s2_pe.sem, 1)
        pe.wait_ge(t5_ld.sem, 16)
        pe.wait_ge(s2_dve.sem, 4)
        for n in range(4):
            mm = pe.matmul(psH[:, n, :], exch[:, :], t5_up[:, 2 * n:2 * n + 2, :].rearrange("p a b -> p (a b)"),
                           start=True, stop=True)
        mm.then_inc(s2_pe.sem, 1)
        pe.wait_ge(s2_act.sem, 3)
        pe.wait_ge(u_ev.sem, 2)
        for q in range(PAIRS):
            mm = pe.transpose(psH[:, q // 4, q % 4 * P:(q % 4 + 1) * P],
                              uc[:, 2 * q:2 * q + 2, :, :].rearrange("p g i c -> p (g i c)"), ident[:, :])
        mm.then_inc(u_tr.sem, 1)
        pe.wait_ge(u_cp.sem, 1)
        pe.wait_ge(q_ev.sem, 3)
        for n in range(9):
            if n < 8:
                blk_n, g = n // 2, n % 2
                rows = slice(HD * g, HD * g + HD)
                k0 = max(blk_n - 1, 0) * P
                w = (blk_n + 1) * P - k0
                if n:
                    pe.wait_ge(l_lg.sem, n)
                for j in range(4):
                    mm = pe.matmul(psH[:, j // 2, (j % 2) * 256:(j % 2) * 256 + w], q2[rows, j, blk_n * P:(blk_n + 1) * P],
                                   k2[rows, k0:k0 + w], start=True, stop=True)
                mm.then_inc(l_mm.sem, 1)
            if n:
                o = n - 1
                blk_n, g = o // 2, o % 2
                pe.wait_ge(l_pt.sem, n)
                parts = [blk_n - 1, blk_n] if blk_n else [0]
                for i, kb in enumerate(parts):
                    mm = pe.matmul(psH[HD * g:HD * g + HD, 2, :], v2[:, kb, HD * g:HD * g + HD], pT[:, i, :],
                                   start=i == 0, stop=i == len(parts) - 1)
                mm.then_inc(l_av.sem, 1)
            if n < 8:
                pe_feature(pe, *un(V_G + n), *jn(V_G + n), h_hi, h_lo)
                pe.wait_ge(l_p.sem, n + 1)
                if n:
                    pe.wait_ge(l_ov.sem, n)
                for i in range(2 if n // 2 else 1):
                    for j in range(4):
                        mm = pe.transpose(psH[:, 2 + i, j * P:(j + 1) * P], lg[:, j, i * P:(i + 1) * P], ident[:, :])
                mm.then_inc(l_tr.sem, 1)
        for g in range(GROUPS):
            q, rows = g // 2, slice(NS * (g % 2), NS * (g % 2) + NS)
            for r in range(2):
                mm = pe.matmul(psH[32 * (g % 4):32 * (g % 4) + GC, g // 16, (g // 4 % 4) * P:(g // 4 % 4 + 1) * P],
                               bb[rows, r, q, :], Wt[rows, r, q, 0:CT, :].rearrange("p n c -> p (n c)"),
                               start=r == 0, stop=r == 1)
        mm.then_inc(k_mm.sem, 1)
        pe.wait_ge(e_ok.sem, 1)
        pe.wait_ge(l_ov.sem, 8)
        for n in range(4):
            if n == 1:
                pe.wait_ge(k_cp.sem, 1)
            if n >= 2:
                pe.wait_ge(win_cp.sem, n - 1)
            for i in range(8):
                r, q = divmod(n * 8 + i, PAIRS)
                b = 2 - 2 * (n % 2) + i // 4
                mm = pe.transpose(psH[:, b, (i % 4) * P:(i % 4 + 1) * P], Et[:, r, q, :, :].rearrange("p i c -> p (i c)"),
                                  ident[:, :])
            mm.then_inc(win_tr.sem, 1)
        pe.wait_ge(win_cp.sem, 4)
        for r in range(2):
            for q in range(PAIRS):
                for half in range(2):
                    rows = slice(NS * half, NS * half + NS)
                    mm = pe.matmul(psH[rows, 2 * r + q // 8, (q % 8) * CH:(q % 8 + 1) * CH], Win[:, r, q, rows],
                                   U[:, 2 * q + half, :], start=True, stop=True)
        mm.then_inc(g_mm.sem, 1)
        pe.wait_ge(toep_ld.sem, 16 * 32)
        pe.wait_ge(h_ok.sem, 1)
        for n in range(2):
            if n:
                pe.wait_ge(y_cp.sem, 4)
            for i in range(16):
                g = 16 * n + i
                q, rows = g // 2, slice(NS * (g % 2), NS * (g % 2) + NS)
                out = psH[0:CH, 2 * (i % 2) + i // 8, i // 2 % 4 * P:(i // 2 % 4 + 1) * P]
                pe.matmul(out, U[:, g, :], Toep[:, g, :], start=True, stop=False)
                pe.matmul(out, hre[rows, q, :], Wt[rows, 0, q, 1:CT + 1, :].rearrange("p n c -> p (n c)"),
                          start=False, stop=False)
                mm = pe.matmul(out, him[rows, q, :], Wt[rows, 1, q, 1:CT + 1, :].rearrange("p n c -> p (n c)"),
                               start=False, stop=True)
                if i % 8 >= 6:
                    mm.then_inc(y_mm.sem, 1)
        pe.wait_ge(y_cp.sem, 8)
        for f in range(4):
            for j in range(CT):
                mm = pe.transpose(psH[:, f, j * CH:(j + 1) * CH], yt[:, j, f * P:(f + 1) * P], ident[0:CH, 0:CH])
            mm.then_inc(z_tr.sem, 1)
        pe.wait_ge(z_lod.sem, 4)
        pe_branch2(pe, V_GLU, K_GLU, z_hi, z_lo)
        pe.wait_ge(o2_lod.sem, 4)
        for k in range(2):
            pe_branch2(pe, V_WA + k, K_WA + 2 * k, o2_hi, o2_lo)
        pe.wait_ge(zz_lod.sem, 4)
        for k in range(2):
            pe_branch2(pe, V_WS + k, K_WS + 2 * k, zz_hi, zz_lo)

        def merged_tile(k):
            pe.wait_ge(m2_lod.sem, k + 1)

        for k in range(4):
            pe_feature(pe, *un(V_WO + k), *jn(K_WO + k), m2_hi, m2_lo, merged_tile if k == 0 else None)
        norm_pe(pe, DEPTH, 2, h_tmp, ALL8)
        norm_pe(pe, DEPTH, 3, h_tmp, ALL8)
        pe.wait_ge(n_lo.sem, n_lo.at(DEPTH, 2 * KD))
        for half, vf, kf, vd, kd in ((0, V_FA, K_FA, V_DA, K_DA), (1, V_FB, K_FB, V_DB, K_DB)):
            with pe.Fori(0, 4) as i:
                for s in range(2):
                    jm, b = step(JB + kf // 2, kf % 2, s)
                    pe_feature(pe, i + (UB + vf // 2), s, i + jm, b, h_hi, h_lo)
            pe.wait_ge(f2_lod.sem, HT2 * (half + 1))
            for c in range(4):
                jm, b = jn(kd + c)
                bank_ready(pe, jm, b)
                for v in range(2):
                    m, s = un(vd + 2 * c + v)
                    pe_part(pe, m, s, b, hid2_hi, hid2_lo, KD * v, KD, v == 0, v == 1)
        norm_pe(pe, DEPTH, 4, h_tmp, ALL8)
        for t in range(TB):
            for h in range(2):
                n = 2 * t + h
                if n == 0:
                    pe.wait_ge(x2_ok.sem, 4)
                if n >= 4:
                    pe.wait_ge(o_cp.sem, n - 3)
                for k in range(4):
                    mm = pe.transpose(psH[:, n % 4, k * P:(k + 1) * P], xT[:, 4 * h + k, t * P:(t + 1) * P],
                                      ident[:, :])
                mm.then_inc(o_tr.sem, 1)

    def pe_branch2(pe, k, j, x_hi, x_lo):
        m, s = un(k)
        unit_ready(pe, m, s)
        wh = w_hi[:, s, :].rearrange("p (k c) -> p k c", k=4)
        wl = w_lo[:, s, :].rearrange("p (k c) -> p k c", k=4)
        nt = 4
        for t in range(nt):
            jm, b = jn(j + t // 2)
            if t % 2 == 0:
                bank_ready(pe, jm, b)
            for kk in range(4):
                c = slice(t * P, (t + 1) * P)
                mm = triple(pe, psG[:, 2 * b + t % 2, :], wh[:, kk, c], wl[:, kk, c], x_hi[:, kk, :], x_lo[:, kk, :],
                            kk == 0, kk == 3)
            if t % 2:
                mm.then_inc(tick.sem, 1)

    def bank2(j, t):
        return 2 * jn(j + t // 2)[1] + t % 2

    def second_act(act):
        act.wait_ge(x_done.sem, x_done.at(DEPTH, 0))
        norm2_act(act, 0, xT[:, :, :])
        act.wait_ge(x2_ok.sem, 1)
        norm2_act(act, 1, xT[:, :, :], split=0)
        for k in range(2):
            split_next(act, V_Q + k)
            b = jn(k)[1]
            for j in range(2):
                act.wait_ge(tick.sem, Tn(k, j))
                for i in range(2):
                    mm = act.copy(q2[HD * k:HD * k + HD, 2 * j + i, :], psG[HD * i:HD * i + HD, 2 * b + j, :])
            mm.then_inc(psum_free[b].sem, 1)
            act.drain().then_inc(q_ev.sem, 1)
        split_next(act, V_KV)
        b = jn(V_KV)[1]
        act.wait_ge(tick.sem, Tn(V_KV, 0))
        act.copy(k2[:, :], psG[:, 2 * b, :])
        act.wait_ge(tick.sem, Tn(V_KV, 1))
        act.copy(v2[:, :, :].rearrange("p t c -> p (t c)"), psG[:, 2 * b + 1, :]).then_inc(psum_free[b].sem, 1)
        act.drain().then_inc(q_ev.sem, 1)
        split_next(act, V_U)
        act.wait_ge(s2_dve.sem, 2)
        act.activation(s5[:, 0, :], s5[:, 0, :], ACT.Exp).then_inc(s2_act.sem, 1)
        act.wait_ge(s2_dve.sem, 3)
        act.activation(s5[:, 3, :], s5[:, 3, :], ACT.Exp)
        act.activation(s5[:, 4, :], s5[:, 4, :], ACT.Sin)
        act.activation(s5[:, 5, :], s5[:, 5, :], ACT.Sin)
        act.drain().then_inc(s2_act.sem, 1)
        act.wait_ge(s2_dve.sem, 4)
        act.wait_ge(s2_pe.sem, 4)
        for n in range(4):
            mm = act.copy(bias[:, 2 * n:2 * n + 2, :].rearrange("p a b -> p (a b)"), psH[:, n, :])
        mm.then_inc(s2_act.sem, 1)
        for v in range(2):
            if v:
                split_next(act, V_U + 1)
            b = jn(V_U + v)[1]
            act.wait_ge(tick.sem, Tn(V_U + v, 1))
            act.copy(uc[:, 16 * v:16 * v + 16, :, :].rearrange("p g t c -> p t g c"),
                     psG[:, 2 * b:2 * b + 2, :].rearrange("p b (t g c) -> p (b t) g c", t=2, c=GC))\
               .then_inc(psum_free[b].sem, 1)
            act.drain().then_inc(u_ev.sem, 1)
        act.wait_ge(u_tr.sem, 1)
        for h in range(2):
            for g in range(2):
                mm = act.copy(U[CH * h:CH * h + CH, :, :].rearrange("p (q g) c -> p g q c", g=2)[:, g],
                              psH[CH * g:CH * g + CH, :, :].rearrange("p a (q c h) -> p h (a q) c", h=2, c=CH)[:, h])
        mm.then_inc(u_cp.sem, 1)
        for n in range(8):
            act.wait_ge(l_nm.sem, n + 1)
            act.activation(lg_w(n), lg_w(n), ACT.Exp)
            act.activation(st2[:, 2, :], st2[:, 1, :], ACT.Exp).then_inc(l_ex.sem, 1)
            split_next(act, V_G + n)
            b = jn(V_G + n)[1]
            for j in range(2):
                act.wait_ge(tick.sem, Tn(V_G + n, j))
                t = 2 * n + j
                mm = act.activation((g2a, g2b)[t // KD][:, t % KD, :], psG[:, 2 * b + j, :], ACT.Sigmoid)
            mm.then_inc(psum_free[b].sem, 1)
            act.wait_ge(l_tr.sem, n + 1)
            w = 2 if n // 2 else 1
            act.copy(pT[:, 0:w, :], psH[:, 2:2 + w, :]).then_inc(l_pt.sem, 1)
            act.wait_ge(l_av.sem, n + 1)
            g = n % 2
            rows = slice(HD * g, HD * g + HD)
            act.copy(q2[rows, :, (n // 2) * P:(n // 2 + 1) * P],
                     psH[rows, 2, :].rearrange("p (j q) -> p j q", j=4)).then_inc(l_ov.sem, 1)
        act.drain().then_inc(g2_sig.sem, 1)
        for n in range(4):
            act.wait_ge(win_tr.sem, n + 1)
            b = 2 - 2 * (n % 2)
            r, q = divmod(n * 8, PAIRS)
            act.copy(Win[:, r, q:q + 8, :].rearrange("p q c -> p (q c)"),
                     psH[:, b:b + 2, :].rearrange("p a b -> p (a b)")).then_inc(win_cp.sem, 1)
        for n in range(8):
            act.wait_ge(y_mm.sem, n + 1)
            act.copy(yt[:, :, n // 2 * P:(n // 2 + 1) * P].rearrange("c j (g two o) -> c two g j o", g=4, two=2)[:, n % 2],
                     psH[0:CH, 2 * (n % 2) + n // 2 % 2, :].rearrange("c (g j o) -> c g j o", g=4, j=CT))\
               .then_inc(y_cp.sem, 1)
        for f in range(4):
            act.wait_ge(z_tr.sem, f + 1)
            src = psH[:, f, :].rearrange("p (j c) -> p c j", j=CT)
            act.copy(z2[:, f, :].rearrange("p (c j) -> p c j", j=CT), src)
        act.drain()
        for f in range(4):
            act.activation(z_w[:, 0, f, :], z2[:, f, :], ACT.Square).then_inc(z_sq.sem, 1)
        for f in range(4):
            act.wait_ge(z_in.sem, f + 1)
            act.activation(z_w[:, 1, f, :], z_w[:, 0, f, :], ACT.Sigmoid, scale=GELU).then_inc(z_sg.sem, 1)
        for f in range(4):
            act.wait_ge(z_ok.sem, f + 1)
            act.copy(z_hi[:, f, :], z2[:, f, :]).then_inc(z_hid.sem, 1)
        for f in range(4):
            act.copy(o2_hi[:, f, :], q2[:, f, :]).then_inc(o2_hid.sem, 1)
        split_next(act, V_GLU)
        for t in range(4):
            act.wait_ge(tick.sem, Tn(V_GLU, t // 2))
            mm = act.activation(z_w[:, 0, t, :], psG[:, bank2(K_GLU, t), :], ACT.Sigmoid)
            if t % 2:
                mm.then_inc(psum_free[jn(K_GLU + t // 2)[1]].sem, 1)
                act.drain().then_inc(glu_sg.sem, 1)
        for f in range(4):
            act.wait_ge(zz_ok.sem, f + 1)
            act.copy(zz_hi[:, f, :], z2[:, f, :]).then_inc(zz_hid.sem, 1)
        for k in range(2):
            split_next(act, V_WA + k)
        for k in range(2):
            split_next(act, V_WS + k)
            for t in range(4 * k, 4 * k + 4):
                act.wait_ge(m2_sum.sem, t + 1)
                act.copy(m2_hi[:, t, :], g2a[:, t, :]).then_inc(m2_hid.sem, 1)
        for k in range(4):
            split_next(act, V_WO + k)
        act.wait_ge(y_ok.sem, 1)
        norm2_act(act, 2, y2[:, :, :])
        act.wait_ge(x2_ok.sem, 2)
        norm2_act(act, 3, xT[:, :, :], split=KD)
        for half, vf, kf in ((0, V_FA, K_FA), (1, V_FB, K_FB)):
            with act.Fori(0, 4) as i:
                for s in range(2):
                    m = i + (UB + vf // 2)
                    split_hi(act, m + 1, s)
                    b = step(0, kf % 2, s)[1]
                    for j in range(2):
                        t = 2 * s + j
                        act.wait_ge(f2_q.sem, i * 4 + (16 * half + t - 1 + f2_q.credit))
                        act.wait_ge(tick.sem, T(m, s, j))
                        mm = act.activation(r2[:, j, :], psG[:, 2 * b + j, :], ACT.Relu).then_inc(f2_r.sem, 1)
                    act.drain().then_inc(psum_free[b].sem, 1)
                    for j in range(2):
                        t = 2 * s + j
                        act.wait_ge(f2_q.sem, i * 4 + (16 * half + t + 1 + f2_q.credit))
                        act.copy(hid2_hi[:, ds(i * 4 + t, 1), :].rearrange("p a t -> p (a t)"), hq2[:, j, :])\
                           .then_inc(f2_hid.sem, 1)
            for k in range(8):
                split_next(act, (V_DA, V_DB)[half] + k)
        act.wait_ge(y_ok.sem, 2)
        norm2_act(act, 4, y2[:, :, :])

    def lg_w(n):
        return lg[:, :, 0:(2 * P if n // 2 else P)]

    def norm2_dve(dve, i, src, gain, out):
        norm_dve_head(dve, DEPTH, i, ALL8)
        for k in range(KD):
            mm = dve.scalar_tensor_tensor(out=out[:, k, :], in0=src[:, k, :], scalar=gain[:, k:k + 1],
                                          in1=psH[:, 0, :], op0=ALU.mult, op1=ALU.mult)
        return mm

    def second_dve(dve):
        norm2_dve(dve, 0, xT, par[:, R_FINAL:R_FINAL + KD], xT)
        dve.drain().then_inc(x2_ok.sem, 1)
        norm_dve_split(dve, DEPTH, 1, 0, xT, h_tmp, par[:, R_PRE2:R_PRE2 + KD], ALL8, h_hi_t, h_lo_t)
        tables_dve(dve)
        dve.wait_ge(u_tr.sem, 1)
        e_dve(dve)
        dve.wait_ge(s2_act.sem, 3)
        for n in range(8):
            blk_n, g = n // 2, n % 2
            w = 2 * P if blk_n else P
            bs = bias[:, 4 * g:4 * g + 4, 2 * P - w:2 * P]
            dve.wait_ge(l_mm.sem, n + 1)
            if n:
                dve.wait_ge(l_tr.sem, n)
            ps = psH[:, 0:2, :].rearrange("p b (j k) -> p (b j) k", j=2)[:, :, 0:w]
            dve.scalar_tensor_tensor(out=lg_w(n), in0=ps, scalar=HD ** -0.5, in1=bs, op0=ALU.mult, op1=ALU.add)\
               .then_inc(l_lg.sem, 1)
            dve.drain()
            dve.tensor_reduce(st2[:, 0, :], lg_w(n), AX.X, ALU.max)
            dve.drain()
            dve.tensor_tensor(st2[:, 0, :], st2[:, 0, :], sink[:, 4 * g:4 * g + 4], ALU.max)
            dve.drain()
            dve.tensor_tensor(st2[:, 1, :], sink[:, 4 * g:4 * g + 4], st2[:, 0, :], ALU.subtract)
            dve.tensor_tensor(lg_w(n), lg_w(n), st2[:, 0, :].unsqueeze(2).broadcast_to([P, 4, w]), ALU.subtract)\
               .then_inc(l_nm.sem, 1)
            dve.wait_ge(l_ex.sem, n + 1)
            dve.tensor_reduce(st2[:, 3, :], lg_w(n), AX.X, ALU.add)
            dve.drain()
            dve.tensor_tensor(st2[:, 3, :], st2[:, 3, :], st2[:, 2, :], ALU.add)
            dve.drain()
            dve.reciprocal(st2[:, 4, :], st2[:, 3, :])
            dve.drain()
            dve.tensor_tensor(lg_w(n), lg_w(n), st2[:, 4, :].unsqueeze(2).broadcast_to([P, 4, w]), ALU.mult)\
               .then_inc(l_p.sem, 1)
        dve.wait_ge(l_ov.sem, 8)
        dve.memset(k_pad[:, :, 0:P], 0.0)
        dve.wait_ge(k_mm.sem, 1)
        for q in range(4):
            rows = slice(32 * q, 32 * q + GC)
            dve.tensor_copy(k_pad[rows, :, P:2 * P], psH[rows, 0:2, :].rearrange("p a (t c) -> p (a t) c", c=P))
            dve.tensor_tensor(s_eye[rows, :, :], eye16[rows, :].unsqueeze(1).broadcast_to([GC, CT, GC]),
                              d_col[rows, :].unsqueeze(2).broadcast_to([GC, CT, GC]), ALU.mult)
        dve.drain()
        for q in range(4):
            rows = slice(32 * q, 32 * q + GC)
            dve.tensor_tensor(k_pad[rows, :, P:P + GC], k_pad[rows, :, P:P + GC], s_eye[rows, :, :], ALU.add)
        dve.drain().then_inc(k_cp.sem, 1)
        dve.wait_ge(win_tr.sem, 4)
        rot_dve(dve)
        dve.wait_ge(g_mm.sem, 1)
        dve.wait_ge(toep_ld.sem, 16 * 32)
        tt = dve.tensor_tensor
        gr = psH[:, 0:2, :].rearrange("p a (q c) -> p (a q) c", c=CH)[:, :, 0:CH - 1]
        gi = psH[:, 2:4, :].rearrange("p a (q c) -> p (a q) c", c=CH)[:, :, 0:CH - 1]
        rc, rs = rot[:, 0, :, 1:CH], rot[:, 1, :, 1:CH]
        dve.memset(hre[:, :, 0:1], 0.0)
        dve.memset(him[:, :, 0:1], 0.0)
        tt(hre[:, :, 1:CH], rc, gr, ALU.mult)
        tt(him[:, :, 1:CH], rc, gi, ALU.mult)
        tt(s_tmp[:, 0, :, 1:CH], rs, gi, ALU.mult)
        tt(s_tmp[:, 1, :, 1:CH], rs, gr, ALU.mult)
        dve.drain()
        tt(hre[:, :, 1:CH], hre[:, :, 1:CH], s_tmp[:, 0, :, 1:CH], ALU.add)
        tt(him[:, :, 1:CH], him[:, :, 1:CH], s_tmp[:, 1, :, 1:CH], ALU.subtract)
        dve.drain()
        flat = "p q c -> p (q c)"
        for r, x in enumerate((hre, him)):
            dve.tensor_tensor_scan(s_tmp[:, r].rearrange(flat), d0[:, :, :].rearrange(flat),
                                   x[:, :, :].rearrange(flat), 0.0, ALU.mult, ALU.add)
        dve.drain()
        tt(hre[:, :, :], rot[:, 0], s_tmp[:, 0], ALU.mult)
        tt(s_tmp[:, 2], rot[:, 1], s_tmp[:, 1], ALU.mult)
        tt(him[:, :, :], rot[:, 1], s_tmp[:, 0], ALU.mult)
        dve.drain()
        tt(hre[:, :, :], hre[:, :, :], s_tmp[:, 2], ALU.subtract)
        tt(s_tmp[:, 1], rot[:, 0], s_tmp[:, 1], ALU.mult)
        dve.drain()
        tt(him[:, :, :], him[:, :, :], s_tmp[:, 1], ALU.add).then_inc(h_ok.sem, 1)
        for f in range(4):
            dve.wait_ge(z_sq.sem, f + 1)
            dve.tensor_scalar(z_w[:, 0, f, :], z_w[:, 0, f, :], 0.044715, 1.0, ALU.mult, ALU.add)
            dve.drain()
            tt(z_w[:, 0, f, :], z_w[:, 0, f, :], z2[:, f, :], ALU.mult).then_inc(z_in.sem, 1)
        for f in range(4):
            dve.wait_ge(z_sg.sem, f + 1)
            tt(z2[:, f, :], z2[:, f, :], z_w[:, 1, f, :], ALU.mult).then_inc(z_ok.sem, 1)
        for f in range(4):
            dve.wait_ge(z_hid.sem, f + 1)
            tt(z_lo[:, f, :], z2[:, f, :], z_hi[:, f, :].bitcast(F32), ALU.subtract).then_inc(z_lod.sem, 1)
        for f in range(4):
            dve.wait_ge(o2_hid.sem, f + 1)
            tt(o2_lo[:, f, :], q2[:, f, :], o2_hi[:, f, :].bitcast(F32), ALU.subtract).then_inc(o2_lod.sem, 1)
        for f in range(4):
            dve.wait_ge(glu_sg.sem, f // 2 + 1)
            tt(z2[:, f, :], z2[:, f, :], z_w[:, 0, f, :], ALU.mult).then_inc(zz_ok.sem, 1)
        for f in range(4):
            dve.wait_ge(zz_hid.sem, f + 1)
            tt(zz_lo[:, f, :], z2[:, f, :], zz_hi[:, f, :].bitcast(F32), ALU.subtract).then_inc(zz_lod.sem, 1)
        dve.wait_ge(g2_sig.sem, 1)
        for k0, v0, gate in ((K_WA, V_WA, g2a), (K_WS, V_WS, g2b)):
            for u in range(2):
                for j in range(4):
                    t = 4 * u + j
                    dve.wait_ge(tick.sem, Tn(v0 + u, j // 2))
                    mm = tt(gate[:, t, :], gate[:, t, :], psG[:, bank2(k0 + 2 * u, j), :], ALU.mult)
                    if j % 2:
                        mm.then_inc(psum_free[jn(k0 + 2 * u + j // 2)[1]].sem, 1)
                if gate is g2a:
                    continue
                dve.drain()
                for t in range(4 * u, 4 * u + 4):
                    tt(g2a[:, t, :], g2a[:, t, :], g2b[:, t, :], ALU.add).then_inc(m2_sum.sem, 1)
                for t in range(4 * u, 4 * u + 4):
                    dve.wait_ge(m2_hid.sem, t + 1)
                    tt(m2_lo[:, t, :], g2a[:, t, :], m2_hi[:, t, :].bitcast(F32), ALU.subtract).then_inc(m2_lod.sem, 1)
        for k in range(4):
            b = jn(K_WO + k)[1]
            for j in range(2):
                dve.wait_ge(tick.sem, Tn(V_WO + k, j))
                mm = dve.tensor_copy(y2[:, 2 * k + j, :], psG[:, 2 * b + j, :])
            mm.then_inc(psum_free[b].sem, 1)
        dve.drain().then_inc(y_ok.sem, 1)
        post_dve(dve, 2, R_POST2)
        dve.drain().then_inc(x2_ok.sem, 1)
        norm_dve_split(dve, DEPTH, 3, KD, xT, h_tmp, par[:, R_MPRE2:R_MPRE2 + KD], ALL8, h_hi_t, h_lo_t)
        for half, vf, kf, vd, kd in ((0, V_FA, K_FA, V_DA, K_DA), (1, V_FB, K_FB, V_DB, K_DB)):
            with dve.Fori(0, 4) as i:
                for s in range(2):
                    dve.drain()
                    for j in range(2):
                        t = 2 * s + j
                        dve.wait_ge(f2_r.sem, i * 4 + (16 * half + t + 1))
                        tt(hq2[:, j, :], r2[:, j, :], r2[:, j, :], ALU.mult).then_inc(f2_q.sem, 1)
                    for j in range(2):
                        t = 2 * s + j
                        dve.wait_ge(f2_hid.sem, i * 4 + (16 * half + t + 1))
                        tt(hid2_lo[:, ds(i * 4 + t, 1), :].rearrange("p a t -> p (a t)"), hq2[:, j, :],
                           hid2_hi[:, ds(i * 4 + t, 1), :].bitcast(F32).rearrange("p a t -> p (a t)"),
                           ALU.subtract).then_inc(f2_lod.sem, 1)
            for c in range(4):
                b = jn(kd + c)[1]
                for j in range(2):
                    dve.wait_ge(tick.sem, Tn(vd + 2 * c + 1, j))
                    y = y2[:, 2 * c + j, :]
                    if half == 0:
                        mm = dve.tensor_copy(y, psG[:, 2 * b + j, :])
                    else:
                        mm = tt(y, y, psG[:, 2 * b + j, :], ALU.add)
                mm.then_inc(psum_free[b].sem, 1)
        dve.drain().then_inc(y_ok.sem, 1)
        post_dve(dve, 4, R_MPOST2)
        dve.drain().then_inc(x2_ok.sem, 2)
        for n in range(8):
            dve.wait_ge(o_tr.sem, n + 1)
            dve.tensor_copy(x_out[:, n // 2, (n % 2) * S:(n % 2 + 1) * S], psH[:, n % 4, :]).then_inc(o_cp.sem, 1)

    def post_dve(dve, i, r):
        norm2_dve(dve, i, y2, par[:, r:r + KD], y2)
        dve.drain()
        for k in range(KD):
            dve.tensor_tensor(xT[:, k, :], xT[:, k, :], y2[:, k, :], ALU.add)

    @block.sync
    def _(sp):
        setup_sync(sp)
        with sp.Fori(0, DEPTH) as l:
            layer_sync(sp, l)
        second_sync(sp)

    @block.gpsimd
    def _(pool):
        setup_pool(pool)
        second_pool(pool)
        with pool.Fori(0, ALL_PAIRS) as m:
            for s in range(2):
                pool.wait_ge(hi_done.sem, m * 2 + (s + 1))
                pool.tensor_tensor(w_lo[:, s, :], raw[:, s, :], w_hi[:, s, :].bitcast(F32), ALU.subtract)\
                    .then_inc(lo_done.sem, 1)

    @block.scalar
    def _(act):
        setup_act_part(act)
        split_hi(act, 0, 0)
        split_hi(act, 0, 1)
        with act.Fori(0, DEPTH) as l:
            layer_act(act, l)
        second_act(act)

    @block.vector
    def _(dve):
        setup_dve(dve)
        with dve.Fori(0, DEPTH) as l:
            layer_dve(dve, l)
        second_dve(dve)

    @block.tensor
    def _(pe):
        setup_pe_part(pe)
        with pe.Fori(0, DEPTH) as l:
            layer_pe(pe, l)
        second_pe(pe)


_INS = ["x", "positions", "w_in", "da_lambda", "da_norm", "hg_lb_logits", "hg_norm", "w_a", "w_b", "w_o", "attn_norm",
        "ffn_norm", "w_gate", "w_up", "w_down", "final_norm", "norm_mix_pre_2", "norm_mix_post_2", "norm_mlp_pre_2",
        "norm_mlp_post_2", "w_in_2", "rel_bias_2", "sinks_2", "lam_re_2", "lam_im_2", "log_dt_2", "b_re_2", "b_im_2",
        "c_re_2", "c_im_2", "d_skip_2", "w_glu_2", "w_attn_branch_2", "w_ssm_branch_2", "w_out_2", "w_ff_in_2",
        "w_ff_out_2"]


def kernel(**inputs):
    import numpy as _np
    import concourse.bacc as _bacc
    from concourse import mybir as _mybir
    from concourse.bass_utils import run_bass_kernel_spmd as _run

    nc = _bacc.Bacc("TRN2", target_bir_lowering=False, num_devices=1)
    arrays, io = {}, {}
    for name in _INS:
        a = _np.ascontiguousarray(inputs[name])
        arrays[f"in_{name}_dram"] = a
        io[name] = nc.dram_tensor(f"in_{name}_dram", a.shape, _mybir.dt.from_np(a.dtype), kind="ExternalInput").ap()
    io["out"] = nc.dram_tensor("out_0_dram", (1, S, D), F32, kind="ExternalOutput").ap()
    build_kernel(nc, io)
    r = _run(nc, [arrays], core_ids=[0])
    return r.results[0]["out_0_dram"]
```

```python
import math
from contextlib import ExitStack

import numpy as np

import concourse.bass as bass
from concourse import mybir

F32 = mybir.dt.float32
F32R = mybir.dt.float32r
I32 = mybir.dt.int32
U8 = mybir.dt.uint8
ALU = mybir.AluOpType
ACT = mybir.ActivationFunctionType
AX = mybir.AxisListType
ds = bass.ds

P = 128
D = 1024
S = 512
KD = D // P
TB = S // P
DEPTH = 2
HEADS = 4
BW = HEADS * P
FT = -(-8 * D // (3 * 256)) * 2
EPS = 1e-6
UC = 256
UNIT = KD * UC

C_AQ, C_AK, C_AV, C_BQ, C_BFF, C_BFB, C_BI, C_BG, C_GA, C_GB = (
    0, 512, 1024, 1536, 2048, 2560, 3072, 3584, 4096, 5120)
WIN_RUNS = [(C_BFF, 2), (C_BQ, 1), (C_BI, 1), (C_AQ, 3), (C_GA, 4), (C_BG, 1)]

U_BFF, U_BQ, U_BI, U_ATT, U_GATES, U_BG, U_WA, U_WB, U_WO, U_GU, U_DN, U_LAYER = (
    0, 2, 3, 4, 7, 11, 12, 13, 14, 16, 27, 33)
J_WA, J_WB, J_WO, J_GU, J_DN, J_LAYER = 12, 14, 16, 18, 29, 31

QH, KVH, HD = 8, 2, 64
D_FF = 4 * D
GROUPS, GC, NS = 32, 16, 64
PAIRS = GROUPS // 2
CT = 8
CH = S // CT
NEG = -1e30
U_SECOND = 27
C2_Q, C2_K, C2_V, C2_U, C2_GA, C2_GB = 0, 512, 640, 768, 1280, 2304

TWO_PI = 2 * math.pi
PI_HI = 6.28125
PI_MID = float(np.float32(np.floor((TWO_PI - PI_HI) * 2**21) / 2**21))
PI_LO = float(np.float32(TWO_PI - PI_HI - PI_MID))
GELU = 2 * math.sqrt(2 / math.pi)
ROUND = 1.5 * 2**23
PI_MAX = 3.1415925

R_ATTN, R_FFN, R_DA, R_HG, R_LB, R_FINAL, R_PRE2, R_POST2, R_MPRE2, R_MPOST2, R_ALL = (
    0, 16, 32, 40, 48, 64, 72, 80, 88, 96, 104)
L_ATTN, L_FFN, L_DA, L_HG, L_LB, L_OMLB, L_NLAM, L_ALL = 0, 8, 16, 20, 24, 32, 40, 41

KB = 1024


class Signal:

    def __init__(self, sem, per_layer=0, credit=0):
        self.sem, self.per, self.credit = sem, per_layer, credit

    def at(self, layer, k):
        return layer * self.per + (k + self.credit)


def step(m, s, k):
    return m + (s + k) // 2, (s + k) % 2


def lam_init(layer):
    return 0.8 - 0.6 * math.exp(-0.3 * layer)


def t5_bucket(d, buckets=32, most=128):
    exact = buckets // 2
    if d < exact:
        return d
    f = np.float32(np.log(np.float32(d) / np.float32(exact))) / np.float32(math.log(most / exact))
    return min(exact + int(np.float32(f) * np.float32(buckets - exact)), buckets - 1)


def build_kernel(nc, io):
    with ExitStack() as ctx:
        build_in(nc, io, ctx)


def build_in(nc, io, ctx):
    def sb(name, shape, dt=F32):
        return ctx.enter_context(nc.sbuf_tensor(name, shape, dt))

    def sem(name, per_layer=0, credit=0):
        return Signal(ctx.enter_context(nc.semaphore(name)), per_layer, credit)

    xT = sb("xT", [P, KD, S])
    h_hi_at = nc.sbuf_base
    h_hi = sb("h_hi", [P, KD, S], F32R)
    h_lo_at = nc.sbuf_base
    h_lo = sb("h_lo", [P, KD, S], F32R)
    raw = sb("raw", [P, 2, UNIT])
    w_hi = sb("w_hi", [P, 2, UNIT], F32R)
    w_lo = sb("w_lo", [P, 2, UNIT], F32R)
    ident = sb("ident", [P, P])
    ones = sb("ones", [P, 2])
    one_hot = sb("one_hot", [P, 4 * HEADS])
    par = sb("par", [P, R_ALL])
    lay = sb("lay", [P, DEPTH, L_ALL])
    cur = sb("cur", [P, L_ALL])
    lbw = sb("lbw", [P, 5, 2, HEADS])
    s5_at = nc.sbuf_base
    masks = sb("masks", [P, 7, P], U8)
    ropec = sb("ropec", [P, TB, 8])
    ropes = sb("ropes", [P, TB, 8])
    ropew = sb("ropew", [P, 3, TB, 8])
    small = sb("small", [P, 64])
    stat = sb("stat", [P, 2, 8])
    exch = sb("exch", [P, P])
    d_col = sb("d_col", [P, CT])
    eye16 = sb("eye16", [P, GC])
    sink = sb("sink", [P, QH])
    st2 = sb("st2", [P, 6, 4])
    ARENA = 107 * KB
    base = nc.sbuf_base
    sb("arena", [P, ARENA // 4])

    def at(name, kb, shape, dt=F32):
        n = 4 * int(np.prod(shape[1:])) if dt != U8 else int(np.prod(shape[1:]))
        assert kb * KB + n <= ARENA, name
        return nc.alloc_sbuf_tensor_at(name, shape, dt, offset=base + int(kb * KB))

    h_tmp = nc.alloc_sbuf_tensor_at("h_tmp", [P, KD, S], F32, offset=h_lo_at)

    rms = at("rms", 104, [P, S])
    x_tok = at("x_tok", 0, [P, TB, D])
    par_rows = at("par_rows", 16, [R_ALL, P])
    lam_rows = at("lam_rows", 20, [P, DEPTH * 4, 64])
    pos_i = at("pos_i", 24, [P, TB], I32)
    pos_f = at("pos_f", 25, [P, TB])
    iota_s = at("iota_s", 26, [P, P], I32)
    iota_t = at("iota_t", 27, [P, P], I32)
    xor = at("xor", 28, [P, P], I32)
    Qf = at("Qf", 0, [P, HEADS, S])
    Kf = at("Kf", 8, [P, HEADS, S])
    Qb = at("Qb", 16, [P, HEADS, S])
    Kb = at("Kb", 24, [P, HEADS, S])
    Tx = at("Tx", 32, [P, 2, HEADS * S])
    Ty = at("Ty", 48, [P, 2, HEADS * S // 2])
    s_diag = at("s_diag", 56, [P, HEADS, S])
    b_v = at("b_v", 64, [P, TB, BW])
    s_mate = at("s_mate", 72, [P, HEADS, TB, P])
    s_far = at("s_far", 32, [P, 2, 2 * TB, P])
    ob = at("ob", 40, [P, HEADS, S])
    a_q = at("a_q", 80, [P, TB, BW])
    a_k = at("a_k", 88, [P, TB, BW])
    a_v = at("a_v", 96, [P, TB, BW])
    qT = at("qT", 0, [P, HEADS, S])
    kT = at("kT", 8, [P, HEADS, S])
    prob = at("prob", 16, [P, 2, 2, S])
    wdiff = at("wdiff", 24, [P, 2, S])
    wT = at("wT", 48, [P, 2, TB, S])
    oa = at("oa", 32, [P, HEADS, S])
    sq_b = at("sq_b", 48, [P, HEADS, S])
    sq_a = at("sq_a", 16, [P, HEADS, S])
    rope_w = at("rope_w", 48, [P, 4, TB, 8, 8])
    rope_w2 = at("rope_w2", 52, [P, 4, TB, 8, 8])
    ga = at("ga", 64, [P, KD, S])
    gb = at("gb", 80, [P, KD, S])
    o_hi = at("o_hi", 0, [P, 2 * HEADS, S], F32R)
    o_lo = at("o_lo", 16, [P, 2 * HEADS, S], F32R)
    sg = at("sg", 96, [P, HEADS, S])
    m_hi = at("m_hi", 32, [P, KD, S], F32R)
    m_lo = at("m_lo", 48, [P, KD, S], F32R)
    hid_hi = at("hid_hi", 0, [P, FT, S], F32R)
    hid_lo = at("hid_lo", 44, [P, FT, S], F32R)
    sgu = at("sgu", 88, [P, 2, S])
    ht = at("ht", 92, [P, 2, S])
    q2 = at("q2", 0, [P, 4, S])
    k2 = at("k2", 8, [P, S])
    v2 = at("v2", 10, [P, TB, P])
    g2a = at("g2a", 12, [P, KD, S])
    g2b = at("g2b", 28, [P, KD, S])
    uc = at("uc", 44, [P, GROUPS, 4, GC])
    U = at("U", 60, [P, GROUPS, CH])
    Wt = at("Wt", 68, [P, 2, PAIRS, CT + 1, GC])
    Et = at("Et", 44, [P, 2, PAIRS, CT, GC])
    wt_tmp = at("wt_tmp", 25, [P, PAIRS, CT + 1, GC])
    bias = at("bias", 86.5, [P, QH, 2 * P])
    k_pad = at("k_pad", 86.5, [P, CT, 2 * P])
    him = at("him", 0, [P, PAIRS, CH])
    b_re, b_im = at("b_re", 94.5, [P, PAIRS, GC]), at("b_im", 95.5, [P, PAIRS, GC])
    c_tok = at("c_tok", 96.5, [P, 2, 4, 2, NS])
    c_t = at("c_t", 100.5, [P, 2, PAIRS, GC])
    e_tmp = at("e_tmp", 94.5, [P, PAIRS, CT, GC])
    lg = at("lg", 94.5, [P, 4, 2 * P])
    pT = at("pT", 98.5, [P, 2, 4 * P])
    rot = at("rot", 94.5, [P, 2, PAIRS, CH])
    bb = at("bb", 102.5, [P, 2, PAIRS, GC])
    rot_tmp = at("rot_tmp", 102.5, [P, 2, PAIRS, CH // 2])
    hre = at("hre", 102.5, [P, PAIRS, CH])
    pw = at("pw", 104.5, [P, 2, PAIRS, CT + 1])
    pr = at("pr", 105.6875, [P, 2, PAIRS, CT])
    d0 = at("d0", 8, [P, PAIRS, CH])
    s5 = nc.alloc_sbuf_tensor_at("s5", [P, 16, PAIRS], F32, offset=s5_at)
    s_rows = at("s_rows", 60, [16, 2])
    s_log = at("s_log", 60.5, [16, 2, NS])
    s_lam = at("s_lam", 61, [32, P])
    s_eye = at("s_eye", 8, [P, CT, GC])
    t5_rows = at("t5_rows", 62, [QH, 3 * P])
    t5_rb = at("t5_rb", 64, [QH, 32])
    t5_up = at("t5_up", 12, [P, QH, 2 * P])
    s_tmp = at("s_tmp", 44, [P, 3, PAIRS, CH])
    yt = at("yt", 44, [CH, CT, GROUPS * GC])
    z2 = at("z2", 60, [P, 4, S])
    z_w = at("z_w", 44, [P, 2, 4, S])
    Win = nc.alloc_sbuf_tensor_at("Win", [P, 2, PAIRS, P], F32, offset=h_hi_at)
    Toep = nc.alloc_sbuf_tensor_at("Toep", [P, GROUPS, P], F32, offset=h_lo_at)
    z_hi = at("z_hi", 68, [P, 4, S], F32R)
    z_lo = at("z_lo", 76, [P, 4, S], F32R)
    zz_hi = nc.alloc_sbuf_tensor_at("zz_hi", [P, 4, S], F32R, offset=h_lo_at)
    zz_lo = nc.alloc_sbuf_tensor_at("zz_lo", [P, 4, S], F32R, offset=h_lo_at + 8 * KB)
    o2_hi = nc.alloc_sbuf_tensor_at("o2_hi", [P, 4, S], F32R, offset=h_hi_at)
    o2_lo = nc.alloc_sbuf_tensor_at("o2_lo", [P, 4, S], F32R, offset=h_hi_at + 8 * KB)
    m2_hi = at("m2_hi", 44, [P, KD, S], F32R)
    m2_lo = at("m2_lo", 84, [P, KD, S], F32R)
    HT2 = D_FF // P // 2
    hid2_hi = at("hid2_hi", 0, [P, HT2, S], F32R)
    hid2_lo = at("hid2_lo", 32, [P, HT2, S], F32R)
    y2 = at("y2", 64, [P, KD, S])
    r2 = at("r2", 80, [P, 2, S])
    hq2 = at("hq2", 84, [P, 2, S])
    x_out = at("x_out", 0, [P, TB, D])
    t5_dram = nc.dram_tensor("t5_dram", (QH, 3 * P), F32, kind="Internal").ap()

    psG = ctx.enter_context(nc.psum_tensor("psG", [P, 4, S], F32))
    psH = ctx.enter_context(nc.psum_tensor("psH", [P, 4, S], F32))

    DNORMS = 2
    NT = 2 * KD + HEADS
    raw_in = [sem("raw_in0"), sem("raw_in1")]
    hi_done = sem("hi_done")
    lo_done = sem("lo_done", credit=2)
    tick = sem("tick", credit=4)
    psum_free = [sem("psum_free0", credit=1), sem("psum_free1", credit=1)]
    ld_x, ld_par, ld_misc = sem("ld_x"), sem("ld_par"), sem("ld_misc")
    consts = sem("consts")
    setup = sem("setup")
    setup_pe = sem("setup_pe")
    setup_act = sem("setup_act")
    x_tr = sem("x_tr")
    x_cp = sem("x_cp")
    n_sq, n_ss, n_sd, n_rs, n_rb = sem("n_sq", 1), sem("n_ss", 1), sem("n_sd", 1), sem("n_rs", 1), sem("n_rb", 2)
    d_sq, d_ss, d_sd = sem("d_sq", DNORMS * 4), sem("d_ss", DNORMS), sem("d_sd", DNORMS)
    n_tmp = sem("n_tmp", NT)
    n_hi = sem("n_hi", NT)
    n_lo = sem("n_lo", NT)
    x_done = sem("x_done", 2 * KD, credit=KD)
    b_sig = sem("b_sig", 4)
    b_q = sem("b_q", 2)
    b_tok = sem("b_tok", 2)
    lev_up = sem("lev_up", 10)
    lev_mm = sem("lev_mm", 9)
    lev_cp = sem("lev_cp", 8)
    mate_cp = sem("mate_cp", 1)
    far_mm = sem("far_mm", HEADS)
    far_cp = sem("far_cp", HEADS)
    av_mm = sem("av_mm", HEADS)
    av_cp = sem("av_cp", HEADS)
    a_tok = sem("a_tok", 6)
    rope_d = sem("rope_d", 2)
    qk_tr = sem("qk_tr", 8)
    qk_cp = sem("qk_cp", 8)
    sc_mm = sem("sc_mm", 32)
    sc_max = sem("sc_max", 32)
    sc_exp = sem("sc_exp", 32)
    w_done = sem("w_done", 16)
    w_tr = sem("w_tr", 16)
    w_cp = sem("w_cp", 16)
    oa_mm = sem("oa_mm", HEADS)
    oa_cp = sem("oa_cp", HEADS)
    g_sig = sem("g_sig", 4)
    g_mul = sem("g_mul", 4)
    g_hi = sem("g_hi", 4)
    g_lo = sem("g_lo", 4)
    m_sum = sem("m_sum", 8)
    m_hid = sem("m_hid", 8)
    m_lod = sem("m_lod", 8)
    f_sig = sem("f_sig", FT)
    f_mul = sem("f_mul", FT, credit=2)
    f_hid = sem("f_hid", FT)
    f_lod = sem("f_lod", FT)
    st_out = sem("st_out")

    block = ctx.enter_context(nc.Block())

    def w_src(m, s, src, eng):
        eng.wait_ge(lo_done.sem, m * 2 + (s + 1))
        k, c = src.shape[1], src.shape[2]
        dst = raw[:, s, 0:k * c].rearrange("p (k c) -> p k c", k=k)
        for half in (slice(0, 64), slice(64, P)):
            eng.dma_start(dst[half], src[half]).then_inc(raw_in[s].sem, 16)

    def split_hi(act, m, s):
        act.wait_ge(raw_in[s].sem, m * 32 + 32)
        act.wait_ge(tick.sem, m * 4 + (2 * s + 2))
        act.copy(w_hi[:, s, :], raw[:, s, :]).then_inc(hi_done.sem, 1)

    def T(m, s, half):
        return m * 4 + (2 * s + 1 + half + tick.credit)

    def triple(pe, out, a_hi, a_lo, b_hi, b_lo, first, last):
        pe.matmul(out, a_hi, b_hi, start=first, stop=False)
        pe.matmul(out, a_hi, b_lo, start=False, stop=False)
        return pe.matmul(out, a_lo, b_hi, start=False, stop=last)

    def unit_ready(pe, m, s):
        pe.wait_ge(lo_done.sem, m * 2 + (s + 1 + lo_done.credit))

    def bank_ready(pe, jm, b):
        pe.wait_ge(psum_free[b].sem, jm + 1)

    def pe_feature(pe, m, s, jm, b, x_hi, x_lo, k_wait=None, tiles=(0, 1)):
        if 0 in tiles:
            unit_ready(pe, m, s)
            bank_ready(pe, jm, b)
        wh = w_hi[:, s, :].rearrange("p (k c) -> p k c", k=KD)
        wl = w_lo[:, s, :].rearrange("p (k c) -> p k c", k=KD)
        for j in tiles:
            for k in range(KD):
                if k_wait is not None and j == 0:
                    k_wait(k)
                c = slice(j * P, (j + 1) * P)
                mm = triple(pe, psG[:, 2 * b + j, :], wh[:, k, c], wl[:, k, c], x_hi[:, k, :], x_lo[:, k, :],
                            k == 0, k == KD - 1)
            mm.then_inc(tick.sem, 1)

    def pe_token(pe, m, s, jm, b, halves=(0, 1)):
        if 0 in halves:
            unit_ready(pe, m, s)
            bank_ready(pe, jm, b)
        wh = w_hi[:, s, :].rearrange("p (k c) -> p k c", k=KD)
        wl = w_lo[:, s, :].rearrange("p (k c) -> p k c", k=KD)
        for t in range(TB):
            if t // 2 not in halves:
                continue
            for k in range(KD):
                c = slice(t * P, (t + 1) * P)
                out = psG[:, 2 * b + t // 2, (t % 2) * UC:(t % 2 + 1) * UC]
                mm = triple(pe, out, h_hi[:, k, c], h_lo[:, k, c], wh[:, k, :], wl[:, k, :], k == 0, k == KD - 1)
            if t % 2:
                mm.then_inc(tick.sem, 1)

    def pe_branch(pe, m, s, jm, x_hi, x_lo, k0):
        unit_ready(pe, m, s)
        wh = w_hi[:, s, :].rearrange("p (k c) -> p k c", k=4)
        wl = w_lo[:, s, :].rearrange("p (k c) -> p k c", k=4)
        for j in range(4):
            if j % 2 == 0:
                bank_ready(pe, jm, j // 2)
            for k in range(4):
                c = slice(j * P, (j + 1) * P)
                mm = triple(pe, psG[:, j, :], wh[:, k, c], wl[:, k, c], x_hi[:, k0 + k, :], x_lo[:, k0 + k, :],
                            k == 0, k == 3)
            if j % 2:
                mm.then_inc(tick.sem, 1)

    def square_pair(act, layer, i, pair, src):
        two = slice(2 * pair, 2 * pair + 2)
        act.activation(h_tmp[:, two, :], src[:, two, :], ACT.Square).then_inc(d_sq.sem, 1)

    def sum_pair(pe, layer, i, pair):
        pe.wait_ge(d_sq.sem, d_sq.at(layer, 4 * i + pair + 1))
        for k in (2 * pair, 2 * pair + 1):
            mm = pe.matmul(psH[:, 0, :], ones[:, 0:1].broadcast_to([P, P]), h_tmp[:, k, :],
                           start=k == 0, stop=k == KD - 1)
        if pair == 3:
            mm.then_inc(d_ss.sem, 1)

    def rms_act(act, layer, i):
        act.wait_ge(d_ss.sem, d_ss.at(layer, i + 1))
        act.activation(rms[:, :], psH[:, 0, :], ACT.Sqrt, scale=1.0 / D, bias=eps_ap).then_inc(d_sd.sem, 1)

    def inverse_rms(dve, layer, i):
        dve.wait_ge(d_sd.sem, d_sd.at(layer, i + 1))
        dve.reciprocal(rms[:, :], rms[:, :])
        dve.drain()

    def split_act(act, layer, t0, tmp, hi, n):
        for k in range(n):
            act.wait_ge(n_tmp.sem, n_tmp.at(layer, t0 + k + 1))
            act.copy(hi(k), tmp[:, k, :]).then_inc(n_hi.sem, 1)

    def split_dve(dve, layer, t0, src, tmp, gain, scale, hi, lo, n):
        for k in range(n + 1):
            if k < n:
                dve.scalar_tensor_tensor(out=tmp[:, k, :], in0=src[:, k, :], scalar=gain[:, k:k + 1],
                                         in1=scale(k), op0=ALU.mult, op1=ALU.mult).then_inc(n_tmp.sem, 1)
            if k > 0:
                dve.wait_ge(n_hi.sem, n_hi.at(layer, t0 + k))
                dve.tensor_tensor(lo(k - 1), tmp[:, k - 1, :], hi(k - 1).bitcast(F32), ALU.subtract)\
                   .then_inc(n_lo.sem, 1)

    def rms_split_dve(dve, layer, i, t0, gain):
        inverse_rms(dve, layer, i)
        split_dve(dve, layer, t0, xT, h_tmp, gain, lambda k: rms[:, :], h_hi_t, h_lo_t, KD)

    def heads_act(act, layer):
        act.activation(sq_a[:, :, :], oa[:, :, :], ACT.Square)
        act.activation(sq_b[:, :, :], ob[:, :, :], ACT.Square).then_inc(n_sq.sem, 1)
        act.wait_ge(n_ss.sem, n_ss.at(layer, 1))
        act.activation(rms[0:2 * HEADS, :], psH[0:2 * HEADS, 0, :], ACT.Sqrt, scale=1.0 / P,
                       bias=eps_ap[0:2 * HEADS, :]).then_inc(n_sd.sem, 1)

    def heads_sum_pe(pe, layer):
        pe.wait_ge(n_sq.sem, n_sq.at(layer, 1))
        for n in range(2 * HEADS):
            mm = pe.matmul(psH[0:2 * HEADS, 0, :], one_hot[:, 2 * HEADS - n:4 * HEADS - n],
                           (sq_a, sq_b)[n // HEADS][:, n % HEADS, :], start=n == 0, stop=n == 2 * HEADS - 1)
        mm.then_inc(n_ss.sem, 1)

    def heads_inverse(dve, layer):
        dve.wait_ge(n_sd.sem, n_sd.at(layer, 1))
        dve.reciprocal(rms[0:2 * HEADS, :], rms[0:2 * HEADS, :]).then_inc(n_rs.sem, 1)

    def heads_spread_pe(pe, layer, b):
        if b == 0:
            pe.wait_ge(n_rs.sem, n_rs.at(layer, 1))
        else:
            pe.wait_ge(n_tmp.sem, n_tmp.at(layer, T_DA + HEADS))
        for a in range(HEADS):
            n = b * HEADS + a
            mm = pe.matmul(psH[:, a, :], ident[0:2 * HEADS, n:n + 1].broadcast_to([2 * HEADS, P]),
                           rms[0:2 * HEADS, :], start=True, stop=True)
        mm.then_inc(n_rb.sem, 1)

    eps_ap = small[:, 48:49]

    def h_hi_t(k):
        return h_hi[:, k, :]

    def h_lo_t(k):
        return h_lo[:, k, :]

    T_ATTN, T_DA, T_FFN = 0, KD, KD + HEADS

    def halves(x, h):
        return x[:, :, :].rearrange("p a (n two i) -> p (a n) two i", two=2, i=h)

    def totals(level):
        n = HEADS * S >> level
        t = Tx if level % 2 == 0 else Ty
        return t[:, :, 0:n]


    ALL_PAIRS = DEPTH * U_LAYER + U_SECOND

    def level_update(dve, h):
        if h == 1:
            dve.tensor_tensor(Qb[:, :, :], Qf[:, :, :], Tx[:, 1, :].rearrange("p (a t) -> p a t", a=HEADS), ALU.mult)
            dve.drain()
            dve.tensor_tensor(Qf[:, :, :], Qf[:, :, :], Tx[:, 0, :].rearrange("p (a t) -> p a t", a=HEADS),
                              ALU.mult).then_inc(lev_up.sem, 1)
            return
        b = h // 2
        lg = b.bit_length() - 1
        n = HEADS * S // (2 * b)
        t = totals(lg).rearrange("p d (n two) -> p d n two", two=2)
        if h < 2 * P:
            dve.tensor_tensor(totals(lg + 1), t[:, :, :, 0], t[:, :, :, 1], ALU.mult)
        for x, side, d in ((Qf, 1, 0), (Kf, 0, 0), (Qb, 0, 1), (Kb, 1, 1)):
            part = halves(x, b)[:, :, side, :]
            mm = dve.tensor_tensor(part, part, t[:, d, :, 1 - side:2 - side].broadcast_to([P, n, b]), ALU.mult)
        mm.then_inc(lev_up.sem, 1)

    def level_pe(pe, layer, lv):
        pe.wait_ge(lev_up.sem, lev_up.at(layer, lv + 1))
        if lv == 0:
            pe.wait_ge(b_q.sem, b_q.at(layer, 2))
        else:
            pe.wait_ge(lev_cp.sem, lev_cp.at(layer, lv))
        for a in range(HEADS):
            for blk in range(TB):
                c = slice(blk * P, (blk + 1) * P)
                out = psH[:, a, c]
                if lv == 0:
                    pe.matmul(out, Kf[:, a, c], Qf[:, a, c], start=True, stop=False)
                    mm = pe.matmul(out, Kb[:, a, c], Qf[:, a, c], start=False, stop=True)
                    continue
                for k, q, side in ((Kf, Qf, 1), (Kb, Qb, 0)):
                    cut = "p (n two i) -> p n two i"
                    i = 1 << (lv - 1)
                    mm = pe.matmul(out.rearrange(cut, two=2, i=i)[:, :, side, :], k[:, a, c],
                                   q[:, a, c].rearrange(cut, two=2, i=i)[:, :, side, :], start=True, stop=True)
        mm.then_inc(lev_mm.sem, 1)

    def level_copy(dve, layer, lv):
        dve.wait_ge(lev_mm.sem, lev_mm.at(layer, lv + 1))
        if lv:
            dve.memset(small[:, 63:64], 0.0)
        for a in range(HEADS):
            if lv == 0:
                mm = dve.tensor_copy(s_diag[:, a, :], psH[:, a, :])
            else:
                m = masks[:, lv - 1:lv, :].broadcast_to([P, TB, P])
                mm = dve.copy_predicated(s_diag[:, a, :].rearrange("p (b t) -> p b t", b=TB), m,
                                         psH[:, a, :].rearrange("p (b t) -> p b t", b=TB))
        mm.then_inc(lev_cp.sem, 1)
        dve.wait_ge(lev_cp.sem, lev_cp.at(layer, lv + 1))

    def blk(x, a, j):
        return x[:, a, j * P:(j + 1) * P]

    def mate_pe(pe, layer):
        pe.wait_ge(lev_up.sem, lev_up.at(layer, 9))
        pe.wait_ge(lev_cp.sem, lev_cp.at(layer, 8))
        for a in range(HEADS):
            for s in range(TB):
                k, q = (Kf, Qf) if s % 2 == 0 else (Kb, Qb)
                mm = pe.matmul(psH[:, a, s * P:(s + 1) * P], blk(k, a, s), blk(q, a, s ^ 1), start=True, stop=True)
        mm.then_inc(lev_mm.sem, 1)

    def far_pe(pe, layer, a):
        if a == 0:
            pe.wait_ge(lev_up.sem, lev_up.at(layer, 10))
            pe.wait_ge(mate_cp.sem, mate_cp.at(layer, 1))
        elif a == 1:
            pe.wait_ge(a_tok.sem, a_tok.at(layer, 6))
        else:
            pe.wait_ge(far_cp.sem, far_cp.at(layer, a - 1))
        for s in range(TB):
            k, q = (Kf, Qf) if s < 2 else (Kb, Qb)
            t0 = 2 * P if s < 2 else 0
            mm = pe.matmul((psH, psG)[a % 2][:, s // 2, (s % 2) * 2 * P:(s % 2 + 1) * 2 * P], blk(k, a, s),
                           q[:, a, t0:t0 + 2 * P], start=True, stop=True)
        mm.then_inc(far_mm.sem, 1)

    def hgrn_out_pe(pe, layer, a):
        pe.wait_ge(far_cp.sem, far_cp.at(layer, a + 1))
        pe.wait_ge(b_tok.sem, b_tok.at(layer, 2))
        if a >= 2:
            pe.wait_ge(av_cp.sem, av_cp.at(layer, a - 1))
        for t in range(TB):
            for s in range(TB):
                if s == t:
                    sc = blk(s_diag, a, t)
                elif s == t ^ 1:
                    sc = s_mate[:, a, s, :]
                else:
                    sc = s_far[:, a % 2, 2 * s + t % 2, :]
                mm = pe.matmul(psH[:, 2 + a % 2, t * P:(t + 1) * P], b_v[:, s, a * P:(a + 1) * P], sc,
                               start=s == 0, stop=s == TB - 1)
        mm.then_inc(av_mm.sem, 1)

    def rope(dve, layer, n):
        for x in ((a_q, a_k)[n],):
            dve.wait_ge(a_tok.sem, a_tok.at(layer, 2 * n + 2))
            v = x[:, :, :].rearrange("p t (c d) -> p t c d", d=64)
            w = rope_w if n == 0 else rope_w2
            for t in range(TB):
                cos = ropec[:, t:t + 1, :].broadcast_to([P, 8, 8])
                sin = ropes[:, t:t + 1, :].broadcast_to([P, 8, 8])
                t1, t2 = v[:, t, :, 0:8], v[:, t, :, 8:16]
                for j, (a, b) in enumerate(((t1, cos), (t2, sin), (t2, cos), (t1, sin))):
                    dve.tensor_tensor(w[:, j, t], a, b, ALU.mult)
            dve.drain()
            for t in range(TB):
                dve.tensor_tensor(v[:, t, :, 0:8], w[:, 0, t], w[:, 1, t], ALU.subtract)
                mm = dve.tensor_tensor(v[:, t, :, 8:16], w[:, 2, t], w[:, 3, t], ALU.add)
            mm.then_inc(rope_d.sem, 1)

    def qk_pe(pe, layer):
        for n, x in enumerate((a_q, a_k)):
            pe.wait_ge(rope_d.sem, rope_d.at(layer, n + 1))
            for a in range(HEADS):
                i = n * HEADS + a
                if not n and a >= 2:
                    pe.wait_ge(av_cp.sem, av_cp.at(layer, a + 1))
                if n:
                    pe.wait_ge(qk_cp.sem, qk_cp.at(layer, i - 3))
                for t in range(TB):
                    mm = pe.transpose(psH[:, a, t * P:(t + 1) * P], x[:, t, a * P:(a + 1) * P], ident[:, :])
                mm.then_inc(qk_tr.sem, 1)

    def qk_act(act, layer):
        for i in range(2 * HEADS):
            act.wait_ge(qk_tr.sem, qk_tr.at(layer, i + 1))
            if i < HEADS:
                act.activation(qT[:, i, :], psH[:, i, :], ACT.Copy, scale=64 ** -0.5).then_inc(qk_cp.sem, 1)
            else:
                act.copy(kT[:, i - HEADS, :], psH[:, i - HEADS, :]).then_inc(qk_cp.sem, 1)

    STEPS = HEADS * TB

    def attention_pe(pe, layer):
        um, jm = layer * U_LAYER, layer * J_LAYER
        pe.wait_ge(qk_cp.sem, qk_cp.at(layer, 8))
        pe.wait_ge(a_tok.sem, a_tok.at(layer, 6))
        for it in range(STEPS + 2):
            if it < STEPS:
                a, qb = divmod(it, TB)
                if it:
                    pe.wait_ge(sc_exp.sem, sc_exp.at(layer, 2 * it))
                for c in range(2):
                    d = slice(64 * c, 64 * c + 64)
                    pe.matmul(psH[:, c, :], qT[d, a, qb * P:(qb + 1) * P], kT[d, a, :],
                              start=True, stop=True).then_inc(sc_mm.sem, 1)
                g = it // 2
                pe_feature(pe, um + (U_GATES + g // 2), g % 2, jm + (U_GATES + g // 2), g % 2, h_hi, h_lo,
                           tiles=(it % 2,))
            if 1 <= it <= STEPS:
                j = it - 1
                pe.wait_ge(w_done.sem, w_done.at(layer, j + 1))
                if j:
                    pe.wait_ge(w_cp.sem, w_cp.at(layer, j))
                for s in range(TB):
                    mm = pe.transpose(psH[:, 2, s * P:(s + 1) * P], wdiff[:, j % 2, s * P:(s + 1) * P],
                                      ident[:, :])
                mm.then_inc(w_tr.sem, 1)
            if it >= 2 and (it - 2) % TB == TB - 1:
                a = (it - 2) // TB
                pe.wait_ge(w_cp.sem, w_cp.at(layer, TB * (a + 1)))
                if a:
                    pe.wait_ge(oa_cp.sem, oa_cp.at(layer, a))
                for s in range(TB):
                    mm = pe.matmul(psH[:, 3, :], a_v[:, s, a * P:(a + 1) * P], wT[:, a % 2, s, :],
                                   start=s == 0, stop=s == TB - 1)
                mm.then_inc(oa_mm.sem, 1)

    def attention_act(act, layer):
        for it in range(STEPS + 1):
            if it < STEPS:
                if it >= 2:
                    act.wait_ge(w_done.sem, w_done.at(layer, it - 1))
                for c in range(2):
                    act.wait_ge(sc_max.sem, sc_max.at(layer, 2 * it + c + 1))
                    act.activation(prob[:, it % 2, c, :], psH[:, c, :], ACT.Exp,
                                   bias=stat[:, it % 2, c:c + 1],
                                   accum_out=stat[:, it % 2, 2 + c:3 + c]).then_inc(sc_exp.sem, 1)
            if it >= 1:
                j = it - 1
                g = j // 2
                m, s = layer * U_LAYER + (U_GATES + g // 2), g % 2
                act.wait_ge(tick.sem, T(m, s, j % 2))
                mm = act.copy((ga, gb)[j // KD][:, j % KD, :], psG[:, 2 * s + j % 2, :])
                if j % 2:
                    mm.then_inc(psum_free[s].sem, 1)
                    split_hi(act, m + 1, s)
                a, qb = divmod(j, TB)
                act.wait_ge(w_tr.sem, w_tr.at(layer, j + 1))
                if a >= 2 and qb == 0:
                    act.wait_ge(oa_mm.sem, oa_mm.at(layer, a - 1))
                act.copy(wT[:, a % 2, :, qb * P:(qb + 1) * P],
                         psH[:, 2, :].rearrange("p (s q) -> p s q", s=TB)).then_inc(w_cp.sem, 1)

    def attention_dve(dve, layer):
        for it in range(STEPS + 3):
            if it < STEPS:
                if it >= 2:
                    dve.wait_ge(w_done.sem, w_done.at(layer, it - 1))
                for c in range(2):
                    dve.wait_ge(sc_mm.sem, sc_mm.at(layer, 2 * it + c + 1))
                    dve.tensor_reduce(stat[:, it % 2, c:c + 1], psH[:, c, :], AX.X, ALU.max,
                                      negate=True).then_inc(sc_max.sem, 1)
            if 1 <= it <= STEPS:
                j = it - 1
                st = stat[:, j % 2, :]
                dve.wait_ge(sc_exp.sem, sc_exp.at(layer, 2 * j + 2))
                dve.reciprocal(st[:, 4:6], st[:, 2:4])
                dve.drain()
                dve.tensor_scalar(st[:, 6:7], st[:, 5:6], cur[:, L_NLAM:L_NLAM + 1], None, ALU.mult)
                dve.tensor_scalar(prob[:, j % 2, 0, :], prob[:, j % 2, 0, :], st[:, 4:5], None, ALU.mult)
                dve.drain()
                if j >= 2:
                    dve.wait_ge(w_tr.sem, w_tr.at(layer, j - 1))
                dve.scalar_tensor_tensor(out=wdiff[:, j % 2, :], in0=prob[:, j % 2, 1, :], scalar=st[:, 6:7],
                                         in1=prob[:, j % 2, 0, :], op0=ALU.mult, op1=ALU.add)\
                   .then_inc(w_done.sem, 1)
            if it >= 3 and (it - 3) % TB == TB - 1:
                a = (it - 3) // TB
                dve.wait_ge(oa_mm.sem, oa_mm.at(layer, a + 1))
                dve.tensor_copy(oa[:, a, :], psH[:, 3, :]).then_inc(oa_cp.sem, 1)

    inv_freq = [float(np.float32(500000.0) ** np.float32(-i / 16)) for i in range(0, 16, 2)]

    def reduce_angle(dve, out, ang, k, cosine):
        dve.tensor_scalar(k, ang, 1 / TWO_PI, 0.25 if cosine else 0.0, ALU.mult, ALU.add)
        dve.drain()
        dve.tensor_scalar(k, k, ROUND, ROUND, ALU.add, ALU.subtract)
        dve.drain()
        dve.scalar_tensor_tensor(out=out, in0=k, scalar=-PI_HI, in1=ang, op0=ALU.mult, op1=ALU.add)
        dve.drain()
        dve.scalar_tensor_tensor(out=out, in0=k, scalar=-PI_MID, in1=out, op0=ALU.mult, op1=ALU.add)
        dve.drain()
        dve.scalar_tensor_tensor(out=out, in0=k, scalar=-PI_LO, in1=out, op0=ALU.mult, op1=ALU.add)
        dve.drain()
        if cosine:
            dve.tensor_scalar(out, out, math.pi / 2, None, ALU.add)
            dve.drain()
        return dve.tensor_scalar(out, out, PI_MAX, -PI_MAX, ALU.min, ALU.max)

    def setup_pool(pool):
        pool.sem_inc(lo_done.sem, lo_done.credit)
        pool.memset(ident[:, :], 0.0).then_inc(consts.sem, 1)
        pool.memset(ones[:, :], 1.0).then_inc(consts.sem, 1)
        pool.memset(small[:, 48:49], EPS).then_inc(consts.sem, 1)
        pool.iota(iota_s[:, :], [[0, P]], base=0, channel_multiplier=1).then_inc(consts.sem, 1)
        pool.iota(iota_t[:, :], [[1, P]], base=0, channel_multiplier=0).then_inc(consts.sem, 1)
        pool.wait_ge(consts.sem, 5)
        pool.affine_select(out=ident[:, :], in_=ident[:, :], compare_op=ALU.not_equal, fill=1.0, base=0,
                           pattern=[[-1, P]], channel_multiplier=1).then_inc(consts.sem, 1)

    def setup_sync(sp):
        sp.dma_start(x_tok[:, :, :], io["x"].rearrange("a (t p) d -> p (a t) d", p=P)).then_inc(ld_x.sem, 16)
        rows = [(R_ATTN, io["attn_norm"].rearrange("l (k p) -> (l k) p", p=P)),
                (R_FFN, io["ffn_norm"].rearrange("l (k p) -> (l k) p", p=P)),
                (R_DA, io["da_norm"].rearrange("l (k p) -> (l k) p", p=P)),
                (R_HG, io["hg_norm"].rearrange("l (k p) -> (l k) p", p=P)),
                (R_LB, io["hg_lb_logits"].rearrange("d l (k p) -> (d l k) p", p=P)),
                (R_FINAL, io["final_norm"].rearrange("(k p) -> k p", p=P)),
                (R_PRE2, io["norm_mix_pre_2"].rearrange("l (k p) -> (l k) p", p=P)),
                (R_POST2, io["norm_mix_post_2"].rearrange("l (k p) -> (l k) p", p=P)),
                (R_MPRE2, io["norm_mlp_pre_2"].rearrange("l (k p) -> (l k) p", p=P)),
                (R_MPOST2, io["norm_mlp_post_2"].rearrange("l (k p) -> (l k) p", p=P))]
        for r, src in rows:
            sp.dma_start(par_rows[r:r + src.shape[0], :], src).then_inc(ld_par.sem, 16)
        sp.dma_start(lam_rows[:, :, :].rearrange("p a d -> p (a d)"),
                     io["da_lambda"].rearrange("l a d -> (l a d)").partition_broadcast(P))\
          .then_inc(ld_misc.sem, 16)
        with nc.allow_non_contiguous_dma(reason="512 positions, one word each"):
            sp.dma_start(pos_i[:, :], io["positions"].rearrange("a (t p) -> p (a t)", p=P)).then_inc(ld_misc.sem, 16)

    def setup_pe_part(pe):
        pe.sem_inc(tick.sem, tick.credit)
        pe.wait_ge(consts.sem, 6)
        pe.wait_ge(ld_par.sem, 160)
        pe.transpose(psG[:, 0, 0:R_ALL], par_rows[:, :], ident[0:R_ALL, 0:R_ALL]).then_inc(setup_pe.sem, 1)
        pe.wait_ge(ld_x.sem, 16)
        for k in range(KD):
            if k >= TB:
                pe.wait_ge(x_cp.sem, k - TB + 1)
            for t in range(TB):
                mm = pe.transpose(psH[:, k % TB, t * P:(t + 1) * P], x_tok[:, t, k * P:(k + 1) * P], ident[:, :])
            mm.then_inc(x_tr.sem, 1)

    def setup_dve(dve):
        dve.sem_inc(psum_free[0].sem, 1)
        dve.sem_inc(f2_q.sem, f2_q.credit)
        dve.sem_inc(f_mul.sem, f_mul.credit)
        dve.sem_inc(psum_free[1].sem, 1)
        dve.wait_ge(setup_pe.sem, 1)
        dve.tensor_copy(par[:, :], psG[:, 0, 0:R_ALL])
        dve.drain()
        lg = par[:, R_LB:R_LB + 16].rearrange("p (d l a) -> p d l a", d=2, l=DEPTH)
        dve.tensor_tensor(lbw[:, 0], lg[:, :, 0, :], lg[:, :, 1, :], ALU.max)
        dve.drain()
        for l in range(DEPTH):
            mm = dve.tensor_tensor(lbw[:, 1 + l], lg[:, :, l, :], lbw[:, 0], ALU.subtract)
        mm.then_inc(setup.sem, 1)
        dve.wait_ge(ld_misc.sem, 32)
        lam = lam_rows[:, :, :].rearrange("p (a b) d -> p a b d", b=2)
        dve.tensor_tensor(lam[:, :, 0, :], lam[:, :, 0, :], lam[:, :, 1, :], ALU.mult)
        dve.tensor_copy(pos_f[:, :], pos_i[:, :])
        dve.drain()
        dve.tensor_reduce(small[:, 50:54], lam[:, :, 0, :], AX.X, ALU.add)
        for f in range(8):
            dve.tensor_scalar(ropew[:, 0, :, f], pos_f[:, :], inv_freq[f], None, ALU.mult)
        dve.drain()
        reduce_angle(dve, ropew[:, 1], ropew[:, 0], ropec[:, :, :], True)
        reduce_angle(dve, ropew[:, 2], ropew[:, 0], ropes[:, :, :], False)
        dve.drain().then_inc(setup.sem, 1)
        for k in range(KD):
            dve.wait_ge(x_tr.sem, k + 1)
            dve.tensor_copy(xT[:, k, :], psH[:, k % TB, :]).then_inc(x_cp.sem, 1)
            if k % 2:
                dve.drain().then_inc(x_done.sem, 2)
        dve.wait_ge(setup_act.sem, 1)
        dve.tensor_tensor(lbw[:, 3], lbw[:, 1], lbw[:, 2], ALU.add)
        dve.drain()
        dve.reciprocal(lbw[:, 0], lbw[:, 3])
        dve.drain()
        for l in range(DEPTH):
            dve.tensor_tensor(lbw[:, 1 + l], lbw[:, 1 + l], lbw[:, 0], ALU.mult)
        dve.drain()
        dve.tensor_tensor(lbw[:, 3], lbw[:, 1], lbw[:, 2], ALU.add)
        dve.tensor_copy(lbw[:, 4], lbw[:, 1])
        dve.drain()
        for l in range(DEPTH):
            p0 = lay[:, l, :]
            dve.tensor_tensor(p0[:, L_LB:L_LB + 8].rearrange("p (d a) -> p d a", d=2), lbw[:, 4 - l], lbw[:, 1],
                              ALU.subtract)
            dve.tensor_copy(p0[:, L_ATTN:L_ATTN + 8], par[:, R_ATTN + 8 * l:R_ATTN + 8 * l + 8])
            dve.tensor_copy(p0[:, L_FFN:L_FFN + 8], par[:, R_FFN + 8 * l:R_FFN + 8 * l + 8])
            dve.tensor_scalar(p0[:, L_DA:L_DA + 4], par[:, R_DA + 4 * l:R_DA + 4 * l + 4], 1.0 - lam_init(l), None,
                              ALU.mult)
            dve.tensor_copy(p0[:, L_HG:L_HG + 4], par[:, R_HG + 4 * l:R_HG + 4 * l + 4])
            dve.scalar_tensor_tensor(out=p0[:, L_NLAM:L_NLAM + 1], in0=small[:, 55 + 2 * l:56 + 2 * l],
                                     scalar=-lam_init(l), in1=small[:, 54 + 2 * l:55 + 2 * l], op0=ALU.add,
                                     op1=ALU.subtract)
        dve.drain()
        for l in range(DEPTH):
            dve.tensor_scalar(lay[:, l, L_OMLB:L_OMLB + 8], lay[:, l, L_LB:L_LB + 8], -1.0, 1.0, ALU.mult, ALU.add)
        dve.wait_ge(consts.sem, 5)
        dve.tensor_tensor(xor[:, :], iota_s[:, :], iota_t[:, :], ALU.bitwise_xor)
        dve.drain()
        for j in range(7):
            dve.tensor_scalar(masks[:, j, :], xor[:, :], float(1 << j), None, ALU.is_ge)
        dve.memset(one_hot[:, :], 0.0)
        dve.drain()
        dve.memset(one_hot[:, 2 * HEADS:2 * HEADS + 1], 1.0)

    def setup_act_part(act):
        act.wait_ge(setup.sem, 1)
        act.activation(lbw[:, 1:3], lbw[:, 1:3], ACT.Exp)
        act.wait_ge(setup.sem, 2)
        act.activation(small[:, 54:58], small[:, 50:54], ACT.Exp)
        act.activation(ropec[:, :, :], ropew[:, 1], ACT.Sin)
        act.activation(ropes[:, :, :], ropew[:, 2], ACT.Sin)
        act.drain().then_inc(setup_act.sem, 1)

    def layer_sync(sp, l):
        def w(name, rows, cols):
            return io[name][ds(l, 1), rows, cols].rearrange("a (k p) c -> p (a k) c", p=P)

        m = l * U_LAYER
        at_pair = 0
        for c0, pairs in WIN_RUNS:
            with sp.Fori(0, pairs) as i:
                for s in range(2):
                    w_src(m + i + at_pair, s, w("w_in", slice(0, D), ds(i * 512 + (c0 + 256 * s), UC)), sp)
            at_pair += pairs
        for name, u in (("w_a", U_WA), ("w_b", U_WB)):
            for s in range(2):
                w_src(m + u, s, w(name, slice(0, BW), slice(512 * s, 512 * s + 512)), sp)
        with sp.Fori(0, 2) as i:
            for s in range(2):
                w_src(m + i + U_WO, s, w("w_o", slice(0, D), ds(i * 512 + 256 * s, UC)), sp)
        with sp.Fori(0, FT // 2) as i:
            for s, name in enumerate(("w_gate", "w_up")):
                w_src(m + i + U_GU, s, w(name, slice(0, D), ds(i * UC, UC)), sp)
        with sp.Fori(0, 2) as i:
            for u in range(6):
                k0 = KD * (u % 3)
                rows = slice(k0 * P, min(k0 + KD, FT) * P)
                w_src(m + i * 3 + (U_DN + u // 2), u % 2, w("w_down", rows, ds(i * 512 + UC * (u // 3), UC)), sp)

    def layer_pe(pe, l):
        um, jm = l * U_LAYER, l * J_LAYER

        def first_tile(k):
            pe.wait_ge(n_lo.sem, n_lo.at(l, T_ATTN + k + 1))

        for u in range(6):
            pe_feature(pe, um + u // 2, u % 2, jm + u // 2, u % 2, h_hi, h_lo, first_tile if u == 0 else None)
        for lv in range(8):
            level_pe(pe, l, lv)
            u = 6 + lv
            pe_token(pe, um + u // 2, u % 2, jm + u // 2, u % 2, (0, 1) if lv < 7 else (0,))
        mate_pe(pe, l)
        pe_token(pe, um + u // 2, u % 2, jm + u // 2, u % 2, (1,))
        for a in range(HEADS + 1):
            if a < HEADS:
                far_pe(pe, l, a)
            if a:
                hgrn_out_pe(pe, l, a - 1)
        qk_pe(pe, l)
        attention_pe(pe, l)
        pe_feature(pe, um + U_BG, 0, jm + U_BG, 0, h_hi, h_lo, tiles=(0,))
        heads_sum_pe(pe, l)
        pe_feature(pe, um + U_BG, 0, jm + U_BG, 0, h_hi, h_lo, tiles=(1,))
        heads_spread_pe(pe, l, 0)
        pe_feature(pe, um + U_BG, 1, jm + U_BG, 1, h_hi, h_lo)
        heads_spread_pe(pe, l, 1)
        pe.wait_ge(n_lo.sem, n_lo.at(l, T_DA + HEADS))
        pe_branch(pe, um + U_WA, 0, jm + J_WA, o_hi, o_lo, 0)
        pe_branch(pe, um + U_WA, 1, jm + (J_WA + 1), o_hi, o_lo, 0)
        for u in range(2):
            if u == 0:
                pe.wait_ge(g_lo.sem, g_lo.at(l, HEADS))
            pe_branch(pe, um + U_WB, u, jm + (J_WB + u), o_hi, o_lo, HEADS)

        def merged_tile(k):
            pe.wait_ge(m_lod.sem, m_lod.at(l, k + 1))

        for u in range(4):
            pe_feature(pe, um + (U_WO + u // 2), u % 2, jm + (J_WO + u // 2), u % 2, m_hi, m_lo,
                       merged_tile if u == 0 else None)
            if u:
                sum_pair(pe, l, 1, u - 1)
        sum_pair(pe, l, 1, 3)

        def ffn_tile(k):
            pe.wait_ge(n_lo.sem, n_lo.at(l, T_FFN + k + 1))

        with pe.Fori(0, FT // 2) as i:
            for s in range(2):
                pe_feature(pe, um + i + U_GU, s, jm + i + J_GU, s, h_hi, h_lo, ffn_tile if s == 0 else None)
        for p in range(4):
            bank_ready(pe, jm + (J_DN + p // 2), p % 2)
            for v in range(3):
                u = 3 * p + v

                def hidden_tile(k, v=v):
                    pe.wait_ge(f_lod.sem, f_lod.at(l, KD * v + k + 1))

                pe_part(pe, um + (U_DN + u // 2), u % 2, p % 2, hid_hi, hid_lo, KD * v,
                        min(KD, FT - KD * v), v == 0, v == 2, hidden_tile if p == 0 else None)
                if p and v == 0:
                    sum_pair(pe, l + 1, 0, p - 1)
        sum_pair(pe, l + 1, 0, 3)

    def pe_part(pe, m, s, b, x_hi, x_lo, k0, nk, first, last, k_wait=None):
        unit_ready(pe, m, s)
        wh = w_hi[:, s, 0:nk * UC].rearrange("p (k c) -> p k c", k=nk)
        wl = w_lo[:, s, 0:nk * UC].rearrange("p (k c) -> p k c", k=nk)
        for j in range(2):
            for k in range(nk):
                if k_wait is not None and j == 0:
                    k_wait(k)
                c = slice(j * P, (j + 1) * P)
                mm = triple(pe, psG[:, 2 * b + j, :], wh[:, k, c], wl[:, k, c], x_hi[:, k0 + k, :],
                            x_lo[:, k0 + k, :], first and k == 0, last and k == nk - 1)
            mm.then_inc(tick.sem, 1)

    def layer_act(act, l):
        um = l * U_LAYER
        rms_act(act, l, 0)
        split_act(act, l, T_ATTN, h_tmp, h_hi_t, KD)
        for u in range(6):
            m, s = um + u // 2, u % 2
            split_hi(act, m + 1, s)
            for j in range(2):
                act.wait_ge(tick.sem, T(m, s, j))
                a = 2 * (u % 2) + j
                src = psG[:, 2 * s + j, :]
                if u < 4:
                    d = u // 2
                    act.activation(Tx[:, d, a * S:(a + 1) * S], src, ACT.Sigmoid)
                    mm = act.activation((Kf, Kb)[d][:, a, :], src, ACT.Sigmoid, scale=-1.0)
                else:
                    mm = act.copy(Qf[:, a, :], src)
            mm.then_inc(psum_free[s].sem, 1)
            act.drain().then_inc((b_sig if u < 4 else b_q).sem, 1)
        for u in range(6, 14):
            if u == 13:
                act.wait_ge(lev_mm.sem, lev_mm.at(l, 9))
                act.copy(s_mate[:, :, :, :].rearrange("p a s t -> p (a s t)"),
                         psH[:, :, :].rearrange("p a t -> p (a t)")).then_inc(mate_cp.sem, 1)
            m, s = um + u // 2, u % 2
            split_hi(act, m + 1, s)
            dst = (b_v, a_q, a_k, a_v)[(u - 6) // 2]
            act.wait_ge(tick.sem, T(m, s, 1))
            act.copy(dst[:, :, s * UC:(s + 1) * UC],
                     psG[:, 2 * s:2 * s + 2, :].rearrange("p b (t c) -> p (b t) c", c=UC))\
               .then_inc(psum_free[s].sem, 1)
            act.drain().then_inc((b_tok if u < 8 else a_tok).sem, 1)
        for a in range(HEADS):
            act.wait_ge(far_mm.sem, far_mm.at(l, a + 1))
            if a >= 2:
                act.wait_ge(av_mm.sem, av_mm.at(l, a - 1))
            act.copy(s_far[:, a % 2, :, :].rearrange("p s t -> p (s t)"),
                     (psH, psG)[a % 2][:, 0:2, :].rearrange("p a t -> p (a t)")).then_inc(far_cp.sem, 1)
        qk_act(act, l)
        attention_act(act, l)
        act.wait_ge(oa_cp.sem, oa_cp.at(l, HEADS))
        heads_act(act, l)
        act.drain()
        act.activation(ga[:, :, :], ga[:, :, :], ACT.Sigmoid).then_inc(g_sig.sem, 1)

        def output_gate(u):
            m, s = um + U_BG, u
            split_hi(act, m + 1, s)
            for j in range(2):
                act.wait_ge(tick.sem, T(m, s, j))
                mm = act.activation(sg[:, 2 * u + j, :], psG[:, 2 * s + j, :], ACT.Sigmoid)
            mm.then_inc(psum_free[s].sem, 1)
            act.drain().then_inc(g_sig.sem, 1)

        output_gate(0)
        split_act(act, l, T_DA, oa, lambda k: o_hi[:, k, :], HEADS)
        output_gate(1)
        act.activation(gb[:, :, :], gb[:, :, :], ACT.Sigmoid).then_inc(g_sig.sem, 1)
        for a in range(HEADS):
            act.wait_ge(g_mul.sem, g_mul.at(l, a + 1))
            act.copy(o_hi[:, HEADS + a, :], ob[:, a, :]).then_inc(g_hi.sem, 1)
        for u in range(4):
            split_hi(act, um + (U_WA + 1 + u // 2), u % 2)
            if u >= 2:
                for k in range(4 * (u - 2), 4 * (u - 2) + 4):
                    act.wait_ge(m_sum.sem, m_sum.at(l, k + 1))
                    act.copy(m_hi[:, k, :], ga[:, k, :]).then_inc(m_hid.sem, 1)
        for u in range(4):
            if u:
                act.wait_ge(x_done.sem, x_done.at(l, 2 * u))
                square_pair(act, l, 1, u - 1, xT)
            split_hi(act, um + (U_WO + 1 + u // 2), u % 2)
        act.wait_ge(x_done.sem, x_done.at(l, KD))
        square_pair(act, l, 1, 3, xT)
        rms_act(act, l, 1)
        split_act(act, l, T_FFN, h_tmp, h_hi_t, KD)
        with act.Fori(0, FT // 2) as i:
            m = um + i + U_GU
            split_hi(act, m + 1, 0)
            for j in range(2):
                act.wait_ge(f_mul.sem, f_mul.at(l, j - 1) + i * 2)
                act.wait_ge(tick.sem, T(m, 0, j))
                act.activation(sgu[:, j, :], psG[:, j, :], ACT.Sigmoid).then_inc(f_sig.sem, 1)
            split_hi(act, m + 1, 1)
            for j in range(2):
                act.wait_ge(f_mul.sem, f_mul.at(l, 0) + i * 2 + (j + 1))
                act.copy(hid_hi[:, ds(i * 2 + j, 1), :].rearrange("p a t -> p (a t)"), ht[:, j, :])\
                   .then_inc(f_hid.sem, 1)
        for u in range(12):
            if u % 3 == 0 and u:
                act.wait_ge(x_done.sem, x_done.at(l, KD + 2 * (u // 3)))
                square_pair(act, l + 1, 0, u // 3 - 1, xT)
            split_hi(act, um + (U_DN + 1 + u // 2), u % 2)
        act.wait_ge(x_done.sem, x_done.at(l, 2 * KD))
        square_pair(act, l + 1, 0, 3, xT)

    def layer_dve(dve, l):
        um = l * U_LAYER
        dve.tensor_copy(cur[:, :], lay[:, ds(l, 1), :].rearrange("p a c -> p (a c)"))
        dve.drain()
        rms_split_dve(dve, l, 0, T_ATTN, cur[:, L_ATTN:L_ATTN + KD])
        for d in range(2):
            dve.wait_ge(b_sig.sem, b_sig.at(l, 2 * d + 2))
            for a in range(HEADS):
                c = 4 * d + a
                lb, omlb = cur[:, L_LB + c:L_LB + c + 1], cur[:, L_OMLB + c:L_OMLB + c + 1]
                t = Tx[:, d, a * S:(a + 1) * S]
                dve.tensor_scalar(t, t, omlb, lb, ALU.mult, ALU.add)
                k = (Kf, Kb)[d][:, a, :]
                mm = dve.tensor_scalar(k, k, omlb, None, ALU.mult)
        mm.then_inc(lev_up.sem, 1)
        dve.wait_ge(lev_up.sem, lev_up.at(l, 1))
        for lv in range(8):
            level_copy(dve, l, lv)
            level_update(dve, 1 << lv)
            dve.wait_ge(lev_up.sem, lev_up.at(l, lv + 2))
        dve.wait_ge(lev_mm.sem, lev_mm.at(l, 9))
        level_update(dve, 2 * P)
        dve.drain()
        rope(dve, l, 0)
        for a in range(HEADS):
            if a == 2:
                rope(dve, l, 1)
            dve.wait_ge(av_mm.sem, av_mm.at(l, a + 1))
            dve.tensor_copy(ob[:, a, :], psH[:, 2 + a % 2, :]).then_inc(av_cp.sem, 1)
        attention_dve(dve, l)
        heads_inverse(dve, l)
        dve.wait_ge(n_rb.sem, n_rb.at(l, 1))
        split_dve(dve, l, T_DA, oa, oa, cur[:, L_DA:L_DA + HEADS], lambda k: psH[:, k, :],
                  lambda k: o_hi[:, k, :], lambda k: o_lo[:, k, :], HEADS)
        dve.wait_ge(n_rb.sem, n_rb.at(l, 2))
        for a in range(HEADS):
            dve.scalar_tensor_tensor(out=ob[:, a, :], in0=ob[:, a, :], scalar=cur[:, L_HG + a:L_HG + a + 1],
                                     in1=psH[:, a, :], op0=ALU.mult, op1=ALU.mult)
        dve.drain()
        dve.wait_ge(g_sig.sem, g_sig.at(l, 3))
        for a in range(HEADS):
            dve.tensor_tensor(ob[:, a, :], ob[:, a, :], sg[:, a, :], ALU.mult).then_inc(g_mul.sem, 1)
        for a in range(HEADS):
            dve.wait_ge(g_hi.sem, g_hi.at(l, a + 1))
            dve.tensor_tensor(o_lo[:, HEADS + a, :], ob[:, a, :], o_hi[:, HEADS + a, :].bitcast(F32),
                              ALU.subtract).then_inc(g_lo.sem, 1)
        dve.wait_ge(g_sig.sem, g_sig.at(l, 4))
        for u in range(2):
            for j in range(4):
                dve.wait_ge(tick.sem, T(um + U_WA, u, j // 2))
                t = 4 * u + j
                mm = dve.tensor_tensor(ga[:, t, :], ga[:, t, :], psG[:, j, :], ALU.mult)
                if j % 2:
                    mm.then_inc(psum_free[j // 2].sem, 1)
        for u in range(2):
            for j in range(4):
                dve.wait_ge(tick.sem, T(um + U_WB, u, j // 2))
                t = 4 * u + j
                mm = dve.tensor_tensor(gb[:, t, :], gb[:, t, :], psG[:, j, :], ALU.mult)
                if j % 2:
                    mm.then_inc(psum_free[j // 2].sem, 1)
            dve.drain()
            for t in range(4 * u, 4 * u + 4):
                dve.tensor_tensor(ga[:, t, :], ga[:, t, :], gb[:, t, :], ALU.add).then_inc(m_sum.sem, 1)
            for t in range(4 * u, 4 * u + 4):
                dve.wait_ge(m_hid.sem, m_hid.at(l, t + 1))
                dve.tensor_tensor(m_lo[:, t, :], ga[:, t, :], m_hi[:, t, :].bitcast(F32), ALU.subtract)\
                   .then_inc(m_lod.sem, 1)
        with dve.Fori(0, 2) as i:
            for s in range(2):
                for j in range(2):
                    dve.wait_ge(tick.sem, T(um + i + U_WO, s, j))
                    x = xT[:, ds(i * 4 + (2 * s + j), 1), :].rearrange("p a t -> p (a t)")
                    mm = dve.tensor_tensor(x, x, psG[:, 2 * s + j, :], ALU.add)
                mm.then_inc(psum_free[s].sem, 1)
                dve.drain().then_inc(x_done.sem, 2)
        rms_split_dve(dve, l, 1, T_FFN, cur[:, L_FFN:L_FFN + KD])
        with dve.Fori(0, FT // 2) as i:
            m = um + i + U_GU
            dve.drain()
            for j in range(2):
                dve.wait_ge(f_sig.sem, f_sig.at(l, 0) + i * 2 + (j + 1))
                mm = dve.tensor_tensor(ht[:, j, :], sgu[:, j, :], psG[:, j, :], ALU.mult)
            mm.then_inc(psum_free[0].sem, 1)
            dve.drain()
            for j in range(2):
                dve.wait_ge(tick.sem, T(m, 1, j))
                mm = dve.tensor_tensor(ht[:, j, :], ht[:, j, :], psG[:, 2 + j, :], ALU.mult)\
                        .then_inc(f_mul.sem, 1)
            dve.drain().then_inc(psum_free[1].sem, 1)
            for j in range(2):
                dve.wait_ge(f_hid.sem, f_hid.at(l, 0) + i * 2 + (j + 1))
                dve.tensor_tensor(hid_lo[:, ds(i * 2 + j, 1), :].rearrange("p a t -> p (a t)"), ht[:, j, :],
                                  hid_hi[:, ds(i * 2 + j, 1), :].bitcast(F32).rearrange("p a t -> p (a t)"),
                                  ALU.subtract).then_inc(f_lod.sem, 1)
        with dve.Fori(0, 2) as i:
            for c in range(2):
                for j in range(2):
                    u = 3 * c + 2
                    dve.wait_ge(tick.sem, T(um + i * 3 + (U_DN + u // 2), u % 2, j))
                    x = xT[:, ds(i * 4 + (2 * c + j), 1), :].rearrange("p a t -> p (a t)")
                    mm = dve.tensor_tensor(x, x, psG[:, 2 * c + j, :], ALU.add)
                mm.then_inc(psum_free[c].sem, 1)
                dve.drain().then_inc(x_done.sem, 2)

    UB, JB = DEPTH * U_LAYER, DEPTH * J_LAYER
    (V_Q, V_KV, V_U, V_G, V_WA, V_GLU, V_WS, V_WO, V_FA, V_DA, V_FB, V_DB) = (
        0, 2, 3, 5, (13, 15), 14, 16, 18, 22, 30, 38, 46)
    (K_WA, K_GLU, K_WS, K_WO, K_FA, K_DA, K_FB, K_DB) = (13, 17), 15, 19, 23, 27, 35, 39, 47

    def un(k):
        return step(UB, 0, k)

    def jn(k):
        return step(JB, 0, k)

    def Tn(k, half):
        return T(*un(k), half)

    def split_next(act, k):
        if k + 2 < 2 * U_SECOND:
            split_hi(act, *un(k + 2))

    ld2 = sem("ld2")
    t5_st = sem("t5_st")
    t5_ld = sem("t5_ld")
    toep_ld = sem("toep_ld")
    s2_pe, s2_act, s2_dve, s2_pool = sem("s2_pe"), sem("s2_act"), sem("s2_dve"), sem("s2_pool")
    q_ev, u_ev = sem("q_ev"), sem("u_ev")
    l_mm, l_lg, l_nm, l_ex, l_p = sem("l_mm"), sem("l_lg"), sem("l_nm"), sem("l_ex"), sem("l_p")
    l_tr, l_pt, l_av, l_ov = sem("l_tr"), sem("l_pt"), sem("l_av"), sem("l_ov")
    g2_sig = sem("g2_sig")
    u_tr, u_cp, e_ok = sem("u_tr"), sem("u_cp"), sem("e_ok")
    k_mm, k_cp = sem("k_mm"), sem("k_cp")
    win_tr, win_cp = sem("win_tr"), sem("win_cp")
    g_mm, g_rd, h_ok = sem("g_mm"), sem("g_rd"), sem("h_ok")
    y_mm, y_cp, z_tr = sem("y_mm"), sem("y_cp"), sem("z_tr")
    z_sq, z_in, z_sg, z_ok, z_hid, z_lod = (sem("z_sq"), sem("z_in"), sem("z_sg"), sem("z_ok"), sem("z_hid"),
                                            sem("z_lod"))
    glu_sg, zz_ok, zz_hid, zz_lod = sem("glu_sg"), sem("zz_ok"), sem("zz_hid"), sem("zz_lod")
    o2_hid, o2_lod = sem("o2_hid"), sem("o2_lod")
    m2_sum, m2_hid, m2_lod = sem("m2_sum"), sem("m2_hid"), sem("m2_lod")
    y_ok = sem("y_ok")
    x2_ok = sem("x2_ok")
    f2_r, f2_q, f2_hid, f2_lod = sem("f2_r"), sem("f2_q", credit=2), sem("f2_hid"), sem("f2_lod")
    o_tr, o_cp = sem("o_tr"), sem("o_cp")

    def second_sync(sp):
        w2 = io["w_in_2"][0].rearrange("(k p) c -> p k c", p=P)
        for s in range(2):
            w_src(*un(V_Q + s), w2[:, :, C2_Q + UC * s:C2_Q + UC * (s + 1)], sp)
        sp.wait_ge(x_done.sem, x_done.at(DEPTH, 0))
        with nc.allow_non_contiguous_dma(reason="small parameter layouts"):
            sp.dma_start(s_lam[0:16, :], io["lam_re_2"].rearrange("o (q g) p -> (o q) (g p)", g=2)).then_inc(ld2.sem, 16)
            sp.dma_start(s_lam[16:32, :], io["lam_im_2"].rearrange("o (q g) p -> (o q) (g p)", g=2)).then_inc(ld2.sem, 16)
            sp.dma_start(s_rows[:, :], io["log_dt_2"].rearrange("o (q g) -> (o q) g", g=2)).then_inc(ld2.sem, 16)
            for dst, name in ((b_re, "b_re_2"), (b_im, "b_im_2")):
                for g in range(2):
                    sp.dma_start(dst[NS * g:NS * g + NS, :, :], io[name][0].rearrange("(q g) p c -> g p q c", g=2)[g])\
                      .then_inc(ld2.sem, 16)
            for r, name in enumerate(("c_re_2", "c_im_2")):
                src = io[name].rearrange("o (t g) c p -> (o g c) t p", t=4)
                for dup in range(2):
                    sp.dma_start(c_tok[:, r, :, dup, :], src).then_inc(ld2.sem, 16)
            sp.dma_start(t5_rb[:, :], io["rel_bias_2"].rearrange("b h -> h b")).then_inc(ld2.sem, 16)
            sp.dma_start(sink[:, :], io["sinks_2"].rearrange("o h -> (o h)").partition_broadcast(P)).then_inc(ld2.sem, 16)
            dsk = io["d_skip_2"].rearrange("o (t q c) -> q c (o t)", q=4, c=GC)
            for q in range(4):
                sp.dma_start(d_col[32 * q:32 * q + GC, :], dsk[q]).then_inc(ld2.sem, 16)
        w_src(*un(V_KV), w2[:, :, C2_K:C2_U], sp)
        for s in range(2):
            w_src(*un(V_U + s), w2[:, :, C2_U + UC * s:C2_U + UC * (s + 1)], sp)
        sp.wait_ge(s2_pool.sem, 1)
        sp.dma_start(t5_dram, t5_rows[:, :]).then_inc(t5_st.sem, 16)
        sp.wait_ge(t5_st.sem, 16)
        with nc.allow_non_contiguous_dma(reason="overlapping rows"):
            sp.dma_start(t5_up[:, :, :], bass.AP(t5_dram.tensor, 0, [[1, P], [3 * P, QH], [1, 2 * P]]))\
              .then_inc(t5_ld.sem, 16)
        for k in range(8):
            w_src(*un(V_G + k), w2[:, :, C2_GA + UC * k:C2_GA + UC * (k + 1)], sp)
        wa = io["w_attn_branch_2"][0].rearrange("(g j d) c -> g d j c", g=KVH, d=HD)

        def w_attn(s):
            m, sl = un(V_WA[s])
            sp.wait_ge(lo_done.sem, m * 2 + sl + 1)
            dst = raw[:, sl, :].rearrange("p (k c) -> p k c", k=4)
            for g in range(KVH):
                sp.dma_start(dst[HD * g:HD * g + HD], wa[g, :, :, 512 * s:512 * s + 512]).then_inc(raw_in[sl].sem, 16)

        w_attn(0)
        w_src(*un(V_GLU), io["w_glu_2"][0].rearrange("(k p) c -> p k c", p=P), sp)
        sp.wait_ge(k_cp.sem, 1)
        for i in range(CT):
            for q in range(4):
                sp.dma_start(Toep[GC * i:GC * i + GC, :, :].rearrange("p (t q) c -> p q t c", q=4)[:, q],
                             k_pad[32 * q:32 * q + GC, :, P - GC * i:2 * P - GC * i]).then_inc(toep_ld.sem, 16)
        w_attn(1)
        for s in range(2):
            w_src(*un(V_WS + s), io["w_ssm_branch_2"][0].rearrange("(k p) c -> p k c", p=P)
                  [:, :, 512 * s:512 * s + 512], sp)
        wo = io["w_out_2"][0].rearrange("(k p) c -> p k c", p=P)
        for s in range(4):
            w_src(*un(V_WO + s), wo[:, :, UC * s:UC * s + UC], sp)
        for half, vf, vd in ((0, V_FA, V_DA), (1, V_FB, V_DB)):
            with sp.Fori(0, 4) as i:
                for s in range(2):
                    c = ds(i * 512 + (half * D_FF // 2 + UC * s), UC)
                    w_src(i + (UB + vf // 2), s, io["w_ff_in_2"][0, :, c].rearrange("(k p) c -> p k c", p=P), sp)
            with sp.Fori(0, 4) as i:
                for s in range(2):
                    r0 = (half * HT2 + KD * s) * P
                    w_src(i + (UB + vd // 2), s, io["w_ff_out_2"][0, r0:r0 + D, ds(i * UC, UC)]
                          .rearrange("(k p) c -> p k c", p=P), sp)
        out = io["out"].rearrange("a (t p) d -> p (a t) d", p=P)
        for t in range(TB):
            sp.wait_ge(o_cp.sem, TB + t + 1)
            sp.dma_start(out[:, t, :], x_out[:, t, :]).then_inc(st_out.sem, 16)
        sp.wait_ge(st_out.sem, 16 * TB)

    def second_pool(pool):
        pool.memset(exch[:, :], 0.0).then_inc(consts.sem, 1)
        pool.wait_ge(consts.sem, 7)
        pool.affine_select(out=exch[:, :], in_=exch[:, :], compare_op=ALU.not_equal, fill=1.0, base=-(P - 1),
                           pattern=[[1, P]], channel_multiplier=1).then_inc(consts.sem, 1)

    def tables_dve(dve):
        d, a = dve, s5
        DT, LR, LI, MAG, CO, SI, AR, AI, FR, FI, A, B, C = range(13)

        def tt(o, x, y, op):
            return d.tensor_tensor(o, x, y, op)

        d.wait_ge(ld2.sem, 16 * 17)
        d.memset(t5_rows[:, :], NEG)
        d.drain()
        lo = 0
        while lo < P:
            b = t5_bucket(lo)
            hi = lo
            while hi < P and t5_bucket(hi) == b:
                hi += 1
            dst = t5_rows[:, 2 * P - hi:2 * P - lo]
            d.tensor_copy(dst, t5_rb[:, b:b + 1].broadcast_to([QH, hi - lo]))
            lo = hi
        d.drain().then_inc(s2_pool.sem, 1)
        d.tensor_copy(s_log[:, 1, :], s_rows[:, 1:2].broadcast_to([16, NS]))
        d.tensor_copy(s_log[:, 0, :], s_rows[:, 0:1].broadcast_to([16, NS]))
        d.drain().then_inc(s2_dve.sem, 1)
        d.wait_ge(s2_pe.sem, 1)
        d.tensor_copy(a[:, 0:3, :].rearrange("p a q -> p (a q)"), psH[:, 0, 0:48])
        d.drain().then_inc(s2_dve.sem, 1)
        d.wait_ge(s2_act.sem, 1)
        tt(a[:, MAG], a[:, LR], a[:, DT], ALU.mult)
        tt(a[:, A], a[:, LI], a[:, DT], ALU.mult)
        d.drain()
        reduce_angle(d, a[:, CO], a[:, A], a[:, B], True)
        reduce_angle(d, a[:, SI], a[:, A], a[:, C], False)
        d.drain().then_inc(s2_dve.sem, 1)
        d.wait_ge(s2_act.sem, 2)
        tt(a[:, AR], a[:, MAG], a[:, CO], ALU.mult)
        tt(a[:, AI], a[:, MAG], a[:, SI], ALU.mult)
        tt(a[:, A], a[:, LR], a[:, LR], ALU.mult)
        tt(a[:, B], a[:, LI], a[:, LI], ALU.mult)
        d.drain()
        tt(a[:, A], a[:, A], a[:, B], ALU.add)
        d.tensor_scalar(a[:, C], a[:, AR], 1.0, None, ALU.subtract)
        d.drain()
        d.reciprocal(a[:, A], a[:, A])
        tt(a[:, FR], a[:, C], a[:, LR], ALU.mult)
        tt(a[:, B], a[:, AI], a[:, LI], ALU.mult)
        d.drain()
        tt(a[:, FR], a[:, FR], a[:, B], ALU.add)
        tt(a[:, FI], a[:, AI], a[:, LR], ALU.mult)
        tt(a[:, C], a[:, C], a[:, LI], ALU.mult)
        d.drain()
        tt(a[:, FI], a[:, FI], a[:, C], ALU.subtract)
        tt(a[:, FR], a[:, FR], a[:, A], ALU.mult)
        d.drain()
        tt(a[:, FI], a[:, FI], a[:, A], ALU.mult)
        d.drain()
        wide = [P, PAIRS, GC]
        fr = a[:, FR, :].unsqueeze(2).broadcast_to(wide)
        fi = a[:, FI, :].unsqueeze(2).broadcast_to(wide)
        t = wt_tmp[:, :, 0, :]
        tt(bb[:, 0], fr, b_re[:, :, :], ALU.mult)
        tt(t, fi, b_im[:, :, :], ALU.mult)
        tt(bb[:, 1], fr, b_im[:, :, :], ALU.mult)
        tt(wt_tmp[:, :, 1, :], fi, b_re[:, :, :], ALU.mult)
        d.drain()
        tt(bb[:, 0], bb[:, 0], t, ALU.subtract)
        tt(bb[:, 1], bb[:, 1], wt_tmp[:, :, 1, :], ALU.add)
        d.memset(pw[:, 0, :, 0:1], 1.0)
        d.memset(pw[:, 1, :, 0:1], 0.0)
        d.tensor_copy(pw[:, 0, :, 1], a[:, AR])
        d.tensor_copy(pw[:, 1, :, 1], a[:, AI])
        for n in (1, 2, 4):
            d.drain()
            w = [P, PAIRS, n]
            r0, i0 = pw[:, 0, :, n:n + 1].broadcast_to(w), pw[:, 1, :, n:n + 1].broadcast_to(w)
            r1, i1 = pw[:, 0, :, 1:n + 1], pw[:, 1, :, 1:n + 1]
            x, y = wt_tmp[:, :, 2, 0:n], wt_tmp[:, :, 3, 0:n]
            tt(pw[:, 0, :, n + 1:2 * n + 1], r0, r1, ALU.mult)
            tt(x, i0, i1, ALU.mult)
            tt(pw[:, 1, :, n + 1:2 * n + 1], r0, i1, ALU.mult)
            tt(y, i0, r1, ALU.mult)
            d.drain()
            tt(pw[:, 0, :, n + 1:2 * n + 1], pw[:, 0, :, n + 1:2 * n + 1], x, ALU.subtract)
            tt(pw[:, 1, :, n + 1:2 * n + 1], pw[:, 1, :, n + 1:2 * n + 1], y, ALU.add)
        d.drain()
        for i in range(CT):
            for r in range(2):
                d.tensor_copy(pr[:, r, :, i], pw[:, r, :, CT - 1 - i])
        for r in range(2):
            d.wait_ge(s2_pe.sem, 2 + r)
            for half in range(2):
                rows = slice(NS * half, NS * half + NS)
                src = psH[rows, 1 + r, :].rearrange("p (t g two c) -> p t g two c", t=4, two=2, c=GC)[:, :, :, half, :]
                dst = c_t[rows, r, :, :].rearrange("p (t g) c -> p t g c", t=4)
                d.tensor_copy(dst, src)
        for q in range(4):
            d.tensor_copy(eye16[32 * q:32 * q + GC, :], ident[32 * q:32 * q + GC, 32 * q:32 * q + GC])
        d.drain().then_inc(s2_dve.sem, 1)
        big = [P, PAIRS, CT + 1, GC]
        cr, ci = (c_t[:, r, :, :].unsqueeze(2).broadcast_to(big) for r in range(2))
        wr, wi = (pw[:, r, :, :].unsqueeze(3).broadcast_to(big) for r in range(2))
        tt(Wt[:, 0], cr, wr, ALU.mult)
        tt(wt_tmp[:, :, :, :], ci, wi, ALU.mult)
        d.drain()
        tt(Wt[:, 0], Wt[:, 0], wt_tmp[:, :, :, :], ALU.subtract)
        d.drain()
        tt(wt_tmp[:, :, :, :], cr, wi, ALU.mult)
        tt(Wt[:, 1], ci, wr, ALU.mult)
        d.drain()
        d.scalar_tensor_tensor(out=Wt[:, 1], in0=wt_tmp[:, :, :, :], scalar=-1.0, in1=Wt[:, 1], op0=ALU.mult,
                               op1=ALU.subtract)
        square_dve(d)

    def e_dve(dve):
        tt = dve.tensor_tensor
        big = [P, PAIRS, CT, GC]
        br, bi = (bb[:, r, :, :].unsqueeze(2).broadcast_to(big) for r in range(2))
        wr, wi = (pr[:, r, :, :].unsqueeze(3).broadcast_to(big) for r in range(2))
        tt(Et[:, 0], br, wr, ALU.mult)
        tt(e_tmp[:, :, :, :], bi, wi, ALU.mult)
        dve.drain()
        tt(Et[:, 0], Et[:, 0], e_tmp[:, :, :, :], ALU.subtract)
        dve.drain()
        tt(e_tmp[:, :, :, :], br, wi, ALU.mult)
        tt(Et[:, 1], bi, wr, ALU.mult)
        dve.drain()
        tt(Et[:, 1], Et[:, 1], e_tmp[:, :, :, :], ALU.add)
        dve.drain().then_inc(e_ok.sem, 1)

    def square_dve(dve):
        tt, a = dve.tensor_tensor, s5
        MAG, CO, SI, A, B, C = 3, 4, 5, 10, 11, 12
        for _ in range(3):
            tt(a[:, A], a[:, CO], a[:, CO], ALU.mult)
            tt(a[:, B], a[:, SI], a[:, SI], ALU.mult)
            tt(a[:, C], a[:, CO], a[:, SI], ALU.mult)
            tt(a[:, MAG], a[:, MAG], a[:, MAG], ALU.mult)
            dve.drain()
            tt(a[:, CO], a[:, A], a[:, B], ALU.subtract)
            dve.tensor_scalar(a[:, SI], a[:, C], 2.0, None, ALU.mult)
            dve.drain()

    def rot_dve(dve):
        tt, a = dve.tensor_tensor, s5
        MAG, CO, SI = 3, 4, 5
        dve.memset(rot[:, 0, :, 0:1], 1.0)
        dve.memset(rot[:, 1, :, 0:1], 0.0)
        dve.tensor_copy(rot[:, 0, :, 1], a[:, CO])
        dve.tensor_copy(rot[:, 1, :, 1], a[:, SI])
        dve.tensor_copy(d0[:, :, :], a[:, MAG, :].unsqueeze(2).broadcast_to([P, PAIRS, CH]))
        dve.drain()
        dve.memset(d0[:, :, 0:1], 0.0)
        for n in (1, 2, 4, 8, 16, 32):
            m = min(n, CH - 1 - n)
            w = [P, PAIRS, m]
            r0, i0 = rot[:, 0, :, n:n + 1].broadcast_to(w), rot[:, 1, :, n:n + 1].broadcast_to(w)
            r1, i1 = rot[:, 0, :, 1:m + 1], rot[:, 1, :, 1:m + 1]
            x, y = rot_tmp[:, 0, :, 0:m], rot_tmp[:, 1, :, 0:m]
            ro, io_ = rot[:, 0, :, n + 1:n + m + 1], rot[:, 1, :, n + 1:n + m + 1]
            tt(ro, r0, r1, ALU.mult)
            tt(x, i0, i1, ALU.mult)
            tt(io_, r0, i1, ALU.mult)
            tt(y, i0, r1, ALU.mult)
            dve.drain()
            tt(ro, ro, x, ALU.subtract)
            tt(io_, io_, y, ALU.add)
            dve.drain()

    def second_pe(pe):
        pe.wait_ge(consts.sem, 8)
        for p in range(4):
            sum_pair(pe, DEPTH, 1, p)

        def first_tile(k):
            pe.wait_ge(n_lo.sem, n_lo.at(DEPTH, k + 1))

        for k in range(2):
            pe_feature(pe, *un(V_Q + k), *jn(V_Q + k), h_hi, h_lo, first_tile if k == 0 else None)
        m, s = un(V_KV)
        jm, b = jn(V_KV)
        unit_ready(pe, m, s)
        bank_ready(pe, jm, b)
        wh = w_hi[:, s, :].rearrange("p (k c) -> p k c", k=KD)
        wl = w_lo[:, s, :].rearrange("p (k c) -> p k c", k=KD)
        for k in range(KD):
            mm = triple(pe, psG[:, 2 * b, :], wh[:, k, 0:P], wl[:, k, 0:P], h_hi[:, k, :], h_lo[:, k, :],
                        k == 0, k == KD - 1)
        mm.then_inc(tick.sem, 1)
        for t in range(TB):
            c = slice(t * P, (t + 1) * P)
            for k in range(KD):
                mm = triple(pe, psG[:, 2 * b + 1, c], h_hi[:, k, c], h_lo[:, k, c], wh[:, k, P:2 * P],
                            wl[:, k, P:2 * P], k == 0, k == KD - 1)
        mm.then_inc(tick.sem, 1)
        pe.wait_ge(s2_dve.sem, 1)
        pe.transpose(psH[:, 0, 0:16], s_log[:, :, :].rearrange("q g p -> q (g p)"), ident[0:16, 0:16])
        pe.transpose(psH[:, 0, 16:48], s_lam[:, :], ident[0:32, 0:32]).then_inc(s2_pe.sem, 1)
        for r in range(2):
            for t in range(4):
                mm = pe.transpose(psH[:, 1 + r, t * P:(t + 1) * P],
                                  c_tok[:, r, t, :, :].rearrange("p a b -> p (a b)"), ident[:, :])
            mm.then_inc(s2_pe.sem, 1)
        for v in range(2):
            m, s = un(V_U + v)
            jm, b = jn(V_U + v)
            unit_ready(pe, m, s)
            bank_ready(pe, jm, b)
            wh = w_hi[:, s, :].rearrange("p (k c) -> p k c", k=KD)
            wl = w_lo[:, s, :].rearrange("p (k c) -> p k c", k=KD)
            for t in range(4):
                for k in range(KD):
                    cut = "p (m i) -> p i m"
                    hh = h_hi[:, k, :].rearrange(cut, i=4)[:, t]
                    hl = h_lo[:, k, :].rearrange(cut, i=4)[:, t]
                    out = psG[:, 2 * b + t // 2, (t % 2) * UC:(t % 2 + 1) * UC]
                    mm = triple(pe, out, hh, hl, wh[:, k, :], wl[:, k, :], k == 0, k == KD - 1)
                if t % 2:
                    mm.then_inc(tick.sem, 1)
        pe.wait_ge(t5_ld.sem, 16)
        pe.wait_ge(s2_dve.sem, 4)
        for n in range(4):
            mm = pe.matmul(psH[:, n, :], exch[:, :], t5_up[:, 2 * n:2 * n + 2, :].rearrange("p a b -> p (a b)"),
                           start=True, stop=True)
        mm.then_inc(s2_pe.sem, 1)
        pe.wait_ge(s2_act.sem, 3)
        pe.wait_ge(u_ev.sem, 2)
        for q in range(PAIRS):
            mm = pe.transpose(psH[:, q // 4, q % 4 * P:(q % 4 + 1) * P],
                              uc[:, 2 * q:2 * q + 2, :, :].rearrange("p g i c -> p (g i c)"), ident[:, :])
        mm.then_inc(u_tr.sem, 1)
        pe.wait_ge(u_cp.sem, 1)
        pe.wait_ge(q_ev.sem, 3)
        for n in range(9):
            if n < 8:
                blk_n, g = n // 2, n % 2
                rows = slice(HD * g, HD * g + HD)
                k0 = max(blk_n - 1, 0) * P
                w = (blk_n + 1) * P - k0
                if n:
                    pe.wait_ge(l_lg.sem, n)
                for j in range(4):
                    mm = pe.matmul(psH[:, j // 2, (j % 2) * 256:(j % 2) * 256 + w], q2[rows, j, blk_n * P:(blk_n + 1) * P],
                                   k2[rows, k0:k0 + w], start=True, stop=True)
                mm.then_inc(l_mm.sem, 1)
            if n < 8:
                pe_feature(pe, *un(V_G + n), *jn(V_G + n), h_hi, h_lo, tiles=(0,))
            if n:
                o = n - 1
                blk_n, g = o // 2, o % 2
                pe.wait_ge(l_pt.sem, n)
                parts = [blk_n - 1, blk_n] if blk_n else [0]
                for i, kb in enumerate(parts):
                    mm = pe.matmul(psH[HD * g:HD * g + HD, 2, :], v2[:, kb, HD * g:HD * g + HD], pT[:, i, :],
                                   start=i == 0, stop=i == len(parts) - 1)
                mm.then_inc(l_av.sem, 1)
            if n < 8:
                pe_feature(pe, *un(V_G + n), *jn(V_G + n), h_hi, h_lo, tiles=(1,))
                pe.wait_ge(l_p.sem, n + 1)
                if n:
                    pe.wait_ge(l_ov.sem, n)
                for i in range(2 if n // 2 else 1):
                    for j in range(4):
                        mm = pe.transpose(psH[:, 2 + i, j * P:(j + 1) * P], lg[:, j, i * P:(i + 1) * P], ident[:, :])
                mm.then_inc(l_tr.sem, 1)
        for g in range(GROUPS):
            q, rows = g // 2, slice(NS * (g % 2), NS * (g % 2) + NS)
            for r in range(2):
                mm = pe.matmul(psH[32 * (g % 4):32 * (g % 4) + GC, g // 16, (g // 4 % 4) * P:(g // 4 % 4 + 1) * P],
                               bb[rows, r, q, :], Wt[rows, r, q, 0:CT, :].rearrange("p n c -> p (n c)"),
                               start=r == 0, stop=r == 1)
        mm.then_inc(k_mm.sem, 1)
        pe.wait_ge(e_ok.sem, 1)
        pe.wait_ge(l_ov.sem, 8)
        for n in range(4):
            if n == 1:
                pe.wait_ge(k_cp.sem, 1)
            if n >= 2:
                pe.wait_ge(win_cp.sem, n - 1)
            for i in range(8):
                r, q = divmod(n * 8 + i, PAIRS)
                b = 2 - 2 * (n % 2) + i // 4
                mm = pe.transpose(psH[:, b, (i % 4) * P:(i % 4 + 1) * P], Et[:, r, q, :, :].rearrange("p i c -> p (i c)"),
                                  ident[:, :])
            mm.then_inc(win_tr.sem, 1)
        pe.wait_ge(win_cp.sem, 4)
        for r in range(2):
            for q in range(PAIRS):
                for half in range(2):
                    rows = slice(NS * half, NS * half + NS)
                    mm = pe.matmul(psH[rows, 2 * r + q // 8, (q % 8) * CH:(q % 8 + 1) * CH], Win[:, r, q, rows],
                                   U[:, 2 * q + half, :], start=True, stop=True)
        mm.then_inc(g_mm.sem, 1)
        pe.wait_ge(o2_lod.sem, 4)
        pe_branch2(pe, V_WA[0], K_WA[0], o2_hi, o2_lo)
        pe.wait_ge(toep_ld.sem, 16 * 32)
        pe.wait_ge(g_rd.sem, 1)
        for n in range(2):
            if n:
                pe.wait_ge(y_cp.sem, 4)

            def y_bank(i):
                return psH[0:CH, 2 * (i % 2) + i // 8, i // 2 % 4 * P:(i // 2 % 4 + 1) * P]

            for i in range(16):
                pe.matmul(y_bank(i), U[:, 16 * n + i, :], Toep[:, 16 * n + i, :], start=i % 8 < 2, stop=False)
            if n == 0:
                pe.wait_ge(h_ok.sem, 1)
            for i in range(16):
                g = 16 * n + i
                q, rows = g // 2, slice(NS * (g % 2), NS * (g % 2) + NS)
                pe.matmul(y_bank(i), hre[rows, q, :], Wt[rows, 0, q, 1:CT + 1, :].rearrange("p n c -> p (n c)"),
                          start=False, stop=False)
                mm = pe.matmul(y_bank(i), him[rows, q, :], Wt[rows, 1, q, 1:CT + 1, :].rearrange("p n c -> p (n c)"),
                               start=False, stop=i % 8 >= 6)
                if i % 8 >= 6:
                    mm.then_inc(y_mm.sem, 1)
        pe.wait_ge(y_cp.sem, 8)
        for f in range(4):
            for j in range(CT):
                mm = pe.transpose(psH[:, f, j * CH:(j + 1) * CH], yt[:, j, f * P:(f + 1) * P], ident[0:CH, 0:CH])
            mm.then_inc(z_tr.sem, 1)

        def gelu_tile(k):
            pe.wait_ge(z_lod.sem, k + 1)

        pe_branch2(pe, V_GLU, K_GLU, z_hi, z_lo, gelu_tile)
        pe_branch2(pe, V_WA[1], K_WA[1], o2_hi, o2_lo)
        pe.wait_ge(zz_lod.sem, 4)
        for k in range(2):
            pe_branch2(pe, V_WS + k, K_WS + 2 * k, zz_hi, zz_lo)

        def merged_tile(k):
            pe.wait_ge(m2_lod.sem, k + 1)

        for k in range(4):
            pe_feature(pe, *un(V_WO + k), *jn(K_WO + k), m2_hi, m2_lo, merged_tile if k == 0 else None)
            if k:
                sum_pair(pe, DEPTH, 2, k - 1)
        sum_pair(pe, DEPTH, 2, 3)
        for p in range(4):
            sum_pair(pe, DEPTH, 3, p)

        def mlp_tile(k):
            pe.wait_ge(n_lo.sem, n_lo.at(DEPTH, KD + k + 1))

        for half, vf, kf, vd, kd in ((0, V_FA, K_FA, V_DA, K_DA), (1, V_FB, K_FB, V_DB, K_DB)):
            with pe.Fori(0, 4) as i:
                for s in range(2):
                    jm, b = step(JB + kf // 2, kf % 2, s)
                    pe_feature(pe, i + (UB + vf // 2), s, i + jm, b, h_hi, h_lo,
                               mlp_tile if half == 0 and s == 0 else None)
            for c in range(4):
                jm, b = jn(kd + c)
                bank_ready(pe, jm, b)
                for v in range(2):
                    m, s = un(vd + 2 * c + v)

                    def hidden_tile(k, v=v, half=half):
                        pe.wait_ge(f2_lod.sem, HT2 * half + KD * v + k + 1)

                    pe_part(pe, m, s, b, hid2_hi, hid2_lo, KD * v, KD, v == 0, v == 1,
                            hidden_tile if c == 0 else None)
                    if half and c and v == 0:
                        sum_pair(pe, DEPTH, 4, c - 1)
        sum_pair(pe, DEPTH, 4, 3)
        for h in range(2):
            for k in range(4):
                pe.wait_ge(x2_ok.sem, 2 * KD + 4 * h + k + 1)
                for t in range(TB):
                    if h and k == 0:
                        pe.wait_ge(o_cp.sem, t + 1)
                    mm = pe.transpose(psH[:, t, k * P:(k + 1) * P], xT[:, 4 * h + k, t * P:(t + 1) * P],
                                      ident[:, :])
                    if k == 3:
                        mm.then_inc(o_tr.sem, 1)

    def pe_branch2(pe, k, j, x_hi, x_lo, k_wait=None):
        m, s = un(k)
        unit_ready(pe, m, s)
        wh = w_hi[:, s, :].rearrange("p (k c) -> p k c", k=4)
        wl = w_lo[:, s, :].rearrange("p (k c) -> p k c", k=4)
        nt = 4
        for t in range(nt):
            jm, b = jn(j + t // 2)
            if t % 2 == 0:
                bank_ready(pe, jm, b)
            for kk in range(4):
                if k_wait is not None and t == 0:
                    k_wait(kk)
                c = slice(t * P, (t + 1) * P)
                mm = triple(pe, psG[:, 2 * b + t % 2, :], wh[:, kk, c], wl[:, kk, c], x_hi[:, kk, :], x_lo[:, kk, :],
                            kk == 0, kk == 3)
            if t % 2:
                mm.then_inc(tick.sem, 1)

    def bank2(j, t):
        return 2 * jn(j + t // 2)[1] + t % 2

    def attention_out(act, n):
        act.wait_ge(l_av.sem, n + 1)
        rows = slice(HD * (n % 2), HD * (n % 2) + HD)
        act.copy(q2[rows, :, (n // 2) * P:(n // 2 + 1) * P],
                 psH[rows, 2, :].rearrange("p (j q) -> p j q", j=4)).then_inc(l_ov.sem, 1)

    def second_act(act):
        rms_act(act, DEPTH, 0)
        for p in range(4):
            act.wait_ge(x2_ok.sem, 2 * p + 2)
            square_pair(act, DEPTH, 1, p, xT)
        rms_act(act, DEPTH, 1)
        split_act(act, DEPTH, 0, h_tmp, h_hi_t, KD)
        for k in range(2):
            split_next(act, V_Q + k)
            b = jn(k)[1]
            for j in range(2):
                act.wait_ge(tick.sem, Tn(k, j))
                for i in range(2):
                    mm = act.copy(q2[HD * k:HD * k + HD, 2 * j + i, :], psG[HD * i:HD * i + HD, 2 * b + j, :])
            mm.then_inc(psum_free[b].sem, 1)
            act.drain().then_inc(q_ev.sem, 1)
        split_next(act, V_KV)
        b = jn(V_KV)[1]
        act.wait_ge(tick.sem, Tn(V_KV, 0))
        act.copy(k2[:, :], psG[:, 2 * b, :])
        act.wait_ge(tick.sem, Tn(V_KV, 1))
        act.copy(v2[:, :, :].rearrange("p t c -> p (t c)"), psG[:, 2 * b + 1, :]).then_inc(psum_free[b].sem, 1)
        act.drain().then_inc(q_ev.sem, 1)
        act.wait_ge(s2_dve.sem, 2)
        act.activation(s5[:, 0, :], s5[:, 0, :], ACT.Exp).then_inc(s2_act.sem, 1)
        act.wait_ge(s2_dve.sem, 3)
        act.activation(s5[:, 3, :], s5[:, 3, :], ACT.Exp)
        act.activation(s5[:, 4, :], s5[:, 4, :], ACT.Sin)
        act.activation(s5[:, 5, :], s5[:, 5, :], ACT.Sin)
        act.drain().then_inc(s2_act.sem, 1)
        split_next(act, V_U)
        act.wait_ge(s2_dve.sem, 4)
        act.wait_ge(s2_pe.sem, 4)
        for n in range(4):
            mm = act.copy(bias[:, 2 * n:2 * n + 2, :].rearrange("p a b -> p (a b)"), psH[:, n, :])
        mm.then_inc(s2_act.sem, 1)
        for v in range(2):
            if v:
                split_next(act, V_U + 1)
            b = jn(V_U + v)[1]
            act.wait_ge(tick.sem, Tn(V_U + v, 1))
            act.copy(uc[:, 16 * v:16 * v + 16, :, :].rearrange("p g t c -> p t g c"),
                     psG[:, 2 * b:2 * b + 2, :].rearrange("p b (t g c) -> p (b t) g c", t=2, c=GC))\
               .then_inc(psum_free[b].sem, 1)
            act.drain().then_inc(u_ev.sem, 1)
        act.wait_ge(u_tr.sem, 1)
        for h in range(2):
            for g in range(2):
                mm = act.copy(U[CH * h:CH * h + CH, :, :].rearrange("p (q g) c -> p g q c", g=2)[:, g],
                              psH[CH * g:CH * g + CH, :, :].rearrange("p a (q c h) -> p h (a q) c", h=2, c=CH)[:, h])
        mm.then_inc(u_cp.sem, 1)
        for n in range(8):
            act.wait_ge(l_nm.sem, n + 1)
            act.activation(lg_w(n), lg_w(n), ACT.Exp)
            act.activation(st2[:, 2, :], st2[:, 1, :], ACT.Exp).then_inc(l_ex.sem, 1)
            b = jn(V_G + n)[1]

            def gate_tile(j):
                act.wait_ge(tick.sem, Tn(V_G + n, j))
                t = 2 * n + j
                return act.activation((g2a, g2b)[t // KD][:, t % KD, :], psG[:, 2 * b + j, :], ACT.Sigmoid)

            gate_tile(0)
            if n:
                attention_out(act, n - 1)
            split_next(act, V_G + n)
            gate_tile(1).then_inc(psum_free[b].sem, 1)
            act.wait_ge(l_tr.sem, n + 1)
            w = 2 if n // 2 else 1
            act.copy(pT[:, 0:w, :], psH[:, 2:2 + w, :]).then_inc(l_pt.sem, 1)
        attention_out(act, 7)
        act.drain().then_inc(g2_sig.sem, 1)
        for n in range(4):
            act.wait_ge(win_tr.sem, n + 1)
            b = 2 - 2 * (n % 2)
            r, q = divmod(n * 8, PAIRS)
            act.copy(Win[:, r, q:q + 8, :].rearrange("p q c -> p (q c)"),
                     psH[:, b:b + 2, :].rearrange("p a b -> p (a b)")).then_inc(win_cp.sem, 1)
        act.wait_ge(g_mm.sem, 1)
        for f in range(4):
            act.copy(o2_hi[:, f, :], q2[:, f, :]).then_inc(o2_hid.sem, 1)
        split_next(act, V_WA[0])
        for n in range(8):
            act.wait_ge(y_mm.sem, n + 1)
            act.copy(yt[:, :, n // 2 * P:(n // 2 + 1) * P].rearrange("c j (g two o) -> c two g j o", g=4, two=2)[:, n % 2],
                     psH[0:CH, 2 * (n % 2) + n // 2 % 2, :].rearrange("c (g j o) -> c g j o", g=4, j=CT))\
               .then_inc(y_cp.sem, 1)
        for f in range(4):
            act.wait_ge(z_tr.sem, f + 1)
            src = psH[:, f, :].rearrange("p (j c) -> p c j", j=CT)
            act.copy(z2[:, f, :].rearrange("p (c j) -> p c j", j=CT), src)
        for f in range(4):
            src = psH[:, f, :].rearrange("p (j c) -> p c j", j=CT)
            act.activation(z_w[:, 0, f, :].rearrange("p (c j) -> p c j", j=CT), src, ACT.Square).then_inc(z_sq.sem, 1)
        for f in range(5):
            if f < 4:
                act.wait_ge(z_in.sem, f + 1)
                act.activation(z_w[:, 1, f, :], z_w[:, 0, f, :], ACT.Sigmoid, scale=GELU).then_inc(z_sg.sem, 1)
            if f:
                act.wait_ge(z_ok.sem, f)
                act.copy(z_hi[:, f - 1, :], z2[:, f - 1, :]).then_inc(z_hid.sem, 1)
        split_next(act, V_GLU)
        for t in range(4):
            act.wait_ge(tick.sem, Tn(V_GLU, t // 2))
            mm = act.activation(z_w[:, 0, t, :], psG[:, bank2(K_GLU, t), :], ACT.Sigmoid)
            if t % 2:
                mm.then_inc(psum_free[jn(K_GLU + t // 2)[1]].sem, 1)
                act.drain().then_inc(glu_sg.sem, 1)
        for f in range(4):
            act.wait_ge(zz_ok.sem, f + 1)
            act.copy(zz_hi[:, f, :], z2[:, f, :]).then_inc(zz_hid.sem, 1)
        split_next(act, V_WA[1])
        for k in range(2):
            split_next(act, V_WS + k)
            for t in range(4 * k, 4 * k + 4):
                act.wait_ge(m2_sum.sem, t + 1)
                act.copy(m2_hi[:, t, :], g2a[:, t, :]).then_inc(m2_hid.sem, 1)
        for k in range(4):
            if k:
                act.wait_ge(y_ok.sem, k)
                square_pair(act, DEPTH, 2, k - 1, y2)
            split_next(act, V_WO + k)
        act.wait_ge(y_ok.sem, 4)
        square_pair(act, DEPTH, 2, 3, y2)
        rms_act(act, DEPTH, 2)
        for p in range(4):
            act.wait_ge(x2_ok.sem, KD + 2 * p + 2)
            square_pair(act, DEPTH, 3, p, xT)
        rms_act(act, DEPTH, 3)
        split_act(act, DEPTH, KD, h_tmp, h_hi_t, KD)
        for half, vf, kf in ((0, V_FA, K_FA), (1, V_FB, K_FB)):
            with act.Fori(0, 4) as i:
                for s in range(2):
                    m = i + (UB + vf // 2)
                    split_hi(act, m + 1, s)
                    b = step(0, kf % 2, s)[1]
                    for j in range(2):
                        t = 2 * s + j
                        act.wait_ge(f2_q.sem, i * 4 + (16 * half + t - 1 + f2_q.credit))
                        act.wait_ge(tick.sem, T(m, s, j))
                        mm = act.activation(r2[:, j, :], psG[:, 2 * b + j, :], ACT.Relu).then_inc(f2_r.sem, 1)
                    act.drain().then_inc(psum_free[b].sem, 1)
                    for j in range(2):
                        t = 2 * s + j
                        act.wait_ge(f2_q.sem, i * 4 + (16 * half + t + 1 + f2_q.credit))
                        act.copy(hid2_hi[:, ds(i * 4 + t, 1), :].rearrange("p a t -> p (a t)"), hq2[:, j, :])\
                           .then_inc(f2_hid.sem, 1)
            for k in range(8):
                if half and k % 2 == 0 and k:
                    act.wait_ge(y_ok.sem, k // 2 + 4)
                    square_pair(act, DEPTH, 4, k // 2 - 1, y2)
                split_next(act, (V_DA, V_DB)[half] + k)
        act.wait_ge(y_ok.sem, 8)
        square_pair(act, DEPTH, 4, 3, y2)
        rms_act(act, DEPTH, 4)

    def lg_w(n):
        return lg[:, :, 0:(2 * P if n // 2 else P)]

    def second_dve(dve):
        inverse_rms(dve, DEPTH, 0)
        for k in range(KD):
            dve.scalar_tensor_tensor(out=xT[:, k, :], in0=xT[:, k, :], scalar=par[:, R_FINAL + k:R_FINAL + k + 1],
                                     in1=rms[:, :], op0=ALU.mult, op1=ALU.mult).then_inc(x2_ok.sem, 1)
        rms_split_dve(dve, DEPTH, 1, 0, par[:, R_PRE2:R_PRE2 + KD])
        tables_dve(dve)
        dve.wait_ge(u_tr.sem, 1)
        e_dve(dve)
        dve.wait_ge(s2_act.sem, 3)
        for n in range(8):
            blk_n, g = n // 2, n % 2
            w = 2 * P if blk_n else P
            bs = bias[:, 4 * g:4 * g + 4, 2 * P - w:2 * P]
            dve.wait_ge(l_mm.sem, n + 1)
            if n:
                dve.wait_ge(l_tr.sem, n)
            ps = psH[:, 0:2, :].rearrange("p b (j k) -> p (b j) k", j=2)[:, :, 0:w]
            dve.scalar_tensor_tensor(out=lg_w(n), in0=ps, scalar=HD ** -0.5, in1=bs, op0=ALU.mult, op1=ALU.add)\
               .then_inc(l_lg.sem, 1)
            dve.drain()
            dve.tensor_reduce(st2[:, 0, :], lg_w(n), AX.X, ALU.max)
            dve.drain()
            dve.tensor_tensor(st2[:, 0, :], st2[:, 0, :], sink[:, 4 * g:4 * g + 4], ALU.max)
            dve.drain()
            dve.tensor_tensor(st2[:, 1, :], sink[:, 4 * g:4 * g + 4], st2[:, 0, :], ALU.subtract)
            dve.tensor_tensor(lg_w(n), lg_w(n), st2[:, 0, :].unsqueeze(2).broadcast_to([P, 4, w]), ALU.subtract)\
               .then_inc(l_nm.sem, 1)
            dve.wait_ge(l_ex.sem, n + 1)
            dve.tensor_reduce(st2[:, 3, :], lg_w(n), AX.X, ALU.add)
            dve.drain()
            dve.tensor_tensor(st2[:, 3, :], st2[:, 3, :], st2[:, 2, :], ALU.add)
            dve.drain()
            dve.reciprocal(st2[:, 4, :], st2[:, 3, :])
            dve.drain()
            dve.tensor_tensor(lg_w(n), lg_w(n), st2[:, 4, :].unsqueeze(2).broadcast_to([P, 4, w]), ALU.mult)\
               .then_inc(l_p.sem, 1)
        dve.wait_ge(l_ov.sem, 8)
        dve.memset(k_pad[:, :, 0:P], 0.0)
        dve.wait_ge(k_mm.sem, 1)
        for q in range(4):
            rows = slice(32 * q, 32 * q + GC)
            dve.tensor_copy(k_pad[rows, :, P:2 * P], psH[rows, 0:2, :].rearrange("p a (t c) -> p (a t) c", c=P))
            dve.tensor_tensor(s_eye[rows, :, :], eye16[rows, :].unsqueeze(1).broadcast_to([GC, CT, GC]),
                              d_col[rows, :].unsqueeze(2).broadcast_to([GC, CT, GC]), ALU.mult)
        dve.drain()
        for q in range(4):
            rows = slice(32 * q, 32 * q + GC)
            dve.tensor_tensor(k_pad[rows, :, P:P + GC], k_pad[rows, :, P:P + GC], s_eye[rows, :, :], ALU.add)
        dve.drain().then_inc(k_cp.sem, 1)
        rot_dve(dve)
        tt = dve.tensor_tensor
        for f in range(4):
            dve.wait_ge(o2_hid.sem, f + 1)
            tt(o2_lo[:, f, :], q2[:, f, :], o2_hi[:, f, :].bitcast(F32), ALU.subtract).then_inc(o2_lod.sem, 1)
        dve.wait_ge(g_mm.sem, 1)
        dve.drain()
        gr = psH[:, 0:2, :].rearrange("p a (q c) -> p (a q) c", c=CH)[:, :, 0:CH - 1]
        gi = psH[:, 2:4, :].rearrange("p a (q c) -> p (a q) c", c=CH)[:, :, 0:CH - 1]
        rc, rs = rot[:, 0, :, 1:CH], rot[:, 1, :, 1:CH]
        dve.memset(hre[:, :, 0:1], 0.0)
        dve.memset(him[:, :, 0:1], 0.0)
        tt(hre[:, :, 1:CH], rc, gr, ALU.mult)
        tt(him[:, :, 1:CH], rc, gi, ALU.mult)
        tt(s_tmp[:, 0, :, 1:CH], rs, gi, ALU.mult)
        tt(s_tmp[:, 1, :, 1:CH], rs, gr, ALU.mult).then_inc(g_rd.sem, 1)
        dve.drain()
        tt(hre[:, :, 1:CH], hre[:, :, 1:CH], s_tmp[:, 0, :, 1:CH], ALU.add)
        tt(him[:, :, 1:CH], him[:, :, 1:CH], s_tmp[:, 1, :, 1:CH], ALU.subtract)
        dve.drain()
        flat = "p q c -> p (q c)"
        for r, x in enumerate((hre, him)):
            dve.tensor_tensor_scan(s_tmp[:, r].rearrange(flat), d0[:, :, :].rearrange(flat),
                                   x[:, :, :].rearrange(flat), 0.0, ALU.mult, ALU.add)
        dve.drain()
        tt(hre[:, :, :], rot[:, 0], s_tmp[:, 0], ALU.mult)
        tt(s_tmp[:, 2], rot[:, 1], s_tmp[:, 1], ALU.mult)
        tt(him[:, :, :], rot[:, 1], s_tmp[:, 0], ALU.mult)
        dve.drain()
        tt(hre[:, :, :], hre[:, :, :], s_tmp[:, 2], ALU.subtract)
        tt(s_tmp[:, 1], rot[:, 0], s_tmp[:, 1], ALU.mult)
        dve.drain()
        tt(him[:, :, :], him[:, :, :], s_tmp[:, 1], ALU.add).then_inc(h_ok.sem, 1)

        def gated(gate, u, k, v):
            for j in range(4):
                t = 4 * u + j
                dve.wait_ge(tick.sem, Tn(v, j // 2))
                mm = tt(gate[:, t, :], gate[:, t, :], psG[:, bank2(k, j), :], ALU.mult)
                if j % 2:
                    mm.then_inc(psum_free[jn(k + j // 2)[1]].sem, 1)

        dve.wait_ge(g2_sig.sem, 1)
        gated(g2a, 0, K_WA[0], V_WA[0])
        for f in range(4):
            dve.wait_ge(z_sq.sem, f + 1)
            dve.tensor_scalar(z_w[:, 0, f, :], z_w[:, 0, f, :], 0.044715, 1.0, ALU.mult, ALU.add)
            dve.drain()
            tt(z_w[:, 0, f, :], z_w[:, 0, f, :], z2[:, f, :], ALU.mult).then_inc(z_in.sem, 1)
        for f in range(5):
            if f < 4:
                dve.wait_ge(z_sg.sem, f + 1)
                tt(z2[:, f, :], z2[:, f, :], z_w[:, 1, f, :], ALU.mult).then_inc(z_ok.sem, 1)
            if f:
                dve.wait_ge(z_hid.sem, f)
                tt(z_lo[:, f - 1, :], z2[:, f - 1, :], z_hi[:, f - 1, :].bitcast(F32), ALU.subtract)\
                    .then_inc(z_lod.sem, 1)
        for f in range(4):
            dve.wait_ge(glu_sg.sem, f // 2 + 1)
            tt(z2[:, f, :], z2[:, f, :], z_w[:, 0, f, :], ALU.mult).then_inc(zz_ok.sem, 1)
        for f in range(4):
            dve.wait_ge(zz_hid.sem, f + 1)
            tt(zz_lo[:, f, :], z2[:, f, :], zz_hi[:, f, :].bitcast(F32), ALU.subtract).then_inc(zz_lod.sem, 1)
        gated(g2a, 1, K_WA[1], V_WA[1])
        for u in range(2):
            gated(g2b, u, K_WS + 2 * u, V_WS + u)
            dve.drain()
            for t in range(4 * u, 4 * u + 4):
                tt(g2a[:, t, :], g2a[:, t, :], g2b[:, t, :], ALU.add).then_inc(m2_sum.sem, 1)
            for t in range(4 * u, 4 * u + 4):
                dve.wait_ge(m2_hid.sem, t + 1)
                tt(m2_lo[:, t, :], g2a[:, t, :], m2_hi[:, t, :].bitcast(F32), ALU.subtract).then_inc(m2_lod.sem, 1)
        for k in range(4):
            b = jn(K_WO + k)[1]
            for j in range(2):
                dve.wait_ge(tick.sem, Tn(V_WO + k, j))
                mm = dve.tensor_copy(y2[:, 2 * k + j, :], psG[:, 2 * b + j, :])
            mm.then_inc(psum_free[b].sem, 1)
            dve.drain().then_inc(y_ok.sem, 1)
        post_dve(dve, 2, R_POST2)
        rms_split_dve(dve, DEPTH, 3, KD, par[:, R_MPRE2:R_MPRE2 + KD])
        for half, vf, kf, vd, kd in ((0, V_FA, K_FA, V_DA, K_DA), (1, V_FB, K_FB, V_DB, K_DB)):
            with dve.Fori(0, 4) as i:
                for s in range(2):
                    dve.drain()
                    for j in range(2):
                        t = 2 * s + j
                        dve.wait_ge(f2_r.sem, i * 4 + (16 * half + t + 1))
                        tt(hq2[:, j, :], r2[:, j, :], r2[:, j, :], ALU.mult).then_inc(f2_q.sem, 1)
                    for j in range(2):
                        t = 2 * s + j
                        dve.wait_ge(f2_hid.sem, i * 4 + (16 * half + t + 1))
                        tt(hid2_lo[:, ds(i * 4 + t, 1), :].rearrange("p a t -> p (a t)"), hq2[:, j, :],
                           hid2_hi[:, ds(i * 4 + t, 1), :].bitcast(F32).rearrange("p a t -> p (a t)"),
                           ALU.subtract).then_inc(f2_lod.sem, 1)
            for c in range(4):
                b = jn(kd + c)[1]
                for j in range(2):
                    dve.wait_ge(tick.sem, Tn(vd + 2 * c + 1, j))
                    y = y2[:, 2 * c + j, :]
                    if half == 0:
                        mm = dve.tensor_copy(y, psG[:, 2 * b + j, :])
                    else:
                        mm = tt(y, y, psG[:, 2 * b + j, :], ALU.add)
                mm.then_inc(psum_free[b].sem, 1)
                if half:
                    dve.drain().then_inc(y_ok.sem, 1)
        post_dve(dve, 4, R_MPOST2)
        for n in range(8):
            dve.wait_ge(o_tr.sem, n + 1)
            dve.tensor_copy(x_out[:, n % TB, (n // TB) * S:(n // TB + 1) * S], psH[:, n % 4, :]).then_inc(o_cp.sem, 1)

    def post_dve(dve, i, r):
        inverse_rms(dve, DEPTH, i)
        for k in range(KD + 1):
            if k < KD:
                dve.scalar_tensor_tensor(out=y2[:, k, :], in0=y2[:, k, :], scalar=par[:, r + k:r + k + 1],
                                         in1=rms[:, :], op0=ALU.mult, op1=ALU.mult)
            dve.drain()
            if k:
                dve.tensor_tensor(xT[:, k - 1, :], xT[:, k - 1, :], y2[:, k - 1, :], ALU.add).then_inc(x2_ok.sem, 1)

    @block.sync
    def _(sp):
        setup_sync(sp)
        with sp.Fori(0, DEPTH) as l:
            layer_sync(sp, l)
        second_sync(sp)

    @block.gpsimd
    def _(pool):
        setup_pool(pool)
        second_pool(pool)
        with pool.Fori(0, ALL_PAIRS) as m:
            for s in range(2):
                pool.wait_ge(hi_done.sem, m * 2 + (s + 1))
                pool.tensor_tensor(w_lo[:, s, :], raw[:, s, :], w_hi[:, s, :].bitcast(F32), ALU.subtract)\
                    .then_inc(lo_done.sem, 1)

    @block.scalar
    def _(act):
        setup_act_part(act)
        split_hi(act, 0, 0)
        split_hi(act, 0, 1)
        for p in range(4):
            act.wait_ge(x_done.sem, 2 * p + 2)
            square_pair(act, 0, 0, p, xT)
        with act.Fori(0, DEPTH) as l:
            layer_act(act, l)
        second_act(act)

    @block.vector
    def _(dve):
        setup_dve(dve)
        with dve.Fori(0, DEPTH) as l:
            layer_dve(dve, l)
        second_dve(dve)

    @block.tensor
    def _(pe):
        setup_pe_part(pe)
        pe.wait_ge(x_cp.sem, TB + 1)
        for p in range(4):
            sum_pair(pe, 0, 0, p)
        with pe.Fori(0, DEPTH) as l:
            layer_pe(pe, l)
        second_pe(pe)


_INS = ["x", "positions", "w_in", "da_lambda", "da_norm", "hg_lb_logits", "hg_norm", "w_a", "w_b", "w_o", "attn_norm",
        "ffn_norm", "w_gate", "w_up", "w_down", "final_norm", "norm_mix_pre_2", "norm_mix_post_2", "norm_mlp_pre_2",
        "norm_mlp_post_2", "w_in_2", "rel_bias_2", "sinks_2", "lam_re_2", "lam_im_2", "log_dt_2", "b_re_2", "b_im_2",
        "c_re_2", "c_im_2", "d_skip_2", "w_glu_2", "w_attn_branch_2", "w_ssm_branch_2", "w_out_2", "w_ff_in_2",
        "w_ff_out_2"]


def kernel(**inputs):
    import numpy as _np
    import concourse.bacc as _bacc
    from concourse import mybir as _mybir
    from concourse.bass_utils import run_bass_kernel_spmd as _run

    nc = _bacc.Bacc("TRN2", target_bir_lowering=False, num_devices=1)
    arrays, io = {}, {}
    for name in _INS:
        a = _np.ascontiguousarray(inputs[name])
        arrays[f"in_{name}_dram"] = a
        io[name] = nc.dram_tensor(f"in_{name}_dram", a.shape, _mybir.dt.from_np(a.dtype), kind="ExternalInput").ap()
    io["out"] = nc.dram_tensor("out_0_dram", (1, S, D), F32, kind="ExternalOutput").ap()
    build_kernel(nc, io)
    r = _run(nc, [arrays], core_ids=[0])
    return r.results[0]["out_0_dram"]
```
